# Optimizing a Trainium2 kernel written in Bass

```python
import math
import jax, jax.numpy as jnp
from jax import lax
import numpy as np

D_MODEL = 2048
BATCH = 1
SEQ = 256
DEPTH = 2

NORM_EPS = 1e-6
BLOCK = 128

LRU_WIDTH = 1024
LRU_BLOCKS = 8
LRU_BLOCK_DIM = LRU_WIDTH // LRU_BLOCKS
CONV_WIDTH = 4
LRU_C = 8.0
SWA_Q_HEADS = 16
SWA_KV_HEADS = 2
SWA_HEAD_DIM = 64
SWA_GROUP = SWA_Q_HEADS // SWA_KV_HEADS
SWA_WIDTH = SWA_Q_HEADS * SWA_HEAD_DIM
SWA_KV_WIDTH = SWA_KV_HEADS * SWA_HEAD_DIM
WINDOW = 128
EVEN_SPLITS = [LRU_WIDTH, LRU_WIDTH, SWA_WIDTH, SWA_KV_WIDTH, SWA_KV_WIDTH, SWA_WIDTH]
EVEN_IN = sum(EVEN_SPLITS)
EVEN_MIX = LRU_WIDTH + SWA_WIDTH

MLA_HEADS = 8
MLA_Q_RANK = 768
MLA_KV_RANK = 512
MLA_NOPE = 128
MLA_ROPE = 64
MLA_V = 128
MLA_WIDTH = MLA_HEADS * MLA_V
ROPE_THETA = 10000.0
DIFF_HEADS = 8
DIFF_QK = 64
DIFF_V = 2 * DIFF_QK
DIFF_QK_WIDTH = DIFF_HEADS * 2 * DIFF_QK
DIFF_WIDTH = DIFF_HEADS * DIFF_V
DIFF_LAYER_IDX = 1
DIFF_LAMBDA_INIT = 0.8 - 0.6 * math.exp(-0.3 * DIFF_LAYER_IDX)
ODD_SPLITS = [MLA_Q_RANK, MLA_KV_RANK, MLA_ROPE, MLA_WIDTH,
              DIFF_QK_WIDTH, DIFF_QK_WIDTH, DIFF_WIDTH, DIFF_WIDTH]
ODD_IN = sum(ODD_SPLITS)
ODD_MIX = MLA_WIDTH + DIFF_WIDTH


def rmsnorm(x, g):
    xf = x.astype(jnp.float32)
    y = xf * lax.rsqrt(jnp.mean(xf * xf, axis=-1, keepdims=True) + NORM_EPS)
    return (y * g.astype(jnp.float32)).astype(x.dtype)

def split_cols(z, sizes):
    idx = [int(i) for i in np.cumsum(sizes)[:-1]]
    return jnp.split(z, idx, axis=-1)

def rope(x, pos):
    half = x.shape[-1] // 2
    freq = ROPE_THETA ** (-jnp.arange(half, dtype=jnp.float32) / half)
    ang = pos.astype(jnp.float32)[:, None] * freq[None, :]
    cos = jnp.cos(ang)[:, None, :]
    sin = jnp.sin(ang)[:, None, :]
    xf = x.astype(jnp.float32)
    x1, x2 = xf[..., :half], xf[..., half:]
    return jnp.concatenate([x1 * cos - x2 * sin, x1 * sin + x2 * cos], axis=-1).astype(x.dtype)

def causal_depthwise_conv(x, w, b):
    y = lax.conv_general_dilated(
        x, w[:, None, :].astype(x.dtype), window_strides=(1,),
        padding=[(CONV_WIDTH - 1, 0)], dimension_numbers=("NWC", "WIO", "NWC"),
        feature_group_count=x.shape[-1])
    return y + b

def rg_lru(x, gx_w, gx_b, ga_w, ga_b, lru_lambda):
    B, S, _ = x.shape
    xb = x.reshape(B, S, LRU_BLOCKS, LRU_BLOCK_DIM)
    gate_i = jax.nn.sigmoid(jnp.einsum("bsnd,nde->bsne", xb, gx_w) + gx_b).reshape(B, S, LRU_WIDTH)
    gate_r = jax.nn.sigmoid(jnp.einsum("bsnd,nde->bsne", xb, ga_w) + ga_b).reshape(B, S, LRU_WIDTH)
    log_a = -LRU_C * jax.nn.softplus(-lru_lambda.astype(jnp.float32)) * gate_r.astype(jnp.float32)
    a = jnp.exp(log_a)
    mult = jnp.sqrt(-jnp.expm1(2.0 * log_a))
    u = mult * gate_i.astype(jnp.float32) * x.astype(jnp.float32)

    def combine(c1, c2):
        a1, b1 = c1
        a2, b2 = c2
        return a1 * a2, a2 * b1 + b2

    _, h = lax.associative_scan(combine, (a, u), axis=1)
    return h.astype(x.dtype)

def sliding_window_gqa_sinks(q, k, v, sinks):
    B, S = q.shape[:2]
    nb = S // BLOCK
    qb = q.reshape(B, nb, BLOCK, SWA_KV_HEADS, SWA_GROUP, SWA_HEAD_DIM)

    def band(t):
        tp = jnp.pad(t, ((0, 0), (BLOCK, 0), (0, 0), (0, 0)))
        cur = tp[:, BLOCK:].reshape(B, nb, BLOCK, SWA_KV_HEADS, SWA_HEAD_DIM)
        prev = tp[:, :S].reshape(B, nb, BLOCK, SWA_KV_HEADS, SWA_HEAD_DIM)
        return jnp.concatenate([prev, cur], axis=2)

    kb, vb = band(k), band(v)
    s = jnp.einsum("bnqhgd,bnkhd->bnhgqk", qb, kb).astype(jnp.float32) * (SWA_HEAD_DIM ** -0.5)
    n = jnp.arange(nb)[:, None, None]
    qi = jnp.arange(BLOCK)[None, :, None]
    ki = jnp.arange(2 * BLOCK)[None, None, :]
    rel = qi + BLOCK - ki
    kpos = n * BLOCK - BLOCK + ki
    mask = (rel >= 0) & (rel < WINDOW) & (kpos >= 0)
    s = jnp.where(mask[None, :, None, None], s, -jnp.inf)
    sink = sinks.astype(jnp.float32).reshape(1, 1, SWA_KV_HEADS, SWA_GROUP, 1, 1)
    m = jnp.maximum(jnp.max(s, axis=-1, keepdims=True), sink)
    p = jnp.exp(s - m)
    p = p / (jnp.sum(p, axis=-1, keepdims=True) + jnp.exp(sink - m))
    o = jnp.einsum("bnhgqk,bnkhd->bnqhgd", p.astype(vb.dtype), vb)
    return o.reshape(B, S, SWA_WIDTH)

def sweep_query_blocks(block_fn, q):
    B, S = q.shape[:2]
    nb = S // BLOCK
    qb = jnp.moveaxis(q.reshape((B, nb, BLOCK) + q.shape[2:]), 1, 0)

    def body(args):
        qblk, n = args
        return block_fn(qblk, n * BLOCK + jnp.arange(BLOCK))

    o = lax.map(body, (qb, jnp.arange(nb)))
    o = jnp.moveaxis(o, 0, 1)
    return o.reshape((B, S) + o.shape[3:])

def causal_mla_attention(q, k, v):
    S = k.shape[1]
    kpos = jnp.arange(S)
    scale = (MLA_NOPE + MLA_ROPE) ** -0.5

    def block_fn(qblk, qpos):
        s = jnp.einsum("bqhd,bkhd->bhqk", qblk, k).astype(jnp.float32) * scale
        s = jnp.where(kpos[None, :] <= qpos[:, None], s, -jnp.inf)
        p = jax.nn.softmax(s, axis=-1)
        return jnp.einsum("bhqk,bkhd->bqhd", p.astype(v.dtype), v)

    return sweep_query_blocks(block_fn, q)

def causal_diff_attention(q, k, v, lam):
    S = k.shape[1]
    kpos = jnp.arange(S)
    scale = DIFF_QK ** -0.5

    def block_fn(qblk, qpos):
        s = jnp.einsum("bqhcd,bkhcd->bchqk", qblk, k).astype(jnp.float32) * scale
        s = jnp.where(kpos[None, :] <= qpos[:, None], s, -jnp.inf)
        p = jax.nn.softmax(s, axis=-1)
        a = p[:, 0] - lam * p[:, 1]
        return jnp.einsum("bhqk,bkhd->bqhd", a.astype(v.dtype), v)

    return sweep_query_blocks(block_fn, q)

def even_layer(h, w_in, conv_w, conv_b, gx_w, gx_b, ga_w, ga_b, lru_lambda, sinks, w_out):
    B, S, _ = h.shape
    z = h @ w_in
    lru_x, lru_gate, q, k, v, swa_gate = split_cols(z, EVEN_SPLITS)
    lru_x = causal_depthwise_conv(lru_x, conv_w, conv_b)
    y_a = rg_lru(lru_x, gx_w, gx_b, ga_w, ga_b, lru_lambda) * jax.nn.silu(lru_gate)
    q = q.reshape(B, S, SWA_Q_HEADS, SWA_HEAD_DIM)
    k = k.reshape(B, S, SWA_KV_HEADS, SWA_HEAD_DIM)
    v = v.reshape(B, S, SWA_KV_HEADS, SWA_HEAD_DIM)
    y_b = sliding_window_gqa_sinks(q, k, v, sinks) * jax.nn.silu(swa_gate)
    return jnp.concatenate([y_a, y_b], axis=-1) @ w_out

def odd_layer(h, w_in, q_norm, w_uq, kv_norm, w_ukv, lambda_q1, lambda_k1, lambda_q2, lambda_k2,
              subln, w_out):
    B, S, _ = h.shape
    pos = jnp.arange(S)
    z = h @ w_in
    c_q, c_kv, k_rope, mla_gate, dq, dk, dv, diff_gate = split_cols(z, ODD_SPLITS)
    q = (rmsnorm(c_q, q_norm) @ w_uq).reshape(B, S, MLA_HEADS, MLA_NOPE + MLA_ROPE)
    q = jnp.concatenate([q[..., :MLA_NOPE], rope(q[..., MLA_NOPE:], pos)], axis=-1)
    kv = (rmsnorm(c_kv, kv_norm) @ w_ukv).reshape(B, S, MLA_HEADS, MLA_NOPE + MLA_V)
    k_nope, v_c = kv[..., :MLA_NOPE], kv[..., MLA_NOPE:]
    k_r = rope(k_rope.reshape(B, S, 1, MLA_ROPE), pos)
    k_c = jnp.concatenate([k_nope, jnp.broadcast_to(k_r, (B, S, MLA_HEADS, MLA_ROPE))], axis=-1)
    y_c = causal_mla_attention(q, k_c, v_c).reshape(B, S, MLA_WIDTH) * jax.nn.silu(mla_gate)
    qd = dq.reshape(B, S, DIFF_HEADS, 2, DIFF_QK)
    kd = dk.reshape(B, S, DIFF_HEADS, 2, DIFF_QK)
    vd = dv.reshape(B, S, DIFF_HEADS, DIFF_V)
    lam = (jnp.exp(jnp.sum(lambda_q1.astype(jnp.float32) * lambda_k1.astype(jnp.float32)))
           - jnp.exp(jnp.sum(lambda_q2.astype(jnp.float32) * lambda_k2.astype(jnp.float32)))
           + DIFF_LAMBDA_INIT)
    od = causal_diff_attention(qd, kd, vd, lam)
    od = rmsnorm(od, subln) * (1.0 - DIFF_LAMBDA_INIT)
    y_d = od.reshape(B, S, DIFF_WIDTH) * jax.nn.silu(diff_gate)
    return jnp.concatenate([y_c, y_d], axis=-1) @ w_out

def first_inputs(seed: int = 0) -> dict:
    key = jax.random.key(seed)
    ks = jax.random.split(key, 32)
    f32 = jnp.float32

    def dense(k, shape, fan_in):
        return jax.random.normal(k, shape, f32) * (fan_in ** -0.5)

    def gain(k, shape):
        return 1.0 + 0.05 * jax.random.normal(k, shape, f32)

    def small(k, shape, s=0.02):
        return s * jax.random.normal(k, shape, f32)

    u = jax.random.uniform(ks[10], (LRU_WIDTH,), f32, minval=0.9, maxval=0.999)
    a_base = u ** (1.0 / LRU_C)
    lru_lambda = jnp.log(a_base) - jnp.log1p(-a_base)

    return {
        "x": jax.random.normal(ks[0], (BATCH, SEQ, D_MODEL), f32),
        "norm_gains": gain(ks[1], (DEPTH, D_MODEL)),
        "final_norm_gain": gain(ks[2], (D_MODEL,)),
        "l0_w_in": dense(ks[3], (D_MODEL, EVEN_IN), D_MODEL),
        "l0_conv_w": dense(ks[4], (CONV_WIDTH, LRU_WIDTH), CONV_WIDTH),
        "l0_conv_b": small(ks[5], (LRU_WIDTH,)),
        "l0_gate_x_w": dense(ks[6], (LRU_BLOCKS, LRU_BLOCK_DIM, LRU_BLOCK_DIM), LRU_BLOCK_DIM),
        "l0_gate_x_b": small(ks[7], (LRU_BLOCKS, LRU_BLOCK_DIM)),
        "l0_gate_a_w": dense(ks[8], (LRU_BLOCKS, LRU_BLOCK_DIM, LRU_BLOCK_DIM), LRU_BLOCK_DIM),
        "l0_gate_a_b": small(ks[9], (LRU_BLOCKS, LRU_BLOCK_DIM)),
        "l0_lru_lambda": lru_lambda,
        "l0_sinks": 0.5 * jax.random.normal(ks[11], (SWA_Q_HEADS,), f32),
        "l0_w_out": dense(ks[12], (EVEN_MIX, D_MODEL), EVEN_MIX),
        "l1_w_in": dense(ks[13], (D_MODEL, ODD_IN), D_MODEL),
        "l1_q_norm": gain(ks[14], (MLA_Q_RANK,)),
        "l1_w_uq": dense(ks[15], (MLA_Q_RANK, MLA_HEADS * (MLA_NOPE + MLA_ROPE)), MLA_Q_RANK),
        "l1_kv_norm": gain(ks[16], (MLA_KV_RANK,)),
        "l1_w_ukv": dense(ks[17], (MLA_KV_RANK, MLA_HEADS * (MLA_NOPE + MLA_V)), MLA_KV_RANK),
        "l1_lambda_q1": small(ks[18], (DIFF_QK,), 0.1),
        "l1_lambda_k1": small(ks[19], (DIFF_QK,), 0.1),
        "l1_lambda_q2": small(ks[20], (DIFF_QK,), 0.1),
        "l1_lambda_k2": small(ks[21], (DIFF_QK,), 0.1),
        "l1_subln": gain(ks[22], (DIFF_V,)),
        "l1_w_out": dense(ks[23], (ODD_MIX, D_MODEL), ODD_MIX),
    }

def first_block(x, norm_gains, final_norm_gain,
              l0_w_in, l0_conv_w, l0_conv_b, l0_gate_x_w, l0_gate_x_b, l0_gate_a_w, l0_gate_a_b,
              l0_lru_lambda, l0_sinks, l0_w_out,
              l1_w_in, l1_q_norm, l1_w_uq, l1_kv_norm, l1_w_ukv,
              l1_lambda_q1, l1_lambda_k1, l1_lambda_q2, l1_lambda_k2, l1_subln, l1_w_out):
    even_params = (l0_w_in, l0_conv_w, l0_conv_b, l0_gate_x_w, l0_gate_x_b, l0_gate_a_w,
                   l0_gate_a_b, l0_lru_lambda, l0_sinks, l0_w_out)
    odd_params = (l1_w_in, l1_q_norm, l1_w_uq, l1_kv_norm, l1_w_ukv, l1_lambda_q1, l1_lambda_k1,
                  l1_lambda_q2, l1_lambda_k2, l1_subln, l1_w_out)
    for layer in range(DEPTH):
        h = rmsnorm(x, norm_gains[layer])
        if layer % 2 == 0:
            x = x + even_layer(h, *even_params)
        else:
            x = x + odd_layer(h, *odd_params)
    return rmsnorm(x, final_norm_gain)


GRID_W = 64
CTX_LEN = 256
EXPAND = 2
D_INNER = EXPAND * D_MODEL
A_WIDTH = D_INNER // 2
H_A = 8
DV_A = A_WIDTH // H_A
DK_A = DV_A // 2
QK_WIDTH = H_A * DK_A
B_WIDTH = D_INNER - A_WIDTH
G_B = 8
GB_DIM = B_WIDTH // G_B
EVEN_IN_2 = 2 * QK_WIDTH + 2 * A_WIDTH + 2 * B_WIDTH
C_WIDTH = D_INNER
ODD_IN_2 = 4 * C_WIDTH
CONV_W = 3
CHUNK = 128
ROPE_BASE = 10000.0
EPS = 1e-6
N_EVEN = (DEPTH + 1) // 2
N_ODD = DEPTH // 2


def _rmsnorm(x, w):
    xf = x.astype(jnp.float32)
    y = xf * lax.rsqrt(jnp.mean(xf * xf, axis=-1, keepdims=True) + EPS)
    return (y * w.astype(jnp.float32)).astype(x.dtype)

def _modulate(x, w, shift, scale):
    return _rmsnorm(x, w) * (1.0 + scale) + shift

def _heads(t, d):
    b, L, _ = t.shape
    return t.reshape(b, L, -1, d).transpose(0, 2, 1, 3).astype(jnp.float32)

def _axial_rope(t):
    L = t.shape[2]
    pos = jnp.arange(L)
    row = (pos // GRID_W).astype(jnp.float32)
    col = (pos % GRID_W).astype(jnp.float32)
    nf = DK_A // 4
    inv = ROPE_BASE ** (-jnp.arange(nf, dtype=jnp.float32) / nf)
    ang = jnp.concatenate([row[:, None] * inv[None], col[:, None] * inv[None]], axis=-1)
    cos, sin = jnp.cos(ang), jnp.sin(ang)
    t1, t2 = t[..., : DK_A // 2], t[..., DK_A // 2:]
    return jnp.concatenate([t1 * cos - t2 * sin, t1 * sin + t2 * cos], axis=-1)

def _retention_scan(q, k, v, log_gamma, s0, inclusive):
    b, h, L, dk = q.shape
    dv = v.shape[-1]
    nc = L // CHUNK
    qc = q.reshape(b, h, nc, CHUNK, dk)
    kc = k.reshape(b, h, nc, CHUNK, dk)
    vc = v.reshape(b, h, nc, CHUNK, dv)
    idx = jnp.arange(CHUNK, dtype=jnp.float32)
    rel = idx[:, None] - idx[None, :]
    keep = (rel >= 0) if inclusive else (rel > 0)
    dmat = jnp.where(keep[None], jnp.exp(log_gamma[:, None, None] * jnp.maximum(rel, 0.0)[None]), 0.0)
    scores = jnp.einsum('bhnid,bhnjd->bhnij', qc, kc) * dmat[None, :, None]
    o = jnp.einsum('bhnij,bhnje->bhnie', scores, vc)
    zeta = jnp.exp(log_gamma[:, None] * (CHUNK - 1.0 - idx)[None])
    inc = jnp.einsum('bhnjd,bhnje->bhnde', kc, vc * zeta[None, :, None, :, None])
    chunk_decay = jnp.exp(log_gamma * CHUNK)[None, :, None, None]

    def step(s, inc_n):
        return chunk_decay * s + inc_n, s

    s_last, s_prev = lax.scan(step, s0, jnp.moveaxis(inc, 2, 0))
    s_prev = jnp.moveaxis(s_prev, 0, 2)
    xi = jnp.exp(log_gamma[:, None] * (idx + 1.0)[None])
    o = o + jnp.einsum('bhnid,bhnde->bhnie', qc, s_prev) * xi[None, :, None, :, None]
    return o.reshape(b, h, L, dv), s_last

def _retention(q, k, v, log_gamma, s0_fwd, s0_bwd):
    flip = lambda t: jnp.flip(t, axis=2)
    o_f, s_f = _retention_scan(q, k, v, log_gamma[0], s0_fwd, True)
    o_b, s_b = _retention_scan(flip(q), flip(k), flip(v), log_gamma[1], s0_bwd, False)
    o = o_f + flip(o_b)
    o = o * lax.rsqrt(jnp.mean(o * o, axis=-1, keepdims=True) + EPS)
    return o, s_f, s_b

def _merge_heads(o, dtype):
    b, h, L, d = o.shape
    return o.transpose(0, 2, 1, 3).reshape(b, L, h * d).astype(dtype)

def _fourier(u, fno_w):
    b, L, _ = u.shape
    ug = u.reshape(b, L, G_B, GB_DIM).astype(jnp.float32)
    f = jnp.fft.fft2(ug, axes=(1, 3), norm='ortho').real
    y = jnp.einsum('blgc,gcd->blgd', f.astype(u.dtype), fno_w)
    return y.reshape(b, L, B_WIDTH)

def _split_even(p):
    cuts = [QK_WIDTH, 2 * QK_WIDTH, 2 * QK_WIDTH + A_WIDTH, 2 * QK_WIDTH + 2 * A_WIDTH,
            2 * QK_WIDTH + 2 * A_WIDTH + B_WIDTH]
    return jnp.split(p, cuts, axis=-1)

def _even_layer(hx, hc, w_in, decay_logit, fno_w, w_out, need_ctx):
    log_gamma = -jnp.exp(decay_logit.astype(jnp.float32))
    qx, kx, vx, gax, ux, gbx = _split_even(hx @ w_in)
    qc, kc, vc, gac, uc, gbc = _split_even(hc @ w_in)
    kscale = DK_A ** -0.5
    b = hx.shape[0]
    zeros = jnp.zeros((b, H_A, DK_A, DV_A), jnp.float32)
    ret_c, s_f, s_b = _retention(_heads(qc, DK_A), _heads(kc, DK_A) * kscale, _heads(vc, DV_A),
                                 log_gamma, zeros, zeros)
    ret_x, _, _ = _retention(_axial_rope(_heads(qx, DK_A)), _axial_rope(_heads(kx, DK_A)) * kscale,
                             _heads(vx, DV_A), log_gamma, s_f, s_b)
    yx = jnp.concatenate([_merge_heads(ret_x, hx.dtype) * jax.nn.silu(gax),
                          _fourier(ux, fno_w) * jax.nn.silu(gbx)], axis=-1) @ w_out
    yc = None
    if need_ctx:
        yc = jnp.concatenate([_merge_heads(ret_c, hc.dtype) * jax.nn.silu(gac),
                              _fourier(uc, fno_w) * jax.nn.silu(gbc)], axis=-1) @ w_out
    return yx, yc

def _conv3(z, w, rows):
    b, L, ch = z.shape
    if rows is None:
        zp = jnp.pad(z, ((0, 0), (1, 1), (0, 0)))
        return zp[:, :-2] * w[0] + zp[:, 1:-1] * w[1] + zp[:, 2:] * w[2]
    zg = z.reshape(b, rows, GRID_W, ch)
    zp = jnp.pad(zg, ((0, 0), (0, 0), (1, 1), (0, 0)))
    y = zp[:, :, :-2] * w[0] + zp[:, :, 1:-1] * w[1] + zp[:, :, 2:] * w[2]
    return y.reshape(b, L, ch)

def _odd_layer(h, w_in, conv_w, w_out, rows):
    bg, cg, xt, g = jnp.split(h @ w_in, 4, axis=-1)
    y = bg * _conv3(cg * xt, conv_w, rows) * jax.nn.silu(g)
    return y @ w_out

def second_inputs(seed: int = 0) -> dict:
    key = jax.random.key(seed)
    ks = jax.random.split(key, 15)

    def nrm(k, shape, scale):
        return jax.random.normal(k, shape, jnp.float32) * scale

    base = jnp.asarray(np.log(-np.log1p(-2.0 ** (-5.0 - np.arange(H_A)))), jnp.float32)
    return {
        'x': nrm(ks[0], (BATCH, SEQ, D_MODEL), 1.0),
        'c': nrm(ks[1], (BATCH, D_MODEL), 1.0),
        'ctx': nrm(ks[2], (BATCH, CTX_LEN, D_MODEL), 1.0),
        'c_ctx': nrm(ks[3], (D_MODEL,), 1.0),
        'ada_w': nrm(ks[4], (DEPTH, D_MODEL, 3 * D_MODEL), 0.5 * D_MODEL ** -0.5),
        'ada_b': nrm(ks[5], (DEPTH, 3 * D_MODEL), 0.02),
        'norm_w': 1.0 + nrm(ks[6], (DEPTH, D_MODEL), 0.02),
        'ev_w_in': nrm(ks[7], (N_EVEN, D_MODEL, EVEN_IN_2), D_MODEL ** -0.5),
        'ret_decay_logit': base[None, None, :] + nrm(ks[8], (N_EVEN, 2, H_A), 0.1),
        'fno_w': nrm(ks[9], (N_EVEN, G_B, GB_DIM, GB_DIM), GB_DIM ** -0.5),
        'ev_w_out': nrm(ks[10], (N_EVEN, D_INNER, D_MODEL), D_INNER ** -0.5),
        'od_w_in': nrm(ks[11], (N_ODD, D_MODEL, ODD_IN_2), D_MODEL ** -0.5),
        'conv_w': nrm(ks[12], (N_ODD, CONV_W, C_WIDTH), CONV_W ** -0.5),
        'od_w_out': nrm(ks[13], (N_ODD, C_WIDTH, D_MODEL), C_WIDTH ** -0.5),
        'final_norm_w': 1.0 + nrm(ks[14], (D_MODEL,), 0.02),
    }

def second_block(x, c, ctx, c_ctx, ada_w, ada_b, norm_w, ev_w_in, ret_decay_logit, fno_w, ev_w_out,
              od_w_in, conv_w, od_w_out, final_norm_w):
    rows = x.shape[1] // GRID_W
    sc = jax.nn.silu(c)
    scc = jax.nn.silu(c_ctx)
    for i in range(DEPTH):
        need_ctx = i < DEPTH - 1
        shift_x, scale_x, gate_x = jnp.split((sc @ ada_w[i] + ada_b[i])[:, None, :], 3, axis=-1)
        shift_c, scale_c, gate_c = jnp.split(scc @ ada_w[i] + ada_b[i], 3, axis=-1)
        hx = _modulate(x, norm_w[i], shift_x, scale_x)
        hc = _modulate(ctx, norm_w[i], shift_c, scale_c)
        j = i // 2
        if i % 2 == 0:
            yx, yc = _even_layer(hx, hc, ev_w_in[j], ret_decay_logit[j], fno_w[j], ev_w_out[j], need_ctx)
        else:
            yx = _odd_layer(hx, od_w_in[j], conv_w[j], od_w_out[j], rows)
            yc = _odd_layer(hc, od_w_in[j], conv_w[j], od_w_out[j], None) if need_ctx else None
        x = x + gate_x * yx
        if need_ctx:
            ctx = ctx + gate_c * yc
    return _rmsnorm(x, final_norm_w)


def setup_inputs(seed=0):
    out = dict(first_inputs(seed))
    for name, value in second_inputs(seed + 1).items():
        if name != "x":
            out[name + "_2"] = value
    return out


def reference(
    x, norm_gains, final_norm_gain, l0_w_in, l0_conv_w, l0_conv_b, l0_gate_x_w, l0_gate_x_b,
    l0_gate_a_w, l0_gate_a_b, l0_lru_lambda, l0_sinks, l0_w_out, l1_w_in, l1_q_norm, l1_w_uq,
    l1_kv_norm, l1_w_ukv, l1_lambda_q1, l1_lambda_k1, l1_lambda_q2, l1_lambda_k2, l1_subln,
    l1_w_out, c_2, ctx_2, c_ctx_2, ada_w_2, ada_b_2, norm_w_2, ev_w_in_2, ret_decay_logit_2,
    fno_w_2, ev_w_out_2, od_w_in_2, conv_w_2, od_w_out_2, final_norm_w_2,
):
    x = first_block(
        x, norm_gains, final_norm_gain, l0_w_in, l0_conv_w, l0_conv_b, l0_gate_x_w, l0_gate_x_b,
        l0_gate_a_w, l0_gate_a_b, l0_lru_lambda, l0_sinks, l0_w_out, l1_w_in, l1_q_norm,
        l1_w_uq, l1_kv_norm, l1_w_ukv, l1_lambda_q1, l1_lambda_k1, l1_lambda_q2, l1_lambda_k2,
        l1_subln, l1_w_out,
    )
    return second_block(
        x, c_2, ctx_2, c_ctx_2, ada_w_2, ada_b_2, norm_w_2, ev_w_in_2, ret_decay_logit_2,
        fno_w_2, ev_w_out_2, od_w_in_2, conv_w_2, od_w_out_2, final_norm_w_2,
    )


_drawn_inputs = setup_inputs


def setup_inputs(seed=0):
    import zlib

    import numpy as np

    out = dict(_drawn_inputs(seed))
    spreads = {}
    factors = {'l0_gate_x_b': 8.0,
     'l0_gate_a_b': 8.0,
     'l0_sinks': 6.919,
     'l1_q_norm': 8.0,
     'l1_kv_norm': 8.0,
     'l1_lambda_q2': 4.414,
     'l1_lambda_k2': 3.03,
     'l1_subln': 4.736,
     'norm_w_2': 4.799,
     'final_norm_w_2': 2.816}
    for name, (base, spread) in spreads.items():
        noise = np.random.default_rng([zlib.crc32(name.encode()), seed]).standard_normal(out[name].shape)
        drawn = base * np.exp(spread * noise) if base else spread * noise
        out[name] = __import__('jax').numpy.asarray(drawn.astype(out[name].dtype))
    for name, factor in factors.items():
        out[name] = (out[name] * factor).astype(out[name].dtype)
    return out
```

```python
from contextlib import ExitStack

import numpy as np

import concourse.bass as bass
from concourse import mybir

F32 = mybir.dt.float32
F32R = mybir.dt.float32r
ALU = mybir.AluOpType
ACT = mybir.ActivationFunctionType
AX = mybir.AxisListType.X
ds = bass.ds

P = 128
T = 256
TT = T // P
D = 2048
KT = D // P
EPS = 1e-6
N_PARAM = 22
RING = 4
SLOT = 1152

LRU_W = 1024
SWA_Q, SWA_KV, SWA_D = 1024, 128, 64
C_K = 2 * LRU_W + SWA_Q
C_V = C_K + SWA_KV
C_G = C_V + SWA_KV

Q_RANK, KV_RANK, ROPE_D = 768, 512, 64
CQ_T, CKV_T = Q_RANK // P, KV_RANK // P
C_MG = Q_RANK + KV_RANK + ROPE_D
C_DIFF = C_MG + 1024
MLA_SCALE = float(192) ** -0.5
LAMBDA_INIT = 0.8 - 0.6 * float(np.exp(-0.3))

RET_H = 8
K_SCALE = float(128) ** -0.5
NEG = -1.0e30

STAGES = [("lru", 4, 8), ("kv", 1, 8), ("swa", 4, 8), ("out0", 4, 8),
          ("cq", 3, 8), ("diff", 4, 16), ("mla", 4, 8), ("out1", 4, 8),
          ("ret", 8, 16), ("four", 8, 8), ("out2", 4, 16), ("conv", 16, 16), ("out3", 4, 16)]
DMAS = {"lru": 2, "kv": 5, "swa": 2, "out0": 1, "cq": 1, "diff": 1, "mla": 1, "out1": 1,
        "ret": 2, "four": 2, "out2": 1, "conv": 1, "out3": 1}
COUNT = {s: n for s, n, _ in STAGES}
PIECES = {s: p for s, _, p in STAGES}
PIECE0, UNIT0, LAND0 = {}, {}, {}
_g = _u = _l = 0
for _s, _n, _p in STAGES:
    PIECE0[_s], UNIT0[_s], LAND0[_s] = _g, _u, _l
    _g, _u, _l = _g + _n * _p, _u + _n, _l + _n * _p // RING * 16 * DMAS[_s]

ADA_COLS = 384
ADA_RING = 4
ADA0 = {"lru": 0, "kv": 4, "swa": 5, "out0": 9, "cq": 13, "diff": 16, "mla": 24, "out1": 28}
ADA_SLABS = 32
ADA_AT = (3, 4, 5, 6)

G_L0, G_L1, G_MOD, CONV_W, CONV_B, GX_B, GA_B, LAM = (
    (0, 0), (0, 16), (0, 32), (0, 64), (0, 96), (0, 104), (0, 112), (0, 120))
ADA_B, G_Q, G_KV, G_SUB, C_X = (1, 0), (1, 96), (1, 102), (1, 106), (1, 107)
CONV3_W, C_CTX = (2, 0), (2, 96)


def constants():
    f = np.float32
    ident = np.eye(P, dtype=f)
    i = np.arange(P)[:, None]
    j = np.arange(P)[None, :]
    causal = np.where(j <= i, 0.0, NEG).astype(f)
    before = np.where(j > i, 0.0, NEG).astype(f)
    zero = np.zeros((P, P), f)
    band = np.concatenate([causal, before, causal], 1)
    full = np.concatenate([causal, zero, causal], 1)
    pos = np.arange(T, dtype=f)

    def rotation(half):
        m = np.zeros((P, P), f)
        for d in range(half):
            m[half + d, d] = -1.0
            m[d, half + d] = 1.0
        return m

    def tables(ang):
        c, s = np.cos(ang).astype(f), np.sin(ang).astype(f)
        return np.concatenate([c, c], 0), np.concatenate([s, s], 0)

    freq = (f(10000.0) ** (-np.arange(32, dtype=f) / f(32))).astype(f)
    cos64, sin64 = tables((pos[None, :] * freq[:, None]).astype(f))
    pad = np.zeros((P - 64, T), f)
    first = np.concatenate([ident, band, full, np.concatenate([cos64, pad], 0),
                            np.concatenate([sin64, pad], 0), rotation(32)], 1)

    inv = (f(10000.0) ** (-np.arange(32, dtype=f) / f(32))).astype(f)
    row = (np.arange(T) // 64).astype(f)
    col = (np.arange(T) % 64).astype(f)
    cos128, sin128 = tables(np.concatenate([row[None] * inv[:, None], col[None] * inv[:, None]], 0).astype(f))
    k = np.arange(T)
    ang = 2 * np.pi * ((k[:, None] * k[None, :]) % T) / T
    dc, dsn = (np.cos(ang) / 16).astype(f), (np.sin(ang) / 16).astype(f)
    cs = np.concatenate([dc, dsn], 1).reshape(2, P, 2 * T).transpose(1, 0, 2).reshape(P, -1)
    ns = (-dsn).reshape(2, P, T).transpose(1, 0, 2).reshape(P, -1)
    rel = (k[None, :] - k[:, None]).astype(f).reshape(2, P, T).transpose(1, 0, 2).reshape(P, -1)
    up = np.broadcast_to(pos + 1, (P, T))
    down = np.broadcast_to(T - pos, (P, T))
    left = np.concatenate([(T - 1 - k).reshape(2, P).T, k.reshape(2, P).T], 1).astype(f)
    second = np.concatenate([cs, ns, np.maximum(rel, 0), np.maximum(-rel, 0), cos128, sin128,
                             rotation(64), up, down, left], 1)
    return np.ascontiguousarray(first, dtype=f), np.ascontiguousarray(second, dtype=f)


def build(nc, d, out, stop_after=None):
    ctx = ExitStack()
    with ctx:
        phase = [ctx]

        def sb(name, shape, dt=F32):
            return phase[0].enter_context(nc.sbuf_tensor(name, shape, dt))

        sems = {}

        def sem(name):
            sems[name] = ctx.enter_context(nc.semaphore(name))
            return sems[name]

        w_raw = sb("w_raw", [P, RING, SLOT])
        w_hi = sb("w_hi", [P, RING, SLOT], F32R)
        w_lo = sb("w_lo", [P, RING, SLOT], F32R)
        x = sb("x_res", [P, TT, D])
        act = sb("act_hl", [P, KT, 2 * T], F32R)
        y = sb("y_mix", [P, 32 * T])
        yt = y[:, :].rearrange("p (k n) -> p k n", n=T)
        pc = sb("param_cols", [P, 3, P])
        ident = sb("ident", [P, P])
        ones = sb("ones", [P, P])
        ada_x = sb("ada_x", [P, 96])
        ada_c = sb("ada_c", [P, 48])
        silu_c = sb("silu_c", [P, 2, KT])
        modc = sb("mod_cols", [P, 3, KT])
        lg = sb("log_gamma", [P, 2 * RET_H])
        state_w = sb("state_w", [P, RET_H, 4])
        sinks = sb("sinks", [P, 16])
        nlam = sb("neg_lambda", [P, 2])
        stat = sb("stat", [P, 4, 2])
        soft = sb("soft", [P, 5, 8])
        lru_c = sb("lru_c", [P, 4, 8])
        sub_g = sb("sub_gain", [P, 1])

        pa = ExitStack()
        phase[0] = pa
        const_a = sb("const_a", [P, 1408])
        ada_ring = sb("ada_ring", [P, ADA_RING, 2 * ADA_COLS])
        acc_x = sb("acc_x", [P, ADA_COLS])
        acc_c = sb("acc_c", [P, ADA_COLS])
        cn = sb("c_norm", [P, CQ_T + CKV_T, 2 * T], F32R)
        k_raw = sb("k_rope_raw", [64, T])
        k_rot = sb("k_rope", [64, T])
        scr_a = sb("scr_a", [P, 4864])
        pa.close()
        pb = ExitStack()
        phase[0] = pb
        act2 = sb("act2_hl", [P, KT, 2 * T], F32R)
        const_b = sb("const_b", [P, 3716])
        fno = sb("fno", [P, 2, T])
        scr_b = sb("scr_b", [P, 4608])
        pb.close()
        phase[0] = ctx

        band = const_a[:, 0:384]
        causal = const_a[:, 384:768]
        cos64 = const_a[0:64, 768:1024]
        sin64 = const_a[0:64, 1024:1280]
        rot64 = const_a[0:64, 1280:1408]
        dft = const_b[:, 0:1024].rearrange("p (k n) -> p k n", k=2)
        dft_ns = const_b[:, 1024:1536].rearrange("p (k n) -> p k n", k=2)
        rel_up = const_b[:, 1536:2048]
        rel_dn = const_b[:, 2048:2560]
        cos128 = const_b[:, 2560:2816]
        sin128 = const_b[:, 2816:3072]
        rot128 = const_b[:, 3072:3200]
        pow_up = const_b[:, 3200:3456]
        pow_dn = const_b[:, 3456:3712]
        pow_left = const_b[:, 3712:3716]

        lam_rows = y[:, 24 * T:25 * T].rearrange("p (v n) -> p v n", v=4)
        kT4 = yt[:, 26:30, :]
        v4 = y[:, 30 * T:32 * T].rearrange("p (h t n) -> p h t n", h=4, t=TT)
        prow = y[:, 0:3 * P].rearrange("p (t n) -> p t n", t=3)
        zc = yt[:, 16:26, :]
        ctx_sb = y[:, 16 * T:32 * T].rearrange("p (t n) -> p t n", t=TT)
        gain_bc = y[:, 8 * T:16 * T]
        junk = y[:, 0:8 * T]

        PS = ctx.enter_context(nc.psum_tensor("banks", [P, 8, 512], F32))

        def bank(n):
            return PS[:, n, :]

        def halves(ap):
            return ap.rearrange("p (k n) -> p k n", k=2)

        A, B, C, E0 = 0, 1, 2, 4

        s_par = sem("params_landed")
        s_x = sem("x_landed")
        s_w = [sem(f"weights_landed{k}") for k in range(RING)]
        s_hi = sem("piece_hi")
        s_lo = sem("piece_lo")
        s_used = sem("piece_used")
        s_free = sem("proj_banks_free")
        s_aw = [sem(f"ada_landed{k}") for k in range(ADA_RING)]
        s_au = sem("ada_piece_used")
        s_aps = sem("ada_cols_in_psum")
        s_acol = sem("ada_cols_read")
        s_gw = sem("gate_w_landed")
        s_fno = sem("fno_landed")
        s_cb = sem("const_b_landed")
        s_ctx = sem("ctx_landed")
        s_gain = sem("gain_landed")
        s_out = sem("out_stored")
        s_set = sem("cleared")
        s_pps = sem("params_in_psum")
        s_pc = sem("params_ready")
        s_pe_ = sem("setup_exp")
        s_dec = sem("decay_logs")
        s_stw = sem("state_weights")
        s_n = {k: sem(f"norm_{k}") for k in ("sum", "mean", "root", "diag", "psum", "tile", "hi", "lo")}
        s_fin = sem("tokens_scaled")
        s_yh = sem("mix_hi")
        s_yl = sem("mix_lo")
        s_gb = sem("gate_rows_in_psum")
        s_gr = sem("gate_rows_ready")
        s_gd = sem("gate_diags_ready")
        S = {}
        for stage, names in {
            "lru": ("conv", "gates", "sig", "y"),
            "swa": ("scores", "max", "exp", "prob", "probT", "probT_sb", "o", "y"),
            "cq": ("squares", "sums", "mean", "root", "gained", "hi", "lo"),
            "diff": ("scores", "max", "exp", "prob", "probT", "probT_sb", "o", "sq", "sum", "mean", "root", "y"),
            "mla": ("rot", "rope", "scores", "max", "exp", "prob", "probT", "probT_sb", "o", "y"),
            "ret": ("arg", "tables", "rot", "rope", "state", "state_sb", "scaled", "scores", "decayed",
                    "o", "sq", "sum", "mean", "root", "y"),
            "four": ("cols", "cols_sb", "rows", "rows_sb", "o", "y"),
            "conv": ("evac", "y"),
        }.items():
            S[stage] = {k: sem(f"{stage}_{k}") for k in names}

        block = ctx.enter_context(nc.Block())
        order = [s for s, _, _ in STAGES]
        last = order if stop_after is None else order[:order.index(stop_after) + 1]

        def wanted(stage):
            return stage in last

        def stage_loop(eng, stage, unit, post, before):
            unit(0, before)
            if COUNT[stage] > 1:
                with eng.Fori(1, COUNT[stage]) as i:
                    unit(i, lambda p: post(p, i - 1))

        def nothing(p):
            pass

        def squeezed(post, i):
            def hook(p):
                post(2 * p, i)
                post(2 * p + 1, i)
            return hook

        def at_end(post, i, steps):
            for p in range(steps):
                post(p, i)

        @block.sync
        def _(sp):
            def row_load(ap, tile, first, n):
                sp.dma_start(prow[first:first + n, tile, :], ap).then_inc(s_par, 16)

            sp.wait_ge(s_set, 1)
            sp.dma_start(ident[:, :], d["const_a"][:, 0:P]).then_inc(s_par, 16)
            row_load(d["norm_gains"].rearrange("l (a b) -> (l a) b", b=P), *G_L0, 32)
            row_load(d["norm_w_2"].rearrange("l (a b) -> (l a) b", b=P), *G_MOD, 32)
            row_load(d["l0_conv_w"].rearrange("l (a b) -> (l a) b", b=P), *CONV_W, 32)
            row_load(d["l0_conv_b"].rearrange("(a b) -> a b", b=P), *CONV_B, 8)
            row_load(d["l0_gate_x_b"], *GX_B, 8)
            row_load(d["l0_gate_a_b"], *GA_B, 8)
            row_load(d["l0_lru_lambda"].rearrange("(a b) -> a b", b=P), *LAM, 8)
            row_load(d["ada_b_2"].rearrange("l (a b) -> (l a) b", b=P), *ADA_B, 96)
            row_load(d["l1_q_norm"].rearrange("(a b) -> a b", b=P), *G_Q, 6)
            row_load(d["l1_kv_norm"].rearrange("(a b) -> a b", b=P), *G_KV, 4)
            row_load(d["l1_subln"].rearrange("(a b) -> a b", b=P), *G_SUB, 1)
            row_load(d["c_2"].rearrange("o (a b) -> (o a) b", b=P), *C_X, 16)
            row_load(d["conv_w_2"].rearrange("o l (a b) -> (o l a) b", b=P), *CONV3_W, 96)
            row_load(d["c_ctx_2"].rearrange("(a b) -> a b", b=P), *C_CTX, 16)
            sp.dma_start(x[:, :, :], d["x"].rearrange("o (t p) n -> p (o t) n", p=P)).then_inc(s_x, 16)
            sp.dma_start(const_a[:, :], d["const_a"][:, P:]).then_inc(s_par, 16)
            sp.dma_start(sinks[:, :], d["l0_sinks"].partition_broadcast(P)).then_inc(s_par, 16)
            sp.dma_start(lg[:, :], d["ret_decay_logit_2"].rearrange("o a h -> (o a h)").partition_broadcast(P))\
                .then_inc(s_par, 16)
            for n, name in enumerate(("l1_lambda_q1", "l1_lambda_k1", "l1_lambda_q2", "l1_lambda_k2")):
                sp.dma_start(lam_rows[:, n, :], d[name].partition_broadcast(P)).then_inc(s_par, 16)

            def two_blocks(t, src):
                return lambda r: r[:, 512 * t:512 * t + 512].rearrange("p (s n) -> p s n", s=2), src

            def sources(stage, i, p):
                if stage == "lru":
                    w = d["l0_w_in"][:, 0:2 * LRU_W].rearrange("(t p) (s n) -> p t s n", p=P, s=2)
                    return [two_blocks(t, w[:, 2 * p + t, :, ds(256 * i, 256)]) for t in range(2)]
                if stage == "kv":
                    w = d["l0_w_in"].rearrange("(t p) n -> p t n", p=P)
                    kk = w[:, 2 * p:2 * p + 2, C_K:C_K + SWA_KV].rearrange("p t (g n) -> p t g n", g=2)

                    def dup(t, n):
                        return lambda r: r[:, t * 384:t * 384 + 256].rearrange("p (g u n) -> p g u n", g=2, u=2)\
                            [:, :, n, :]
                    return [(dup(t, n), kk[:, t, :, :]) for t in range(2) for n in range(2)] + [
                        (lambda r: r[:, 0:768].rearrange("p (t c) -> p t c", t=2)[:, :, 256:384],
                         w[:, 2 * p:2 * p + 2, C_V:C_V + SWA_KV])]
                if stage == "swa":
                    w = d["l0_w_in"].rearrange("(t p) n -> p t n", p=P)

                    def part(n):
                        return lambda r: r[:, 0:1024].rearrange("p (t s n) -> p t s n", t=2, s=2)[:, :, n, :]
                    return [(part(0), w[:, 2 * p:2 * p + 2, ds(256 * i + 2 * LRU_W, 256)]),
                            (part(1), w[:, 2 * p:2 * p + 2, ds(256 * i + C_G, 256)])]
                if stage in ("out0", "out1", "out2", "out3"):
                    name = {"out0": "l0_w_out", "out1": "l1_w_out", "out2": "ev_w_out_2", "out3": "od_w_out_2"}[stage]
                    w = d[name]
                    if len(w.shape) == 3:
                        w = w.rearrange("o k n -> (o k) n")
                    w = w.rearrange("(t p) n -> p t n", p=P)
                    return [(lambda r: r[:, 0:1024].rearrange("p (t n) -> p t n", t=2),
                             w[:, 2 * p:2 * p + 2, ds(512 * i, 512)])]
                if stage == "cq":
                    w = d["l1_w_in"].rearrange("(t p) n -> p t n", p=P)
                    n = 320 if isinstance(i, int) and i == 2 else 512
                    return [(lambda r: r[:, 0:2 * n].rearrange("p (t n) -> p t n", t=2),
                             w[:, 2 * p:2 * p + 2, ds(512 * i, n)])]
                if stage == "diff":
                    w = d["l1_w_in"][:, C_DIFF:C_DIFF + 4096].rearrange("(t p) (s n) -> p t s n", p=P, s=4)
                    return [(lambda r: r[:, 0:1024].rearrange("p (s n) -> p s n", s=4), w[:, p, :, ds(256 * i, 256)])]
                if stage == "mla":
                    if p < 2:
                        w = d["l1_w_uq"].rearrange("(t p) n -> p t n", p=P)
                        return [(lambda r: r[:, 0:1152].rearrange("p (t n) -> p t n", t=CQ_T),
                                 w[:, :, ds(384 * i + 192 * p, 192)])]
                    if p < 4:
                        w = d["l1_w_ukv"].rearrange("(t p) n -> p t n", p=P)
                        return [(lambda r: r[:, 0:1024].rearrange("p (t n) -> p t n", t=CKV_T),
                                 w[:, :, ds(512 * i + 256 * (p - 2), 256)])]
                    w = d["l1_w_in"].rearrange("(t p) n -> p t n", p=P)
                    return [(lambda r: r[:, 0:1024].rearrange("p (t n) -> p t n", t=4),
                             w[:, 4 * (p - 4):4 * (p - 4) + 4, ds(256 * i + C_MG, 256)])]
                if stage == "ret":
                    w = d["ev_w_in_2"].rearrange("o (t p) n -> p (o t) n", p=P)
                    qk = w[:, :, 0:2048].rearrange("p t (s n) -> p t s n", s=2)
                    vg = w[:, :, 2048:6144].rearrange("p t (s n) -> p t s n", s=2)
                    return [(lambda r: r[:, 0:256].rearrange("p (s n) -> p s n", s=2), qk[:, p, :, ds(128 * i, 128)]),
                            (lambda r: r[:, 256:768].rearrange("p (s n) -> p s n", s=2), vg[:, p, :, ds(256 * i, 256)])]
                if stage == "four":
                    w = d["ev_w_in_2"].rearrange("o (t p) n -> p (o t) n", p=P)[:, :, 6144:10240]\
                        .rearrange("p t (s n) -> p t s n", s=2)
                    return [two_blocks(t, w[:, 2 * p + t, :, ds(256 * i, 256)]) for t in range(2)]
                w = d["od_w_in_2"].rearrange("o (t p) (s n) -> p (o t) s n", p=P, s=4)
                return [(lambda r: r[:, 0:1024].rearrange("p (s n) -> p s n", s=4), w[:, p, :, ds(256 * i, 256)])]

            def load_ada(u, layer, p):
                a = u * 8 + p
                if not isinstance(a, int) or a >= ADA_RING:
                    sp.wait_ge(s_au, a - (ADA_RING - 1))
                w = d["ada_w_2"].rearrange("l (t p) n -> p l t n", p=P)
                sp.dma_start(ada_ring[:, p % ADA_RING, :].rearrange("p (t n) -> p t n", t=2),
                             w[:, layer, 2 * p:2 * p + 2, ds((u - 16 * layer) * ADA_COLS, ADA_COLS)])\
                    .then_inc(s_aw[p % ADA_RING], 16)

            def unit(stage):
                def load(i, hook):
                    for p in range(PIECES[stage]):
                        g = PIECE0[stage] + PIECES[stage] * i + p
                        if not isinstance(g, int) or g >= RING:
                            sp.wait_ge(s_lo, g - (RING - 1))
                        for dst, src in sources(stage, i, p):
                            sp.dma_start(dst(w_raw[:, p % RING, :]), src).then_inc(s_w[p % RING], 16)
                        if stage in ADA0 and p % 8 in ADA_AT:
                            u = ADA0[stage] + i * (PIECES[stage] // 8) + p // 8
                            layer = 0 if ADA0[stage] < 16 else 1
                            q = 2 * (p % 8 - ADA_AT[0])
                            load_ada(u, layer, q)
                            load_ada(u, layer, q + 1)
                return load

            for stage in last:
                if stage == "cq":
                    with sp.Fori(0, 2) as i:
                        unit(stage)(i, nothing)
                    unit(stage)(2, nothing)
                elif stage == "ret":
                    sp.wait_ge(s_yl, 8)
                    sp.dma_start(gain_bc, d["final_norm_gain"].partition_broadcast(P)).then_inc(s_gain, 16)
                    sp.dma_start(ctx_sb, d["ctx_2"].rearrange("o (t p) n -> p (o t) n", p=P)).then_inc(s_ctx, 16)
                    sp.wait_ge(s_free, UNIT0["out1"] + COUNT["out1"])
                    sp.dma_start(const_b[:, :], d["const_b"]).then_inc(s_cb, 16)
                    stage_loop(sp, stage, unit(stage), lambda p, i: None, nothing)
                else:
                    stage_loop(sp, stage, unit(stage), lambda p, i: None, nothing)
            if stop_after is None:
                sp.wait_ge(s_yl, 24)
                sp.dma_start(gain_bc, d["final_norm_w_2"].partition_broadcast(P)).then_inc(s_gain, 16)
                for t in range(TT):
                    sp.wait_ge(s_fin, TT + t + 1)
                    sp.dma_start(out[0, t * P:(t + 1) * P, :], x[:, t, :]).then_inc(s_out, 16)
                sp.wait_ge(s_out, 16 * TT)

        def view(ap, *dims):
            names = " ".join("abc"[:len(dims)])
            return ap.rearrange(f"p ({names}) -> p {names}", **dict(zip("abc", dims)))

        lru_x = view(scr_a[:, 0:518], 2, 259)
        lru_xc, lru_g, lru_gi, lru_gr, lru_r, lru_u, lru_sg = (
            scr_a[:, 518 + 512 * n:1030 + 512 * n] for n in range(7))
        gate_w = scr_a[:, 4102:4614].rearrange("p (b w n) -> p b w n", b=2, w=2)
        swa_q, swa_g = scr_a[:, 0:512], scr_a[:, 512:1024]
        swa_k, swa_v = scr_a[:, 1024:1280], view(scr_a[:, 1280:1408], TT, 64)
        swa_s, swa_t = scr_a[:, 1408:2944], scr_a[:, 2944:4480]
        at_q, at_k, at_v, at_g = (scr_a[:, 512 * n:512 * n + 512] for n in range(4))
        dif_s, dif_t = scr_a[:, 2048:3584], scr_a[:, 3584:4352]
        dif_o, dif_sq, dif_r = scr_a[:, 2048:2560], scr_a[:, 2560:3072], scr_a[:, 3072:3584]
        cq_r = view(scr_a[:, 3584:4096], 2, T)
        cq_sq = view(y[:, 0:(CQ_T + CKV_T) * T], CQ_T + CKV_T, T)
        mla_s, mla_t = scr_a[:, 2048:2816], scr_a[:, 2816:3584]
        mla_qr0, mla_qr = scr_a[0:64, 3584:4096], scr_a[0:64, 4096:4608]
        ret_qk, ret_tmp, ret_v, ret_g, ret_kc, ret_vc, ret_S, ret_D, ret_xi = (
            scr_b[:, 512 * n:512 * n + 512] for n in range(9))
        ret_sq, ret_r = ret_kc, ret_vc[:, 0:T]
        four_u, four_g = scr_b[:, 0:512], scr_b[:, 512:1024]
        four_c, four_f = view(scr_b[:, 1024:2048], 2, 512), view(scr_b[:, 2048:2560], 2, T)
        conv_x, conv_g, conv_b, conv_y = (scr_b[:, 512 * n:512 * n + 512] for n in range(4))
        conv_z = scr_b[:, 2048:2576].rearrange("p (b r n) -> p b r n", b=2, r=4)
        gate_rows = scr_b[:, 2560:4608]
        gate_diag = view(scr_b[:, 0:2048], 16, P)
        out_t = view(scr_b[:, 0:1024], TT, 512)

        def ada_cols(stage, group):
            return PS[:, {"diff": (6, 7)[group % 2], "mla": 7}.get(stage, 2), 500:506]

        def pcol(which, n, width=1):
            tile, first = which
            return pc[:, tile, ds(first + n, width)]

        def landed(eng, stage, i, p):
            per = 16 * DMAS[stage]
            eng.wait_ge(s_w[p % RING], LAND0[stage] + per * (i * (PIECES[stage] // RING) + p // RING + 1))

        def width(stage, i):
            return {"kv": 768, "ret": 768, "mla": None}.get(stage, 1024)

        def cols(stage, i, p):
            if stage == "mla":
                return 1152 if p < 2 else 1024
            if stage == "cq" and isinstance(i, int) and i == 2:
                return 640
            return width(stage, i)

        def unit_of(stage, i):
            return UNIT0[stage] + i

        def pieces_before(stage, i):
            return PIECE0[stage] + PIECES[stage] * i

        MIX_KT = {"out0": 16, "out1": 16, "out2": 32, "out3": 32}
        MIX0 = {"out0": 0, "out1": 4, "out2": 8, "out3": 16}
        NORM_BANKS = {0: 0, 1: 8, 3: 16, 4: 24, 5: 32}
        SUMS = {0: 0, 1: 1, 2: 2, 3: 3, 4: 4, 5: 5, 6: 6}
        DIAGS = {0: 0, 1: 1, 3: 2, 4: 3, 5: 4}

        def mix_dst(kt):
            return (act if kt < KT else act2), kt % KT

        @block.gpsimd
        def _(pool):
            nc.gpsimd.memset(y[:, 0:3 * P], 0.0)
            nc.gpsimd.memset(ones[:, :], 1.0).then_inc(s_set, 1)
            gx = d["l0_gate_x_w"].rearrange("b k n -> k b n")
            ga = d["l0_gate_a_w"].rearrange("b k n -> k b n")

            def gates(i):
                pool.dma_start(gate_w[:, :, 0, :], gx[:, ds(2 * i, 2), :]).then_inc(s_gw, 16)
                pool.dma_start(gate_w[:, :, 1, :], ga[:, ds(2 * i, 2), :]).then_inc(s_gw, 16)

            gates(0)
            with pool.Fori(1, COUNT["lru"]) as i:
                pool.wait_ge(S["lru"]["gates"], i)
                gates(i)
            if wanted("four"):
                f = d["fno_w_2"].rearrange("o g (c p) n -> p (o g) c n", p=P)
                pool.wait_ge(s_cb, 16)
                pool.dma_start(fno[:, :, :], f[:, 0, :, :]).then_inc(s_fno, 16)
                with pool.Fori(1, COUNT["four"]) as i:
                    pool.wait_ge(S["four"]["o"], i)
                    pool.dma_start(fno[:, :, :], f[:, ds(i, 1), :, :].rearrange("p g c n -> p (g c) n"))\
                        .then_inc(s_fno, 16)

        @block.scalar
        def _(sc):
            def split(stage):
                def run(i, hook):
                    for p in range(PIECES[stage]):
                        g = pieces_before(stage, i) + p
                        n = cols(stage, i, p)
                        landed(sc, stage, i, p)
                        if not isinstance(g, int) or g >= RING:
                            sc.wait_ge(s_used, g - (RING - 1))
                        nc.scalar.activation(w_hi[:, p % RING, 0:n], w_raw[:, p % RING, 0:n], ACT.Copy)\
                            .then_inc(s_hi, 1)
                        hook(p)
                return run

            def projected(stage, i):
                sc.wait_ge(s_used, pieces_before(stage, i) + PIECES[stage])

            def copy(dst, src, **k):
                return nc.scalar.activation(dst, src, ACT.Copy, **k)

            def norm(k, src, ready, dst):
                ready()
                for t in range(TT):
                    nc.scalar.drain()
                    last = nc.scalar.activation(junk, src[:, t, :], ACT.Square, accum_out=stat[:, 0, t:t + 1])
                last.then_inc(s_n["sum"], 1)
                sc.wait_ge(s_n["mean"], SUMS[k] + 1)
                nc.scalar.activation(stat[:, 2, :], stat[:, 1, :], ACT.Sqrt).then_inc(s_n["root"], 1)
                if dst is None:
                    return
                scratch = scr_a if k < 2 else scr_b
                for b in range(8):
                    sc.wait_ge(s_n["tile"], NORM_BANKS[k] + b + 1)
                    copy(dst[:, 2 * b:2 * b + 2, 0:T], halves(scratch[:, (b % 4) * 512:(b % 4 + 1) * 512]))\
                        .then_inc(s_n["hi"], 1)

            def mix(stage):
                for q in range(MIX_KT[stage] // 4):
                    dst, kt = mix_dst(4 * q)
                    copy(dst[:, kt:kt + 4, 0:T], yt[:, 4 * q:4 * q + 4, :]).then_inc(s_yh, 1)

            def lru(p, i):
                s = S["lru"]
                if p == 2:
                    projected("lru", i)
                    if not isinstance(i, int) or i > 0:
                        sc.wait_ge(s["y"], i + 1)
                    copy(lru_x[:, :, 3:259], halves(bank(A)))
                    copy(lru_g, bank(B))
                    nc.scalar.activation(lru_sg, bank(B), ACT.Sigmoid).then_inc(s_free, 1)
                if p == 5:
                    sc.wait_ge(s["gates"], i + 1)
                    for b in range(2):
                        nc.scalar.activation(halves(lru_gi)[:, b, :], halves(bank(4))[:, b, :], ACT.Sigmoid,
                                             bias=pcol(GX_B, 2 * i + b))
                        nc.scalar.activation(halves(lru_gr)[:, b, :], halves(bank(5))[:, b, :], ACT.Sigmoid,
                                             bias=pcol(GA_B, 2 * i + b))
                    nc.scalar.drain()
                    for b in range(2):
                        nc.scalar.activation(halves(lru_gr)[:, b, :], halves(lru_gr)[:, b, :], ACT.Tanh,
                                             scale=lru_c[:, 0, ds(2 * i + b, 1)])
                    nc.scalar.drain()
                    nc.scalar.activation(lru_u, lru_gr, ACT.Sqrt, scale=-1.0).then_inc(s["sig"], 1)

            def kv(p, i=0):
                if p == 2:
                    projected("kv", 0)
                    for h in range(4):
                        copy(kT4[:, h, :], halves(bank(A))[:, h // 2, :])
                        last = copy(v4[:, h, :, :], bank(B)[:, 0:256].rearrange("p (t g n) -> p t g n", t=2, g=2)
                                    [:, :, h // 2, :])
                    last.then_inc(s_free, 1)

            def exps(s_tile, n, ready, done, sink):
                ready()
                if sink:
                    nc.scalar.activation(soft[:, 3, :], soft[:, 3, :], ACT.Exp)
                v = s_tile.rearrange("p (h c) -> p h c", c=384)
                for h in range(n):
                    for b, (lo, hi) in enumerate(((0, 128), (128, 384))):
                        last = nc.scalar.activation(v[:, h, lo:hi], v[:, h, lo:hi], ACT.Exp,
                                                    bias=soft[:, 1, 2 * h + b:2 * h + b + 1],
                                                    accum_out=soft[:, 2, 2 * h + b:2 * h + b + 1])
                last.then_inc(done, 1)

            def swa(p, i):
                s = S["swa"]
                if p == 2:
                    projected("swa", i)
                    if isinstance(i, int) and i == 0:
                        sc.wait_ge(S["lru"]["y"], COUNT["lru"] + 1)
                    else:
                        sc.wait_ge(s["y"], i + 1)
                    copy(swa_q, bank(A), scale=SWA_D ** -0.5)
                    copy(swa_k, kT4[:, ds(i, 1), :].rearrange("p a n -> p (a n)"))
                    copy(swa_v, v4[:, ds(i, 1), :, :].rearrange("p a t n -> p (a t) n"))
                    nc.scalar.activation(swa_g, bank(B), ACT.Silu).then_inc(s_free, 1)
                if p == 4:
                    exps(swa_s, 4, lambda: sc.wait_ge(s["max"], i + 1), s["exp"], True)
                if p == 6:
                    sc.wait_ge(s["probT"], i + 1)
                    copy(view(swa_t, 4, 384), PS[:, 4:8, 0:384]).then_inc(s["probT_sb"], 1)

            def cq_evac(i, last):
                projected("cq", i)
                if not last:
                    copy(zc[:, ds(4 * i, 2), :], halves(bank(A)))
                    copy(zc[:, ds(4 * i + 2, 2), :], halves(bank(B))).then_inc(s_free, 1)
                else:
                    copy(zc[:, 8:10, :], halves(bank(A)))
                    copy(k_raw[:, :], PS[0:64, B, 0:T]).then_inc(s_free, 1)

            def cq(p, i):
                if p == 2:
                    cq_evac(i, False)

            def cq_end(p, i=2):
                s = S["cq"]
                if p == 2:
                    cq_evac(2, True)
                    nc.scalar.drain()
                    nc.scalar.activation(cq_sq, zc, ACT.Square).then_inc(s["squares"], 1)
                if p == 6:
                    sc.wait_ge(s["mean"], 1)
                    nc.scalar.activation(cq_r, cq_r, ACT.Sqrt).then_inc(s["root"], 1)
                if p == 8:
                    sc.wait_ge(s["gained"], 1)
                    copy(cn[:, :, 0:T], zc).then_inc(s["hi"], 1)

            def diff(p, i):
                s = S["diff"]
                if p == 2:
                    projected("diff", i)
                    if isinstance(i, int) and i == 0:
                        sc.wait_ge(S["cq"]["lo"], 1)
                    else:
                        sc.wait_ge(s["y"], i + 1)
                    copy(at_q, bank(A), scale=64 ** -0.5)
                    copy(at_k, bank(B))
                    copy(at_v, bank(3))
                    nc.scalar.activation(at_g, bank(C), ACT.Silu).then_inc(s_free, 1)
                if p == 6:
                    exps(dif_s, 4, lambda: sc.wait_ge(s["max"], i + 1), s["exp"], False)
                if p == 10:
                    sc.wait_ge(s["probT"], i + 1)
                    copy(view(dif_t, 2, 384), PS[:, 4:6, 0:384]).then_inc(s["probT_sb"], 1)
                if p == 12:
                    sc.wait_ge(s["o"], i + 1)
                    copy(dif_o, bank(6))
                    nc.scalar.activation(dif_sq, bank(6), ACT.Square).then_inc(s["sq"], 1)
                if p == 14:
                    sc.wait_ge(s["mean"], i + 1)
                    nc.scalar.activation(dif_r, dif_r, ACT.Sqrt).then_inc(s["root"], 1)

            def mla(p, i):
                s = S["mla"]
                if p == 2:
                    projected("mla", i)
                    if isinstance(i, int) and i == 0:
                        sc.wait_ge(S["diff"]["y"], COUNT["diff"] + 1)
                    else:
                        sc.wait_ge(s["y"], i + 1)
                    copy(mla_qr0, PS[0:64, 4, :], scale=MLA_SCALE)
                    copy(at_q, bank(A), scale=MLA_SCALE)
                    copy(at_k, bank(B))
                    copy(at_v, bank(3))
                    nc.scalar.activation(at_g, bank(C), ACT.Silu).then_inc(s_free, 1)
                if p == 4:
                    exps(mla_s, 2, lambda: sc.wait_ge(s["max"], i + 1), s["exp"], False)
                if p == 6:
                    sc.wait_ge(s["probT"], i + 1)
                    copy(view(mla_t, 2, 384), PS[:, 5:7, 0:384]).then_inc(s["probT_sb"], 1)

            def ret(p, i):
                s = S["ret"]
                if p == 1:
                    sc.wait_ge(s["arg"], i + 1)
                    nc.scalar.activation(ret_D, ret_D, ACT.Exp)
                    nc.scalar.activation(ret_xi[:, 0:T], pow_up, ACT.Exp, scale=lg[:, ds(i, 1)])
                    nc.scalar.activation(ret_xi[:, T:], pow_dn, ACT.Exp, scale=lg[:, ds(i + RET_H, 1)])\
                        .then_inc(s["tables"], 1)
                if p == 2:
                    projected("ret", i)
                    if not isinstance(i, int) or i > 0:
                        sc.wait_ge(s["y"], i + 1)
                    copy(ret_qk, bank(A))
                    copy(ret_v, bank(C))
                    for t in range(TT):
                        ctx_k, ctx_v = PS[:, 3 + t, 0:P], PS[:, 3 + t, P:384]
                        for n in range(2):
                            wcol = state_w[:, ds(i, 1), 2 * n + t:2 * n + t + 1].rearrange("p a b -> p (a b)")
                            copy(ret_kc[:, (2 * n + t) * P:(2 * n + t + 1) * P], ctx_k, scale=wcol)
                        copy(ret_vc[:, t * T:(t + 1) * T], ctx_v)
                    nc.scalar.activation(ret_g, bank(B), ACT.Silu).then_inc(s_free, 1)
                if p == 4:
                    sc.wait_ge(s["state"], i + 1)
                    copy(ret_S, bank(6)).then_inc(s["state_sb"], 1)
                if p == 11:
                    sc.wait_ge(s["o"], i + 1)
                    nc.scalar.activation(ret_sq, bank(5), ACT.Square).then_inc(s["sq"], 1)
                if p == 13:
                    sc.wait_ge(s["mean"], i + 1)
                    nc.scalar.activation(ret_r, ret_r, ACT.Sqrt).then_inc(s["root"], 1)

            def four(p, i):
                s = S["four"]
                if p == 2:
                    projected("four", i)
                    if isinstance(i, int) and i == 0:
                        sc.wait_ge(S["ret"]["y"], COUNT["ret"] + 1)
                    else:
                        sc.wait_ge(s["y"], i + 1)
                    copy(four_u, bank(A))
                    nc.scalar.activation(four_g, bank(B), ACT.Silu).then_inc(s_free, 1)
                if p == 4:
                    sc.wait_ge(s["cols"], i + 1)
                    copy(four_c, PS[:, 4:6, :]).then_inc(s["cols_sb"], 1)
                if p == 6:
                    sc.wait_ge(s["rows"], i + 1)
                    copy(four_f, halves(bank(6))).then_inc(s["rows_sb"], 1)

            def conv(p, i):
                s = S["conv"]
                if p == 2:
                    projected("conv", i)
                    if not isinstance(i, int) or i > 0:
                        sc.wait_ge(s["y"], i + 1)
                    copy(conv_x, bank(C))
                    copy(conv_b, bank(A))
                    nc.scalar.activation(conv_g, bank(3), ACT.Silu).then_inc(s["evac"], 1)

            def gate_rows_copy(n):
                sc.wait_ge(s_gb, n)
                copy(view(gate_rows, 4, 512), PS[:, 4:8, :]).then_inc(s_gr, 1)

            def none(p, i):
                pass

            sc.wait_ge(s_pc, 1)
            nc.scalar.activation(silu_c[:, 0, :], pc[:, 1, C_X[1]:C_X[1] + KT], ACT.Silu)
            nc.scalar.activation(silu_c[:, 1, :], pc[:, 2, C_CTX[1]:C_CTX[1] + KT], ACT.Silu)
            nc.scalar.activation(lru_c[:, 1, :], pc[:, 0, LAM[1]:LAM[1] + 8], ACT.Abs)
            nc.scalar.drain()
            nc.scalar.activation(lru_c[:, 1, :], lru_c[:, 1, :], ACT.Exp, scale=-1.0)
            nc.scalar.activation(lg[:, :], lg[:, :], ACT.Exp)
            nc.scalar.activation(nlam[:, :], nlam[:, :], ACT.Exp).then_inc(s_pe_, 1)

            norm(0, x, lambda: sc.wait_ge(s_x, 16), act)
            stage_loop(sc, "lru", split("lru"), lru, nothing)
            if wanted("kv"):
                split("kv")(0, lambda p: lru(p, COUNT["lru"] - 1))
                stage_loop(sc, "swa", split("swa"), swa, kv)
                at_end(swa, COUNT["swa"] - 1, 8)
            if wanted("out0"):
                sc.wait_ge(S["swa"]["y"], COUNT["swa"] + 1)
                sc.wait_ge(s_used, pieces_before("out0", 0))
                mix("out0")
                stage_loop(sc, "out0", split("out0"), none, nothing)
            if wanted("cq"):
                norm(1, x, lambda: sc.wait_ge(s_free, UNIT0["cq"]), act)
                split("cq")(0, nothing)
                with sc.Fori(1, 2) as i:
                    split("cq")(i, lambda p: cq(p, i - 1))
                split("cq")(2, lambda p: cq(p, 1))
            if wanted("diff"):
                stage_loop(sc, "diff", split("diff"), diff, cq_end)
                at_end(diff, COUNT["diff"] - 1, 16)
                stage_loop(sc, "mla", split("mla"), mla, nothing)
                at_end(mla, COUNT["mla"] - 1, 8)
            if wanted("out1"):
                sc.wait_ge(S["mla"]["y"], COUNT["mla"] + 1)
                sc.wait_ge(s_used, pieces_before("out1", 0))
                mix("out1")
                stage_loop(sc, "out1", split("out1"), none, nothing)
            if wanted("ret"):
                norm(2, x, lambda: sc.wait_ge(s_free, UNIT0["ret"]), None)
                sc.wait_ge(s_dec, 1)
                nc.scalar.activation(state_w[:, :, :], state_w[:, :, :], ACT.Exp).then_inc(s_stw, 1)
                norm(3, ctx_sb, lambda: sc.wait_ge(s_ctx, 16), act2)
                norm(4, x, lambda: sc.wait_ge(s_fin, TT), act)
                sc.wait_ge(s_stw, 2)
                stage_loop(sc, "ret", split("ret"), ret, nothing)
            if wanted("four"):
                stage_loop(sc, "four", split("four"), four, squeezed(ret, COUNT["ret"] - 1))
                at_end(four, COUNT["four"] - 1, 8)
            if wanted("out2"):
                sc.wait_ge(S["four"]["y"], COUNT["four"] + 1)
                sc.wait_ge(s_used, pieces_before("out2", 0))
                mix("out2")
                gate_rows_copy(1)
                stage_loop(sc, "out2", split("out2"), none, nothing)
            if wanted("conv"):
                norm(5, x, lambda: sc.wait_ge(s_free, UNIT0["conv"]), act)
                stage_loop(sc, "conv", split("conv"), conv, nothing)
                at_end(conv, COUNT["conv"] - 1, 16)
            if wanted("out3"):
                sc.wait_ge(S["conv"]["y"], COUNT["conv"] + 1)
                sc.wait_ge(s_used, pieces_before("out3", 0))
                mix("out3")
                gate_rows_copy(2)
                stage_loop(sc, "out3", split("out3"), none, nothing)
                norm(6, x, lambda: sc.wait_ge(s_free, UNIT0["out3"] + COUNT["out3"]), None)

        @block.vector
        def _(ve):
            drain = nc.vector.drain
            tt = nc.vector.tensor_tensor
            stt = nc.vector.scalar_tensor_tensor
            ts = nc.vector.tensor_scalar

            def ada_column(u, context, sums):
                ve.wait_ge(s_aps, u)
                r = tt(ada_x[:, ds(3 * (u - 1), 3)], sums[:, 0:3], pcol(ADA_B, 3 * (u - 1), 3), ALU.add)
                if context:
                    r = tt(ada_c[:, ds(3 * (u - 1), 3)], sums[:, 3:6], pcol(ADA_B, 3 * (u - 1), 3), ALU.add)
                r.then_inc(s_acol, 1)

            def ada_piece(u, q, context):
                ve.wait_ge(s_aw[q % ADA_RING], 16 * (u * 2 + q // ADA_RING + 1))
                for t in range(2):
                    kt = 2 * q + t
                    w = ada_ring[:, q % ADA_RING, t * ADA_COLS:(t + 1) * ADA_COLS]
                    for n, acc in enumerate((acc_c, acc_x)):
                        if n == 0 and not context:
                            continue
                        cond = silu_c[:, 1 - n, kt:kt + 1]
                        if kt == 0:
                            last = ts(acc[:, :], w, cond, None, ALU.mult)
                        else:
                            last = stt(acc[:, :], w, cond, acc[:, :], ALU.mult, ALU.add)
                    if t == 0:
                        drain()
                last.then_inc(s_au, 1)
                drain()

            def split(stage):
                def run(i, hook):
                    for p in range(PIECES[stage]):
                        g = pieces_before(stage, i) + p
                        n = cols(stage, i, p)
                        ve.wait_ge(s_hi, g + 1)
                        tt(w_lo[:, p % RING, 0:n], w_raw[:, p % RING, 0:n], w_hi[:, p % RING, 0:n].bitcast(F32),
                           ALU.subtract).then_inc(s_lo, 1)
                        hook(p)
                        if stage in ADA0 and p % 8 in ADA_AT:
                            u = ADA0[stage] + i * (PIECES[stage] // 8) + p // 8
                            context = ADA0[stage] < 16
                            q = 2 * (p % 8 - ADA_AT[0])
                            if q == 0 and not (isinstance(u, int) and u == 0):
                                ada_column(u, context or (isinstance(u, int) and u == 16), ada_cols(stage, p // 8))
                            ada_piece(u, q, context)
                            ada_piece(u, q + 1, context)
                return run

            def root(k):
                ve.wait_ge(s_n["sum"], SUMS[k] + 1)
                ts(stat[:, 1, :], stat[:, 0, :], 1.0 / D, EPS, ALU.mult, ALU.add).then_inc(s_n["mean"], 1)
                ve.wait_ge(s_n["root"], SUMS[k] + 1)
                nc.vector.reciprocal(stat[:, 3, :], stat[:, 2, :])
                drain()
                tt(stat[:, 2, :], stat[:, 3, :], stat[:, 3, :], ALU.mult)
                drain()
                tt(stat[:, 2, :], stat[:, 2, :], stat[:, 1, :], ALU.mult)
                drain()
                ts(stat[:, 2, :], stat[:, 2, :], -0.5, 1.5, ALU.mult, ALU.add)
                drain()
                tt(stat[:, 3, :], stat[:, 3, :], stat[:, 2, :], ALU.mult)
                drain()

            def norm(k, gain, bias, dst, scratch):
                root(k)
                diag = view(scratch[:, 2048:2304], TT, P)
                for t in range(TT):
                    last = ts(diag[:, t, :], ident[:, :], stat[:, 3, t:t + 1], None, ALU.mult)
                last.then_inc(s_n["diag"], 1)
                def low(b):
                    tmp = scratch[:, (b % 4) * 512:(b % 4 + 1) * 512]
                    ve.wait_ge(s_n["hi"], NORM_BANKS[k] + b + 1)
                    tt(dst[:, 2 * b:2 * b + 2, T:2 * T], halves(tmp), dst[:, 2 * b:2 * b + 2, 0:T].bitcast(F32),
                       ALU.subtract).then_inc(s_n["lo"], 1)

                for b in range(8):
                    tmp = scratch[:, (b % 4) * 512:(b % 4 + 1) * 512]
                    ve.wait_ge(s_n["psum"], NORM_BANKS[k] + b + 1)
                    for h, f in enumerate((2 * b, 2 * b + 1)):
                        last = ts(tmp[:, h * T:(h + 1) * T], PS[:, b, h * T:(h + 1) * T], gain(f),
                                  0.0 if bias is None else bias(f), ALU.mult, ALU.add)
                    last.then_inc(s_n["tile"], 1)
                    if b > 0:
                        low(b - 1)
                drain()
                low(7)

            def scaled(k, n):
                root(k)
                ve.wait_ge(s_gain, 16 * n)
                for t in range(TT):
                    stt(x[:, t, :], x[:, t, :], stat[:, 3, t:t + 1], gain_bc, ALU.mult, ALU.mult)\
                        .then_inc(s_fin, 1)

            def mix(stage):
                for q in range(MIX_KT[stage] // 4):
                    dst, kt = mix_dst(4 * q)
                    ve.wait_ge(s_yh, MIX0[stage] + q + 1)
                    tt(dst[:, kt:kt + 4, T:2 * T], yt[:, 4 * q:4 * q + 4, :], dst[:, kt:kt + 4, 0:T].bitcast(F32),
                       ALU.subtract).then_inc(s_yl, 1)

            def lru(p, i):
                s = S["lru"]
                if p == 3:
                    ve.wait_ge(s_free, unit_of("lru", i) + 1)
                    xc = halves(lru_xc)
                    for b in range(2):
                        ts(xc[:, b, :], lru_x[:, b, 3:259], pcol(CONV_W, 24 + 2 * i + b),
                           pcol(CONV_B, 2 * i + b), ALU.mult, ALU.add)
                    for tap in range(3):
                        drain()
                        for b in range(2):
                            last = stt(xc[:, b, :], lru_x[:, b, tap:tap + T], pcol(CONV_W, 8 * tap + 2 * i + b),
                                       xc[:, b, :], ALU.mult, ALU.add)
                    last.then_inc(s["conv"], 1)
                if p == 6:
                    ve.wait_ge(s["sig"], i + 1)
                    ts(lru_r, lru_gr, -1.0, 1.0, ALU.mult, ALU.add)
                    drain()
                    nc.vector.reciprocal(lru_r, lru_r)
                    drain()
                    stt(lru_u, lru_u, 2.0, lru_r, ALU.mult, ALU.mult)
                    stt(lru_gr, lru_gr, 1.0, lru_r, ALU.add, ALU.mult)
                    drain()
                    tt(lru_u, lru_u, lru_gi, ALU.mult)
                    drain()
                    tt(lru_u, lru_u, lru_xc, ALU.mult)
                    drain()
                    for b in range(2):
                        nc.vector.tensor_tensor_scan(halves(lru_gi)[:, b, :], halves(lru_gr)[:, b, :],
                                                     halves(lru_u)[:, b, :], 0.0, ALU.mult, ALU.add)
                    drain()
                    tt(lru_gi, lru_gi, lru_g, ALU.mult)
                    drain()
                    tt(yt[:, ds(2 * i, 2), :], halves(lru_gi), halves(lru_sg), ALU.mult).then_inc(s["y"], 1)

            def kv(p, i=0):
                pass

            def scores_max(s_tile, n, mask, first_bank, done, sink):
                v = s_tile.rearrange("p (h c) -> p h c", c=384)
                tt(v, PS[:, first_bank:first_bank + n, 0:384], mask.unsqueeze(1).broadcast_to([P, n, 384]), ALU.add)
                drain()
                mx = soft[:, 0, 0:2 * n].rearrange("p (h b) -> p h b", b=2)
                nc.vector.tensor_reduce(mx[:, :, 0], v[:, :, 0:128], AX, ALU.max)
                nc.vector.tensor_reduce(mx[:, :, 1], v[:, :, 128:384], AX, ALU.max)
                drain()
                if sink is not None:
                    tt(mx, mx, sink, ALU.max)
                    drain()
                    tt(soft[:, 3, :].rearrange("p (h b) -> p h b", b=2), sink, mx, ALU.subtract)
                ts(soft[:, 1, 0:2 * n], soft[:, 0, 0:2 * n], -1.0, None, ALU.mult).then_inc(done, 1)

            def normalise(s_tile, n, weight):
                v = s_tile.rearrange("p (h c) -> p h c", c=384)
                r = soft[:, 4, 0:2 * n].rearrange("p (h b) -> p h b", b=2)
                nc.vector.reciprocal(soft[:, 4, 0:2 * n], soft[:, 2, 0:2 * n])
                drain()
                if weight is not None:
                    weight(soft[:, 4, 0:2 * n])
                    drain()
                tt(v[:, :, 0:128], v[:, :, 0:128], r[:, :, 0:1].broadcast_to([P, n, 128]), ALU.mult)
                return tt(v[:, :, 128:384], v[:, :, 128:384], r[:, :, 1:2].broadcast_to([P, n, 256]), ALU.mult)

            def swa(p, i):
                s = S["swa"]
                if p == 4:
                    ve.wait_ge(s["scores"], i + 1)
                    sink = sinks[:, ds(4 * i, 4)].unsqueeze(2).broadcast_to([P, 4, 2])
                    scores_max(swa_s, 4, band, 4, s["max"], sink)
                if p == 5:
                    ve.wait_ge(s["exp"], i + 1)
                    tt(soft[:, 2, :], soft[:, 2, :], soft[:, 3, :], ALU.add)
                    drain()
                    normalise(swa_s, 4, None).then_inc(s["prob"], 1)
                if p == 7:
                    ve.wait_ge(s["o"], i + 1)
                    tt(yt[:, ds(2 * i + 8, 2), :], halves(bank(4)), halves(swa_g), ALU.mult).then_inc(s["y"], 1)

            def cq_end(p, i=2):
                s = S["cq"]
                if p == 6:
                    ve.wait_ge(s["sums"], 1)
                    ts(cq_r[:, 0, :], PS[:, 5, 0:T], 1.0 / Q_RANK, EPS, ALU.mult, ALU.add)
                    ts(cq_r[:, 1, :], PS[:, 7, 0:T], 1.0 / KV_RANK, EPS, ALU.mult, ALU.add).then_inc(s["mean"], 1)
                    rot = at_q[0:64, 0:T]
                    tt(rot, PS[0:64, 4, 0:T], sin64, ALU.mult)
                    tt(k_rot[:, :], k_raw[:, :], cos64, ALU.mult)
                    drain()
                    tt(k_rot[:, :], k_rot[:, :], rot, ALU.add)
                if p == 7:
                    ve.wait_ge(s["root"], 1)
                    nc.vector.reciprocal(cq_r, cq_r)
                    drain()
                    for t in range(CQ_T + CKV_T):
                        gain = pcol(G_Q, t) if t < CQ_T else pcol(G_KV, t - CQ_T)
                        last = stt(zc[:, t, :], zc[:, t, :], gain, cq_r[:, 0 if t < CQ_T else 1, :],
                                   ALU.mult, ALU.mult)
                    last.then_inc(s["gained"], 1)
                if p == 9:
                    ve.wait_ge(s["hi"], 1)
                    tt(cn[:, :, T:2 * T], zc, cn[:, :, 0:T].bitcast(F32), ALU.subtract).then_inc(s["lo"], 1)

            def diff(p, i):
                s = S["diff"]
                if p == 6:
                    ve.wait_ge(s["scores"], i + 1)
                    scores_max(dif_s, 4, causal, 4, s["max"], None)
                if p == 8:
                    ve.wait_ge(s["exp"], i + 1)

                    def second(r):
                        r = r.rearrange("p (h c b) -> p h c b", h=2, c=2)[:, :, 1, :]
                        ts(r, r, nlam[:, 0:1], None, ALU.mult)
                    normalise(dif_s, 4, second)
                    drain()
                    v = dif_s.rearrange("p (h c n) -> p h c n", h=2, c=2)
                    tt(v[:, :, 0, :], v[:, :, 0, :], v[:, :, 1, :], ALU.add).then_inc(s["prob"], 1)
                if p == 14:
                    ve.wait_ge(s["sum"], i + 1)
                    ts(dif_r, bank(4), 1.0 / 128, EPS, ALU.mult, ALU.add).then_inc(s["mean"], 1)
                if p == 15:
                    ve.wait_ge(s["root"], i + 1)
                    nc.vector.reciprocal(dif_r, dif_r)
                    drain()
                    stt(dif_o, dif_o, sub_g[:, :], dif_r, ALU.mult, ALU.mult)
                    drain()
                    tt(yt[:, ds(2 * i + 8, 2), :], halves(dif_o), halves(at_g), ALU.mult).then_inc(s["y"], 1)

            def mla(p, i):
                s = S["mla"]
                if p == 3:
                    ve.wait_ge(s["rot"], i + 1)
                    v0, v1 = halves(mla_qr0), halves(mla_qr)
                    tt(v1, halves(PS[0:64, 5, :]), sin64.unsqueeze(1).broadcast_to([64, 2, T]), ALU.mult)
                    tt(v0, v0, cos64.unsqueeze(1).broadcast_to([64, 2, T]), ALU.mult)
                    drain()
                    tt(v1, v1, v0, ALU.add).then_inc(s["rope"], 1)
                if p == 4:
                    ve.wait_ge(s["scores"], i + 1)
                    scores_max(mla_s, 2, causal, 5, s["max"], None)
                if p == 5:
                    ve.wait_ge(s["exp"], i + 1)
                    normalise(mla_s, 2, None).then_inc(s["prob"], 1)
                if p == 7:
                    ve.wait_ge(s["o"], i + 1)
                    tt(yt[:, ds(2 * i, 2), :], halves(bank(5)), halves(at_g), ALU.mult).then_inc(s["y"], 1)

            def ret(p, i):
                s = S["ret"]
                if p == 0:
                    ts(ret_D, rel_up, lg[:, ds(i, 1)], None, ALU.mult)
                    drain()
                    stt(ret_D, rel_dn, lg[:, ds(i + RET_H, 1)], ret_D, ALU.mult, ALU.add).then_inc(s["arg"], 1)
                if p == 4:
                    ve.wait_ge(s["rot"], i + 1)
                    tt(halves(ret_tmp), halves(bank(5)), sin128.unsqueeze(1).broadcast_to([P, 2, T]), ALU.mult)
                    tt(halves(ret_qk), halves(ret_qk), cos128.unsqueeze(1).broadcast_to([P, 2, T]), ALU.mult)
                    drain()
                    tt(ret_qk, ret_qk, ret_tmp, ALU.add).then_inc(s["rope"], 1)
                if p == 5:
                    drain()
                    ve.wait_ge(s["tables"], i + 1)
                    q2 = ret_qk[:, 0:T].unsqueeze(1).broadcast_to([P, 2, T])
                    tt(halves(ret_xi), halves(ret_xi), q2, ALU.mult).then_inc(s["scaled"], 1)
                if p == 8:
                    ve.wait_ge(s["scores"], i + 1)
                    stt(ret_tmp, bank(7), K_SCALE, ret_D, ALU.mult, ALU.mult).then_inc(s["decayed"], 1)
                if p == 13:
                    ve.wait_ge(s["sum"], i + 1)
                    ts(ret_r, PS[:, 6, 0:T], 1.0 / T, EPS, ALU.mult, ALU.add).then_inc(s["mean"], 1)
                if p == 14:
                    ve.wait_ge(s["root"], i + 1)
                    nc.vector.reciprocal(ret_r, ret_r)
                    drain()
                    r2 = ret_r.unsqueeze(1).broadcast_to([P, 2, T])
                    tt(halves(ret_v), halves(bank(5)), r2, ALU.mult)
                    drain()
                    tt(yt[:, ds(2 * i, 2), :], halves(ret_v), halves(ret_g), ALU.mult).then_inc(s["y"], 1)

            def four(p, i):
                s = S["four"]
                if p == 7:
                    ve.wait_ge(s["o"], i + 1)
                    tt(yt[:, ds(2 * i + 16, 2), :], halves(bank(7)), halves(four_g), ALU.mult).then_inc(s["y"], 1)

            def conv(p, i):
                s = S["conv"]
                if p == 3:
                    ve.wait_ge(s["evac"], i + 1)
                    rows = "p (b r n) -> p b r n"
                    z, v = conv_z, conv_y.rearrange(rows, b=2, r=4)
                    tt(z[:, :, :, 1:65], bank(B).rearrange(rows, b=2, r=4), conv_x.rearrange(rows, b=2, r=4),
                       ALU.mult).then_inc(s_free, 1)
                    drain()
                    for tap in (1, 0, 2):
                        for b in range(2):
                            w = pcol(CONV3_W, 32 * tap + 2 * i + b)
                            zs = z[:, b, :, tap:tap + 64]
                            if tap == 1:
                                ts(v[:, b, :, :], zs, w, None, ALU.mult)
                            else:
                                stt(v[:, b, :, :], zs, w, v[:, b, :, :], ALU.mult, ALU.add)
                        drain()
                    tt(conv_y, conv_y, conv_b, ALU.mult)
                    drain()
                    tt(yt[:, ds(2 * i, 2), :], halves(conv_y), halves(conv_g), ALU.mult).then_inc(s["y"], 1)

            def out_of(stage):
                def add(p, i):
                    if p != 2:
                        return
                    ve.wait_ge(s_used, pieces_before(stage, i) + PIECES[stage])
                    xs = x[:, :, ds(512 * i, 512)]
                    if stage in ("out0", "out1"):
                        tt(xs, xs, PS[:, A:A + 2, :], ALU.add).then_inc(s_free, 1)
                        return
                    g = gate_rows[:, ds(512 * i, 512)].unsqueeze(1).broadcast_to([P, TT, 512])
                    tt(out_t, PS[:, A:A + 2, :], g, ALU.mult)
                    drain()
                    tt(xs, xs, out_t, ALU.add).then_inc(s_free, 1)
                return add

            def gate_diags(n, first):
                for q in range(16):
                    ts(gate_diag[:, q, :], ident[:, :], ada_x[:, first + q:first + q + 1], None, ALU.mult)\
                        .then_inc(s_gd, 1)
                ve.wait_ge(s_gr, n)

            def mod_gain(k, norm_col, scale):
                stt(modc[:, k, :], scale, 1.0, norm_col, ALU.add, ALU.mult)
                drain()

            for stage in ("lru", "swa", "diff", "mla", "ret", "four", "conv"):
                ve.sem_inc(S[stage]["y"], 1)
            ve.wait_ge(s_pps, 1)
            nc.vector.tensor_copy(pc[:, :, :], PS[:, 0, 0:3 * P].rearrange("p (t n) -> p t n", t=3))
            for n in range(2):
                prod = lam_rows[:, 2 * n, :]
                tt(prod, prod, lam_rows[:, 2 * n + 1, :], ALU.mult)
            drain()
            for n in range(2):
                nc.vector.tensor_reduce(nlam[:, n:n + 1], lam_rows[:, 2 * n, :], AX, ALU.add)
            drain()
            ts(sub_g[:, :], pcol(G_SUB, 0), 1.0 - LAMBDA_INIT, None, ALU.mult).then_inc(s_pc, 1)
            ve.wait_ge(s_pe_, 1)
            ts(lg[:, :], lg[:, :], -1.0, None, ALU.mult)
            tt(nlam[:, 0:1], nlam[:, 1:2], nlam[:, 0:1], ALU.subtract)
            e, z, z2, acc = (lru_c[:, k, :] for k in (1, 2, 3, 0))
            ts(z, e, 2.0, None, ALU.add)
            drain()
            ts(nlam[:, 0:1], nlam[:, 0:1], -LAMBDA_INIT, None, ALU.add)
            nc.vector.reciprocal(z, z)
            drain()
            tt(z, z, e, ALU.mult)
            drain()
            tt(z2, z, z, ALU.mult)
            drain()
            ts(acc, z2, 1.0 / 17, None, ALU.mult)
            for k in range(15, 1, -2):
                drain()
                stt(acc, acc, 1.0 / k, z2, ALU.add, ALU.mult)
            drain()
            stt(acc, acc, 1.0, z, ALU.add, ALU.mult)
            ts(e, pc[:, 0, LAM[1]:LAM[1] + 8], -1.0, 0.0, ALU.mult, ALU.max)
            drain()
            ts(acc, acc, 2.0, None, ALU.mult)
            drain()
            tt(acc, acc, e, ALU.add)
            drain()
            ts(acc, acc, -4.0, None, ALU.mult).then_inc(s_pc, 1)

            def none(p, i):
                pass

            ve.wait_ge(s_x, 16)
            norm(0, lambda f: pcol(G_L0, f), None, act, scr_a)
            drain()
            nc.vector.memset(lru_x, 0.0)
            drain()
            stage_loop(ve, "lru", split("lru"), lru, nothing)
            if wanted("kv"):
                split("kv")(0, lambda p: lru(p, COUNT["lru"] - 1))
                stage_loop(ve, "swa", split("swa"), swa, kv)
                at_end(swa, COUNT["swa"] - 1, 8)
            if wanted("out0"):
                mix("out0")
                add = out_of("out0")
                stage_loop(ve, "out0", split("out0"), add, nothing)
                add(2, COUNT["out0"] - 1)
            if wanted("cq"):
                drain()
                norm(1, lambda f: pcol(G_L1, f), None, act, scr_a)
                split("cq")(0, nothing)
                with ve.Fori(1, 2) as i:
                    split("cq")(i, nothing)
                split("cq")(2, nothing)
            if wanted("diff"):
                stage_loop(ve, "diff", split("diff"), diff, cq_end)
                at_end(diff, COUNT["diff"] - 1, 16)
                stage_loop(ve, "mla", split("mla"), mla, nothing)
                at_end(mla, COUNT["mla"] - 1, 8)
            if wanted("out1"):
                mix("out1")
                add = out_of("out1")
                stage_loop(ve, "out1", split("out1"), add, nothing)
                add(2, COUNT["out1"] - 1)
                ada_column(ADA_SLABS, False, ada_cols("out1", 0))
            if wanted("ret"):
                drain()
                scaled(2, 1)
                mod_gain(0, pc[:, 0, G_MOD[1]:G_MOD[1] + KT], ada_c[:, KT:2 * KT])
                mod_gain(1, pc[:, 0, G_MOD[1]:G_MOD[1] + KT], ada_x[:, KT:2 * KT])
                mod_gain(2, pc[:, 0, G_MOD[1] + KT:G_MOD[1] + 2 * KT], ada_x[:, 64:80])
                ve.wait_ge(s_cb, 16)
                for n in range(2):
                    tt(state_w[:, :, 2 * n:2 * n + 2],
                       lg[:, RET_H * n:RET_H * (n + 1)].unsqueeze(2).broadcast_to([P, RET_H, 2]),
                       pow_left[:, 2 * n:2 * n + 2].unsqueeze(1).broadcast_to([P, RET_H, 2]), ALU.mult)
                drain().then_inc(s_dec, 1)
                ve.wait_ge(s_stw, 1)
                ts(state_w[:, :, :], state_w[:, :, :], K_SCALE, None, ALU.mult).then_inc(s_stw, 1)
                norm(3, lambda f: modc[:, 0, f:f + 1], lambda f: ada_c[:, f:f + 1], act2, scr_b)
                drain()
                norm(4, lambda f: modc[:, 1, f:f + 1], lambda f: ada_x[:, f:f + 1], act, scr_b)
                drain()
                stage_loop(ve, "ret", split("ret"), ret, nothing)
            if wanted("four"):
                stage_loop(ve, "four", split("four"), four, squeezed(ret, COUNT["ret"] - 1))
                at_end(four, COUNT["four"] - 1, 8)
            if wanted("out2"):
                mix("out2")
                gate_diags(1, 32)
                add = out_of("out2")
                stage_loop(ve, "out2", split("out2"), add, nothing)
                add(2, COUNT["out2"] - 1)
            if wanted("conv"):
                drain()
                norm(5, lambda f: modc[:, 2, f:f + 1], lambda f: ada_x[:, 48 + f:49 + f], act, scr_b)
                drain()
                nc.vector.memset(conv_z, 0.0)
                drain()
                stage_loop(ve, "conv", split("conv"), conv, nothing)
                at_end(conv, COUNT["conv"] - 1, 16)
            if wanted("out3"):
                mix("out3")
                gate_diags(2, 80)
                add = out_of("out3")
                stage_loop(ve, "out3", split("out3"), add, nothing)
                add(2, COUNT["out3"] - 1)
                drain()
                scaled(6, 2)

        @block.tensor
        def _(te):
            mm = nc.tensor.matmul

            def features(out, slot, c, a, kt, start, stop, m=P):
                hi, lo = w_hi[:, slot, c:c + m], w_lo[:, slot, c:c + m]
                mm(out, hi, a[:, kt, 0:T], start=start, stop=False, skip_group_check=True)
                mm(out, hi, a[:, kt, T:2 * T], start=False, stop=False, skip_group_check=True)
                return mm(out, lo, a[:, kt, 0:T], start=False, stop=stop, skip_group_check=True)

            def tokens(out, slot, c, n, a, kt, t, start, stop):
                hi, lo = w_hi[:, slot, c:c + n], w_lo[:, slot, c:c + n]
                ah, al = a[:, kt, t * P:(t + 1) * P], a[:, kt, T + t * P:T + (t + 1) * P]
                mm(out, ah, hi, start=start, stop=False, skip_group_check=True)
                mm(out, ah, lo, start=False, stop=False, skip_group_check=True)
                return mm(out, al, hi, start=False, stop=stop, skip_group_check=True)

            def half(b, n):
                return PS[:, b, n * T:(n + 1) * T]

            def project(stage, i, p):
                slot = p % RING
                first, last = p == 0, p == PIECES[stage] - 1
                if stage in ("lru", "swa", "cq", "four"):
                    partial = stage == "cq" and isinstance(i, int) and i == 2
                    n = 320 if partial else 512
                    for q in range(4 if not partial else 3):
                        m = 64 if n - q * P < P else P
                        out = PS[0:m, A + q // 2, (q % 2) * T:(q % 2 + 1) * T]
                        for t in range(2):
                            r = features(out, slot, t * n + q * P, act, 2 * p + t,
                                         first and t == 0 and q % 2 == 0, last and t == 1, m)
                    return r
                if stage == "kv":
                    for t in range(2):
                        st, sp_ = first and t == 0, last and t == 1
                        for q in range(2):
                            features(half(A, q), slot, t * 384 + q * P, act, 2 * p + t, st and q == 0, sp_)
                        for k in range(TT):
                            r = tokens(PS[:, B, k * P:(k + 1) * P], slot, t * 384 + 256, P, act, 2 * p + t, k,
                                       st and k == 0, sp_)
                    return r
                if stage in MIX_KT:
                    for t in range(2):
                        a, kt = mix_dst(2 * p + t)
                        for k in range(TT):
                            r = tokens(bank(A + k), slot, t * 512, 512, a, kt, k, first and t == 0, last and t == 1)
                    return r
                if stage == "diff":
                    for b, c in ((A, 0), (B, 256), (C, 768)):
                        for q in range(2):
                            features(half(b, q), slot, c + q * P, act, p, first and q == 0, last)
                    for k in range(TT):
                        r = tokens(half(3, k), slot, 512, 256, act, p, k, first and k == 0, last)
                    return r
                if stage == "mla":
                    if p < 2:
                        for t in range(CQ_T):
                            st, sp_ = t == 0, t == CQ_T - 1
                            features(half(A, p), slot, t * 192, cn, t, st and p == 0, sp_)
                            r = features(PS[0:64, 4, p * T:(p + 1) * T], slot, t * 192 + P, cn, t,
                                         st and p == 0, sp_, 64)
                        return r
                    if p < 4:
                        h = p - 2
                        for t in range(CKV_T):
                            st, sp_ = t == 0, t == CKV_T - 1
                            features(half(B, h), slot, t * 256, cn, CQ_T + t, st and h == 0, sp_)
                            for k in range(TT):
                                r = tokens(PS[:, 3, k * T + h * P:k * T + (h + 1) * P], slot, t * 256 + P, P, cn,
                                           CQ_T + t, k, st and h == 0 and k == 0, sp_)
                        return r
                    for t in range(4):
                        for q in range(2):
                            r = features(half(C, q), slot, t * 256 + q * P, act, 4 * (p - 4) + t,
                                         p == 4 and t == 0 and q == 0, last and t == 3)
                    return r
                if stage == "ret":
                    for b, q, c in ((A, 0, 0), (A, 1, 128), (B, 0, 512), (B, 1, 640)):
                        features(half(b, q), slot, c, act, p, first and q == 0, last)
                    for k in range(TT):
                        tokens(half(C, k), slot, 256, 256, act, p, k, first and k == 0, last)
                        r = tokens(PS[:, 3 + k, 0:384], slot, 128, 384, act2, p, k, first, last)
                    return r
                for b in range(4):
                    for q in range(2):
                        r = features(half(b, q), slot, 256 * b + q * P, act, p, first and q == 0, last)
                return r

            def ada_sums(u, context, sums):
                te.wait_ge(s_au, 8 * u)
                for b in range(3):
                    last = mm(sums[:, b:b + 1], acc_x[:, b * P:(b + 1) * P], ones[:, 0:1], start=True, stop=True,
                              skip_group_check=True)
                    if context:
                        last = mm(sums[:, 3 + b:4 + b], acc_c[:, b * P:(b + 1) * P], ones[:, 0:1], start=True,
                                  stop=True, skip_group_check=True)
                last.then_inc(s_aps, 1)

            def run(stage):
                def unit(i, hook):
                    u0 = unit_of(stage, i)
                    for p in range(PIECES[stage]):
                        if stage in ADA0 and p % 8 == 0:
                            u = ADA0[stage] + i * (PIECES[stage] // 8) + p // 8
                            if not (isinstance(u, int) and u == 0):
                                ada_sums(u, ADA0[stage] < 16 or (isinstance(u, int) and u == 16),
                                         ada_cols(stage, p // 8))
                        if p == 0 and not (isinstance(u0, int) and u0 == 0):
                            te.wait_ge(s_free, u0)
                        if stage in MIX_KT and p % 2 == 0 and isinstance(i, int) and i == 0:
                            te.wait_ge(s_yl, MIX0[stage] + p // 2 + 1)
                        te.wait_ge(s_lo, pieces_before(stage, i) + p + 1)
                        project(stage, i, p).then_inc(s_used, 1)
                        hook(p)
                return unit

            def norm(k, src, scratch):
                te.wait_ge(s_n["diag"], DIAGS[k] + 1)
                diag = view(scratch[:, 2048:2304], TT, P)
                for b in range(8):
                    for f in (2 * b, 2 * b + 1):
                        for t in range(TT):
                            r = mm(PS[:, b, (f % 2) * T + t * P:(f % 2) * T + (t + 1) * P],
                                   src[:, t, f * P:(f + 1) * P], diag[:, t, :], start=True, stop=True,
                                   skip_group_check=True)
                    r.then_inc(s_n["psum"], 1)

            def normed(k):
                te.wait_ge(s_n["lo"], NORM_BANKS[k] + 8)

            def lru(p, i):
                s = S["lru"]
                if p == 2:
                    te.wait_ge(s["conv"], i + 1)
                    te.wait_ge(s_gw, 32 * i + 32)
                    if not isinstance(i, int) or i > 0:
                        te.wait_ge(s["y"], i + 1)
                    for b in range(2):
                        for w in range(2):
                            r = mm(half(4 + w, b), gate_w[:, b, w, :], halves(lru_xc)[:, b, :], start=True, stop=True,
                                   skip_group_check=True)
                    r.then_inc(s["gates"], 1)

            def kv(p, i=0):
                pass

            def sets_scores(pairs, first_bank):
                for n, terms in enumerate(pairs):
                    for lo, hi, q0, keys in ((0, 128, 0, P), (128, 384, P, T)):
                        for m, (q, k) in enumerate(terms):
                            r = mm(PS[:, first_bank + n, lo:hi], q[:, q0:q0 + P], k[:, 0:keys], start=m == 0,
                                   stop=m == len(terms) - 1, skip_group_check=True)
                return r

            def transposes(tiles, first_bank):
                for n, tile in enumerate(tiles):
                    for b in range(3):
                        r = nc.tensor.transpose(PS[:, first_bank + n, b * P:(b + 1) * P], tile[:, b * P:(b + 1) * P],
                                                ident[:, :])
                return r

            def values(out, v, pT):
                mm(out[:, 0:P], v(0), pT[:, 0:P], start=True, stop=True, skip_group_check=True)
                mm(out[:, P:T], v(0), pT[:, P:2 * P], start=True, stop=False, skip_group_check=True)
                return mm(out[:, P:T], v(1), pT[:, 2 * P:3 * P], start=False, stop=True, skip_group_check=True)

            def swa(p, i):
                s = S["swa"]
                if p == 1:
                    te.wait_ge(s_free, unit_of("swa", i) + 1)
                    if not isinstance(i, int) or i > 0:
                        te.wait_ge(s["y"], i + 1)
                    q = halves(swa_q)
                    pairs = [[(q[64 * (h % 2):64 * (h % 2) + 64, h // 2, :], swa_k[64 * (h % 2):64 * (h % 2) + 64, :])]
                             for h in range(4)]
                    sets_scores(pairs, 4).then_inc(s["scores"], 1)
                if p == 4:
                    te.wait_ge(s["prob"], i + 1)
                    v = view(swa_s, 4, 384)
                    transposes([v[:, h, :] for h in range(4)], 4).then_inc(s["probT"], 1)
                if p == 6:
                    te.wait_ge(s["probT_sb"], i + 1)
                    v = view(swa_t, 4, 384)
                    for h in range(4):
                        r = values(PS[64 * (h % 2):64 * (h % 2) + 64, 4, (h // 2) * T:(h // 2 + 1) * T],
                                   lambda t: swa_v[:, t, :], v[:, h, :])
                    r.then_inc(s["o"], 1)

            def cq_end(p, i=2):
                s = S["cq"]
                if p == 1:
                    te.wait_ge(s["squares"], 1)
                    mm(half(4, 0), rot64, k_raw[:, :], start=True, stop=True, skip_group_check=True)
                    for t in range(CQ_T + CKV_T):
                        q = t < CQ_T
                        r = mm(PS[:, 5 if q else 7, 0:T], ones[:, :], cq_sq[:, t, :], start=t in (0, CQ_T),
                               stop=t in (CQ_T - 1, CQ_T + CKV_T - 1), skip_group_check=True)
                    r.then_inc(s["sums"], 1)
                if p == 7:
                    te.wait_ge(s["gained"], 1)

            def diff(p, i):
                s = S["diff"]
                q, k = halves(at_q), halves(at_k)
                if p == 1:
                    te.wait_ge(s_free, unit_of("diff", i) + 1)
                    if not isinstance(i, int) or i > 0:
                        te.wait_ge(s["y"], i + 1)
                    if not isinstance(i, int) or i < COUNT["diff"] - 1:
                        te.wait_ge(s_acol, ADA0["diff"] + 2 * i + 2)
                    pairs = [[(q[64 * c:64 * c + 64, h, :], k[64 * c:64 * c + 64, h, :])]
                             for h in range(2) for c in range(2)]
                    sets_scores(pairs, 4).then_inc(s["scores"], 1)
                if p == 7:
                    te.wait_ge(s["prob"], i + 1)
                    v = dif_s.rearrange("p (h c n) -> p h c n", h=2, c=2)
                    transposes([v[:, h, 0, :] for h in range(2)], 4).then_inc(s["probT"], 1)
                if p == 9:
                    te.wait_ge(s["probT_sb"], i + 1)
                    v, t2 = halves(at_v), view(dif_t, 2, 384)
                    for h in range(2):
                        r = values(half(6, h), lambda t: v[:, t, h * P:(h + 1) * P], t2[:, h, :])
                    r.then_inc(s["o"], 1)
                if p == 11:
                    te.wait_ge(s["sq"], i + 1)
                    mm(bank(4), ones[:, :], dif_sq, start=True, stop=True, skip_group_check=True)\
                        .then_inc(s["sum"], 1)

            def mla(p, i):
                s = S["mla"]
                q, k, qr = halves(at_q), halves(at_k), halves(mla_qr)
                if p == 1:
                    te.wait_ge(s_free, unit_of("mla", i) + 1)
                    if not isinstance(i, int) or i > 0:
                        te.wait_ge(s["y"], i + 1)
                    mm(bank(5), rot64, mla_qr0, start=True, stop=True, skip_group_check=True)\
                        .then_inc(s["rot"], 1)
                if p == 2:
                    te.wait_ge(s["rope"], i + 1)
                    pairs = [[(q[:, h, :], k[:, h, :]), (qr[:, h, :], k_rot[:, :])] for h in range(2)]
                    sets_scores(pairs, 5).then_inc(s["scores"], 1)
                if p == 4:
                    te.wait_ge(s["prob"], i + 1)
                    v = view(mla_s, 2, 384)
                    transposes([v[:, h, :] for h in range(2)], 5).then_inc(s["probT"], 1)
                if p == 6:
                    te.wait_ge(s["probT_sb"], i + 1)
                    v, t2 = halves(at_v), view(mla_t, 2, 384)
                    for h in range(2):
                        r = values(half(5, h), lambda t: v[:, t, h * P:(h + 1) * P], t2[:, h, :])
                    r.then_inc(s["o"], 1)

            def ret(p, i):
                s = S["ret"]
                if p == 1:
                    te.wait_ge(s_free, unit_of("ret", i) + 1)
                    if not isinstance(i, int) or i > 0:
                        te.wait_ge(s["y"], i + 1)
                    mm(bank(5), rot128, ret_qk, start=True, stop=True, skip_group_check=True).then_inc(s["rot"], 1)
                    kc, vc = view(ret_kc, 4, P), halves(ret_vc)
                    for n in range(2):
                        for t in range(TT):
                            r = mm(half(6, n), kc[:, 2 * n + t, :], vc[:, t, :], start=t == 0, stop=t == TT - 1,
                                   skip_group_check=True)
                    r.then_inc(s["state"], 1)
                if p == 5:
                    te.wait_ge(s["rope"], i + 1)
                    for j in range(TT):
                        r = mm(half(7, j), ret_qk[:, T + j * P:T + (j + 1) * P], ret_qk[:, 0:T], start=True, stop=True,
                               skip_group_check=True)
                    r.then_inc(s["scores"], 1)
                if p == 7:
                    te.wait_ge(s["decayed"], i + 1)
                    te.wait_ge(s["scaled"], i + 1)
                    te.wait_ge(s["state_sb"], i + 1)
                    v, sd, xi = halves(ret_v), halves(ret_tmp), halves(ret_xi)
                    for e in range(2):
                        terms = [(v[:, j, e * P:(e + 1) * P], sd[:, j, :]) for j in range(TT)]
                        terms += [(ret_S[:, n * T + e * P:n * T + (e + 1) * P], xi[:, n, :]) for n in range(2)]
                        for m, (a, b) in enumerate(terms):
                            r = mm(half(5, e), a, b, start=m == 0, stop=m == 3, skip_group_check=True)
                    r.then_inc(s["o"], 1)
                if p == 10:
                    te.wait_ge(s["sq"], i + 1)
                    for e in range(2):
                        r = mm(PS[:, 6, 0:T], ones[:, :], halves(ret_sq)[:, e, :], start=e == 0, stop=e == 1,
                               skip_group_check=True)
                    r.then_inc(s["sum"], 1)

            def four(p, i):
                s = S["four"]
                if p == 1:
                    te.wait_ge(s_free, unit_of("four", i) + 1)
                    if isinstance(i, int) and i == 0:
                        te.wait_ge(S["ret"]["y"], COUNT["ret"] + 1)
                    else:
                        te.wait_ge(s["y"], i + 1)
                    u = halves(four_u)
                    for t in range(TT):
                        for c in range(2):
                            r = mm(bank(4 + t), u[:, c, t * P:(t + 1) * P], dft[:, c, :], start=c == 0, stop=c == 1,
                                   skip_group_check=True)
                    r.then_inc(s["cols"], 1)
                if p == 3:
                    te.wait_ge(s["cols_sb"], i + 1)
                    for e in range(2):
                        for t in range(TT):
                            mm(half(6, e), four_c[:, t, e * P:(e + 1) * P], dft[:, t, 0:T], start=t == 0, stop=False,
                               skip_group_check=True)
                            r = mm(half(6, e), four_c[:, t, T + e * P:T + (e + 1) * P], dft_ns[:, t, :], start=False,
                                   stop=t == 1, skip_group_check=True)
                    r.then_inc(s["rows"], 1)
                if p == 5:
                    te.wait_ge(s["rows_sb"], i + 1)
                    te.wait_ge(s_fno, 16 * i + 16)
                    for e in range(2):
                        for c in range(2):
                            r = mm(half(7, e), fno[:, c, e * P:(e + 1) * P], four_f[:, c, :], start=c == 0,
                                   stop=c == 1, skip_group_check=True)
                    r.then_inc(s["o"], 1)

            def gates_rows(n):
                for q in range(16):
                    te.wait_ge(s_gd, 16 * (n - 1) + q + 1)
                    r = mm(PS[:, 4 + q // 4, (q % 4) * P:(q % 4 + 1) * P], ones[:, :],
                           gate_diag[:, q, :], start=True, stop=True, skip_group_check=True)
                r.then_inc(s_gb, 1)

            def none(p, i):
                pass

            te.wait_ge(s_set, 1)
            te.wait_ge(s_par, 16 * N_PARAM)
            for t in range(3):
                r = nc.tensor.transpose(PS[:, 0, t * P:(t + 1) * P], prow[:, t, :], ident[:, :])
            r.then_inc(s_pps, 1)
            norm(0, x, scr_a)
            normed(0)
            stage_loop(te, "lru", run("lru"), lru, nothing)
            if wanted("kv"):
                run("kv")(0, lambda p: lru(p, COUNT["lru"] - 1))
                stage_loop(te, "swa", run("swa"), swa, kv)
                at_end(swa, COUNT["swa"] - 1, 8)
            if wanted("out0"):
                stage_loop(te, "out0", run("out0"), none, nothing)
            if wanted("cq"):
                norm(1, x, scr_a)
                normed(1)
                run("cq")(0, nothing)
                with te.Fori(1, 2) as i:
                    run("cq")(i, nothing)
                run("cq")(2, nothing)
            if wanted("diff"):
                stage_loop(te, "diff", run("diff"), diff, cq_end)
                at_end(diff, COUNT["diff"] - 1, 16)
                stage_loop(te, "mla", run("mla"), mla, nothing)
                at_end(mla, COUNT["mla"] - 1, 8)
            if wanted("out1"):
                stage_loop(te, "out1", run("out1"), none, nothing)
                ada_sums(ADA_SLABS, False, ada_cols("out1", 0))
            if wanted("ret"):
                norm(3, ctx_sb, scr_b)
                normed(3)
                norm(4, x, scr_b)
                normed(4)
                te.wait_ge(s_cb, 16)
                stage_loop(te, "ret", run("ret"), ret, nothing)
            if wanted("four"):
                stage_loop(te, "four", run("four"), four, squeezed(ret, COUNT["ret"] - 1))
                at_end(four, COUNT["four"] - 1, 8)
            if wanted("out2"):
                gates_rows(1)
                stage_loop(te, "out2", run("out2"), none, nothing)
            if wanted("conv"):
                norm(5, x, scr_b)
                normed(5)
                stage_loop(te, "conv", run("conv"), none, nothing)
            if wanted("out3"):
                gates_rows(2)
                stage_loop(te, "out3", run("out3"), none, nothing)


_INS = ["x", "norm_gains", "final_norm_gain", "l0_w_in", "l0_conv_w", "l0_conv_b", "l0_gate_x_w", "l0_gate_x_b",
        "l0_gate_a_w", "l0_gate_a_b", "l0_lru_lambda", "l0_sinks", "l0_w_out", "l1_w_in", "l1_q_norm", "l1_w_uq",
        "l1_kv_norm", "l1_w_ukv", "l1_lambda_q1", "l1_lambda_k1", "l1_lambda_q2", "l1_lambda_k2", "l1_subln",
        "l1_w_out", "c_2", "ctx_2", "c_ctx_2", "ada_w_2", "ada_b_2", "norm_w_2", "ev_w_in_2", "ret_decay_logit_2",
        "fno_w_2", "ev_w_out_2", "od_w_in_2", "conv_w_2", "od_w_out_2", "final_norm_w_2"]


def kernel(**inputs):
    import concourse.bacc as bacc
    from concourse.bass_utils import run_bass_kernel_spmd

    nc = bacc.Bacc("TRN2", target_bir_lowering=False, num_devices=1)
    arrays = {name: np.ascontiguousarray(inputs[name]) for name in _INS}
    arrays["const_a"], arrays["const_b"] = constants()
    drams = {name: nc.dram_tensor(f"in_{name}", a.shape, mybir.dt.from_np(a.dtype), kind="ExternalInput").ap()
             for name, a in arrays.items()}
    out = nc.dram_tensor("out_0", (1, T, D), F32, kind="ExternalOutput").ap()
    build(nc, drams, out)
    r = run_bass_kernel_spmd(nc, [{f"in_{name}": a for name, a in arrays.items()}], core_ids=[0])
    return r.results[0]["out_0"]
```

```python
from contextlib import ExitStack

import numpy as np

import concourse.bass as bass
from concourse import mybir

F32 = mybir.dt.float32
F32R = mybir.dt.float32r
ALU = mybir.AluOpType
ACT = mybir.ActivationFunctionType
AX = mybir.AxisListType.X
ds = bass.ds

P = 128
T = 256
TT = T // P
D = 2048
KT = D // P
EPS = 1e-6
N_PARAM = 22
RING = 4
SLOT = 1152

LRU_W = 1024
SWA_Q, SWA_KV, SWA_D = 1024, 128, 64
C_K = 2 * LRU_W + SWA_Q
C_V = C_K + SWA_KV
C_G = C_V + SWA_KV

Q_RANK, KV_RANK, ROPE_D = 768, 512, 64
CQ_T, CKV_T = Q_RANK // P, KV_RANK // P
C_MG = Q_RANK + KV_RANK + ROPE_D
C_DIFF = C_MG + 1024
MLA_SCALE = float(192) ** -0.5
LAMBDA_INIT = 0.8 - 0.6 * float(np.exp(-0.3))

RET_H = 8
K_SCALE = float(128) ** -0.5
NEG = -1.0e30

STAGES = [("lru", 4, 8), ("kv", 1, 8), ("swa", 4, 8), ("out0", 4, 8),
          ("cq", 3, 8), ("diff", 4, 16), ("mla", 4, 8), ("out1", 4, 8),
          ("ret", 8, 16), ("four", 8, 8), ("out2", 4, 16), ("conv", 16, 16), ("out3", 4, 16)]
DMAS = {"lru": 2, "kv": 5, "swa": 2, "out0": 1, "cq": 1, "diff": 1, "mla": 1, "out1": 1,
        "ret": 2, "four": 2, "out2": 1, "conv": 1, "out3": 1}
COUNT = {s: n for s, n, _ in STAGES}
PIECES = {s: p for s, _, p in STAGES}
BANKS = {"diff": (0, 1, 2, 3), "mla": (0, 4, 1, 3, 2), "ret": (0, 1, 2, 3, 4), "conv": (0, 1, 2, 3)}
BANKS = {s: BANKS.get(s, (0, 1)) for s, _, _ in STAGES}
FULLS = {s: 0 if s == "mla" else len(b) - 1 for s, b in BANKS.items()}
PIECE0, BANK0, FULL0, LAND0 = {}, {}, {}, {}
_g = _b = _f = _l = 0
for _s, _n, _p in STAGES:
    PIECE0[_s], BANK0[_s], FULL0[_s], LAND0[_s] = _g, _b, _f, _l
    _g, _b, _f = _g + _n * _p, _b + _n * len(BANKS[_s]), _f + _n * FULLS[_s]
    _l += _n * _p // RING * 16 * DMAS[_s]

ADA_RING = 4
ADA0 = {"kv": 0, "out0": 1, "cq": 5, "diff": 8, "mla": 16, "out1": 20, "ret": 24}
ADA_FIRST = {"kv": 0, "out0": 1, "cq": 5, "diff": 16, "mla": 8, "out1": 12, "ret": 0}
ADA_COLS = {s: 384 if s == "ret" else 256 for s in ADA0}
ADA_AT = (3, 4, 5, 6)

G_L0, G_L1, G_MOD, CONV_W, CONV_B, GX_B, GA_B, LAM = (
    (0, 0), (0, 16), (0, 32), (0, 64), (0, 96), (0, 104), (0, 112), (0, 120))
ADA_B, G_Q, G_KV, G_SUB, C_X = (1, 0), (1, 96), (1, 102), (1, 106), (1, 107)
CONV3_W, C_CTX = (2, 0), (2, 96)


def constants():
    f = np.float32
    ident = np.eye(P, dtype=f)
    i = np.arange(P)[:, None]
    j = np.arange(P)[None, :]
    causal = np.where(j <= i, 0.0, NEG).astype(f)
    before = np.where(j > i, 0.0, NEG).astype(f)
    zero = np.zeros((P, P), f)
    band = np.concatenate([causal, before, causal], 1)
    full = np.concatenate([causal, zero, causal], 1)
    pos = np.arange(T, dtype=f)

    def rotation(half):
        m = np.zeros((P, P), f)
        for d in range(half):
            m[half + d, d] = -1.0
            m[d, half + d] = 1.0
        return m

    def tables(ang):
        c, s = np.cos(ang).astype(f), np.sin(ang).astype(f)
        return np.concatenate([c, c], 0), np.concatenate([s, s], 0)

    freq = (f(10000.0) ** (-np.arange(32, dtype=f) / f(32))).astype(f)
    cos64, sin64 = tables((pos[None, :] * freq[:, None]).astype(f))
    pad = np.zeros((P - 64, T), f)
    first = np.concatenate([ident, band, full, np.concatenate([cos64, pad], 0),
                            np.concatenate([sin64, pad], 0), rotation(32)], 1)

    inv = (f(10000.0) ** (-np.arange(32, dtype=f) / f(32))).astype(f)
    row = (np.arange(T) // 64).astype(f)
    col = (np.arange(T) % 64).astype(f)
    cos128, sin128 = tables(np.concatenate([row[None] * inv[:, None], col[None] * inv[:, None]], 0).astype(f))
    k = np.arange(T)
    ang = 2 * np.pi * ((k[:, None] * k[None, :]) % T) / T
    dc, dsn = (np.cos(ang) / 16).astype(f), (np.sin(ang) / 16).astype(f)
    cs = np.concatenate([dc, dsn], 1).reshape(2, P, 2 * T).transpose(1, 0, 2).reshape(P, -1)
    ns = (-dsn).reshape(2, P, T).transpose(1, 0, 2).reshape(P, -1)
    rel = (k[None, :] - k[:, None]).astype(f).reshape(2, P, T).transpose(1, 0, 2).reshape(P, -1)
    up = np.broadcast_to(pos + 1, (P, T))
    down = np.broadcast_to(T - pos, (P, T))
    left = np.concatenate([(T - 1 - k).reshape(2, P).T, k.reshape(2, P).T], 1).astype(f)
    second = np.concatenate([cs, ns, np.maximum(rel, 0), np.maximum(-rel, 0), cos128, sin128,
                             rotation(64), up, down, left], 1)
    return np.ascontiguousarray(first, dtype=f), np.ascontiguousarray(second, dtype=f)


def build(nc, d, out, stop_after=None):
    ctx = ExitStack()
    with ctx:
        phase = [ctx]

        def sb(name, shape, dt=F32):
            return phase[0].enter_context(nc.sbuf_tensor(name, shape, dt))

        sems = {}

        def sem(name):
            sems[name] = ctx.enter_context(nc.semaphore(name))
            return sems[name]

        w_raw = sb("w_raw", [P, RING, SLOT])
        w_hi = sb("w_hi", [P, RING, SLOT], F32R)
        w_lo = sb("w_lo", [P, RING, SLOT], F32R)
        x = sb("x_res", [P, TT, D])
        act = sb("act_hl", [P, KT, 2 * T], F32R)
        y = sb("y_mix", [P, 32 * T])
        yt = y[:, :].rearrange("p (k n) -> p k n", n=T)
        pc = sb("param_cols", [P, 3, P])
        ident = sb("ident", [P, P])
        ones = sb("ones", [P, P])
        ada_x = sb("ada_x", [P, 96])
        ada_c = sb("ada_c", [P, 32])
        silu_c = sb("silu_c", [P, 2, KT])
        modc = sb("mod_cols", [P, 3, KT])
        lg = sb("log_gamma", [P, 2 * RET_H])
        state_w = sb("state_w", [P, RET_H, 4])
        sinks = sb("sinks", [P, 16])
        nlam = sb("neg_lambda", [P, 2])
        stat = sb("stat", [P, 4, 2])
        soft = sb("soft", [P, 5, 8])
        lru_c = sb("lru_c", [P, 4, 8])
        sub_g = sb("sub_gain", [P, 1])

        pa = ExitStack()
        phase[0] = pa
        const_a = sb("const_a", [P, 1408])
        ada_ring = sb("ada_ring", [P, ADA_RING, 2 * 256])
        acc_x = sb("acc_x", [P, 256])
        acc_c = sb("acc_c", [P, 256])
        cn = sb("c_norm", [P, CQ_T + CKV_T, 2 * T], F32R)
        k_raw = sb("k_rope_raw", [64, T])
        k_rot = sb("k_rope", [64, T])
        scr_a = sb("scr_a", [P, 4864])
        pa.close()
        pb = ExitStack()
        phase[0] = pb
        act2 = sb("act2_hl", [P, KT, 2 * T], F32R)
        const_b = sb("const_b", [P, 3716])
        fno = sb("fno", [P, 2, T])
        scr_b = sb("scr_b", [P, 4608])
        pb.close()
        phase[0] = ctx

        band = const_a[:, 0:384]
        causal = const_a[:, 384:768]
        cos64 = const_a[0:64, 768:1024]
        sin64 = const_a[0:64, 1024:1280]
        rot64 = const_a[0:64, 1280:1408]
        dft = const_b[:, 0:1024].rearrange("p (k n) -> p k n", k=2)
        dft_ns = const_b[:, 1024:1536].rearrange("p (k n) -> p k n", k=2)
        rel_up = const_b[:, 1536:2048]
        rel_dn = const_b[:, 2048:2560]
        cos128 = const_b[:, 2560:2816]
        sin128 = const_b[:, 2816:3072]
        rot128 = const_b[:, 3072:3200]
        pow_up = const_b[:, 3200:3456]
        pow_dn = const_b[:, 3456:3712]
        pow_left = const_b[:, 3712:3716]

        lam_rows = y[:, 24 * T:25 * T].rearrange("p (v n) -> p v n", v=4)
        kT4 = yt[:, 26:30, :]
        v4 = y[:, 30 * T:32 * T].rearrange("p (h t n) -> p h t n", h=4, t=TT)
        prow = y[:, 0:3 * P].rearrange("p (t n) -> p t n", t=3)
        zc = yt[:, 16:26, :]
        ctx_sb = y[:, 16 * T:32 * T].rearrange("p (t n) -> p t n", t=TT)
        ada_ring2 = y[:, 16 * T:28 * T].rearrange("p (r n) -> p r n", r=ADA_RING)
        acc_x2 = y[:, 28 * T:28 * T + 384]
        gain_bc = y[:, 8 * T:16 * T]
        junk = y[:, 0:8 * T]

        PS = ctx.enter_context(nc.psum_tensor("banks", [P, 8, 512], F32))

        def bank(n):
            return PS[:, n, :]

        def halves(ap):
            return ap.rearrange("p (k n) -> p k n", k=2)

        A, B, C, E0 = 0, 1, 2, 4

        s_par = sem("params_landed")
        s_x = sem("x_landed")
        s_w = [sem(f"weights_landed{k}") for k in range(RING)]
        s_hi = sem("piece_hi")
        s_lo = sem("piece_lo")
        s_used = sem("piece_used")
        s_full = sem("proj_banks_full")
        s_free = sem("proj_banks_free")
        s_aw = [sem(f"ada_landed{k}") for k in range(ADA_RING)]
        s_au = sem("ada_piece_used")
        s_aps = sem("ada_cols_in_psum")
        s_acol = sem("ada_cols_read")
        s_gw = sem("gate_w_landed")
        s_fno = sem("fno_landed")
        s_cb = sem("const_b_landed")
        s_ctx = sem("ctx_landed")
        s_gain = sem("gain_landed")
        s_out = sem("out_stored")
        s_set = sem("cleared")
        s_pps = sem("params_in_psum")
        s_pc = sem("params_ready")
        s_pe_ = sem("setup_exp")
        s_dec = sem("decay_logs")
        s_stw = sem("state_weights")
        s_n = {k: sem(f"norm_{k}") for k in ("sum", "mean", "root", "diag", "psum", "tile", "hi", "lo")}
        s_added = sem("residual_added")
        s_fin = sem("tokens_scaled")
        s_yh = sem("mix_hi")
        s_yl = sem("mix_lo")
        s_gb = sem("gate_rows_in_psum")
        s_gr = sem("gate_rows_ready")
        s_gd = sem("gate_diags_ready")
        S = {}
        for stage, names in {
            "lru": ("conv", "gates", "sig", "y"),
            "swa": ("scores", "max", "exp", "prob", "probT", "probT_sb", "o", "y"),
            "cq": ("squares", "sums", "mean", "root", "gained", "hi", "lo"),
            "diff": ("scores", "max", "exp", "prob", "probT", "probT_sb", "o", "sq", "sum", "mean", "root", "y"),
            "mla": ("rot", "rope", "scores", "max", "exp", "prob", "probT", "probT_sb", "o", "y"),
            "ret": ("arg", "tables", "rot", "rope", "state", "state_sb", "scaled", "scores", "decayed",
                    "o", "sq", "sum", "mean", "root", "y"),
            "four": ("cols", "cols_sb", "rows", "rows_sb", "o", "y"),
            "conv": ("y",),
        }.items():
            S[stage] = {k: sem(f"{stage}_{k}") for k in names}

        block = ctx.enter_context(nc.Block())
        order = [s for s, _, _ in STAGES]
        last = order if stop_after is None else order[:order.index(stop_after) + 1]

        def wanted(stage):
            return stage in last

        def stage_loop(eng, stage, unit, post, before):
            unit(0, before)
            if COUNT[stage] > 1:
                with eng.Fori(1, COUNT[stage]) as i:
                    unit(i, lambda p: post(p, i - 1))

        def nothing(p):
            pass

        def squeezed(post, i):
            def hook(p):
                post(2 * p, i)
                post(2 * p + 1, i)
            return hook

        def at_end(post, i, steps):
            for p in range(steps):
                post(p, i)

        NORM_BANKS = {0: 0, 1: 8, 3: 16, 4: 24, 5: 32}

        def ada_cols(stage, group):
            return PS[:, {"diff": (6, 7)[group % 2], "mla": 7, "ret": 7, "four": 7}.get(stage, 2), 500:506]

        def ada_buffers(stage):
            return (ada_ring2, acc_x2) if stage == "ret" else (ada_ring, acc_x)

        def ada_slab(stage, i, p):
            group = i * (PIECES[stage] // 8) + p // 8
            if not isinstance(group, int) or group > 0:
                return (stage, group - 1) if stage in ADA0 else None
            before = {"out0": "kv", "cq": "out0", "diff": "cq", "mla": "diff", "out1": "mla", "four": "ret"}.get(stage)
            return before and (before, COUNT[before] * (PIECES[before] // 8) - 1)

        def ada_context(stage):
            return stage not in ("diff", "ret")

        @block.sync
        def _(sp):
            def row_load(ap, tile, first, n):
                sp.dma_start(prow[first:first + n, tile, :], ap).then_inc(s_par, 16)

            sp.wait_ge(s_set, 1)
            sp.dma_start(ident[:, :], d["const_a"][:, 0:P]).then_inc(s_par, 16)
            row_load(d["norm_gains"].rearrange("l (a b) -> (l a) b", b=P), *G_L0, 32)
            row_load(d["norm_w_2"].rearrange("l (a b) -> (l a) b", b=P), *G_MOD, 32)
            row_load(d["l0_conv_w"].rearrange("l (a b) -> (l a) b", b=P), *CONV_W, 32)
            row_load(d["l0_conv_b"].rearrange("(a b) -> a b", b=P), *CONV_B, 8)
            row_load(d["l0_gate_x_b"], *GX_B, 8)
            row_load(d["l0_gate_a_b"], *GA_B, 8)
            row_load(d["l0_lru_lambda"].rearrange("(a b) -> a b", b=P), *LAM, 8)
            row_load(d["ada_b_2"].rearrange("l (a b) -> (l a) b", b=P), *ADA_B, 96)
            row_load(d["l1_q_norm"].rearrange("(a b) -> a b", b=P), *G_Q, 6)
            row_load(d["l1_kv_norm"].rearrange("(a b) -> a b", b=P), *G_KV, 4)
            row_load(d["l1_subln"].rearrange("(a b) -> a b", b=P), *G_SUB, 1)
            row_load(d["c_2"].rearrange("o (a b) -> (o a) b", b=P), *C_X, 16)
            row_load(d["conv_w_2"].rearrange("o l (a b) -> (o l a) b", b=P), *CONV3_W, 96)
            row_load(d["c_ctx_2"].rearrange("(a b) -> a b", b=P), *C_CTX, 16)
            sp.dma_start(x[:, :, :], d["x"].rearrange("o (t p) n -> p (o t) n", p=P)).then_inc(s_x, 16)
            sp.dma_start(const_a[:, :], d["const_a"][:, P:]).then_inc(s_par, 16)
            sp.dma_start(sinks[:, :], d["l0_sinks"].partition_broadcast(P)).then_inc(s_par, 16)
            sp.dma_start(lg[:, :], d["ret_decay_logit_2"].rearrange("o a h -> (o a h)").partition_broadcast(P))\
                .then_inc(s_par, 16)
            for n, name in enumerate(("l1_lambda_q1", "l1_lambda_k1", "l1_lambda_q2", "l1_lambda_k2")):
                sp.dma_start(lam_rows[:, n, :], d[name].partition_broadcast(P)).then_inc(s_par, 16)

            def two_blocks(t, src):
                return lambda r: r[:, 512 * t:512 * t + 512].rearrange("p (s n) -> p s n", s=2), src

            def sources(stage, i, p):
                if stage == "lru":
                    w = d["l0_w_in"][:, 0:2 * LRU_W].rearrange("(t p) (s n) -> p t s n", p=P, s=2)
                    return [two_blocks(t, w[:, 2 * p + t, :, ds(256 * i, 256)]) for t in range(2)]
                if stage == "kv":
                    w = d["l0_w_in"].rearrange("(t p) n -> p t n", p=P)
                    kk = w[:, 2 * p:2 * p + 2, C_K:C_K + SWA_KV].rearrange("p t (g n) -> p t g n", g=2)

                    def dup(t, n):
                        return lambda r: r[:, t * 384:t * 384 + 256].rearrange("p (g u n) -> p g u n", g=2, u=2)\
                            [:, :, n, :]
                    return [(dup(t, n), kk[:, t, :, :]) for t in range(2) for n in range(2)] + [
                        (lambda r: r[:, 0:768].rearrange("p (t c) -> p t c", t=2)[:, :, 256:384],
                         w[:, 2 * p:2 * p + 2, C_V:C_V + SWA_KV])]
                if stage == "swa":
                    w = d["l0_w_in"].rearrange("(t p) n -> p t n", p=P)

                    def part(n):
                        return lambda r: r[:, 0:1024].rearrange("p (t s n) -> p t s n", t=2, s=2)[:, :, n, :]
                    return [(part(0), w[:, 2 * p:2 * p + 2, ds(256 * i + 2 * LRU_W, 256)]),
                            (part(1), w[:, 2 * p:2 * p + 2, ds(256 * i + C_G, 256)])]
                if stage in ("out0", "out1", "out2", "out3"):
                    name = {"out0": "l0_w_out", "out1": "l1_w_out", "out2": "ev_w_out_2", "out3": "od_w_out_2"}[stage]
                    w = d[name]
                    if len(w.shape) == 3:
                        w = w.rearrange("o k n -> (o k) n")
                    w = w.rearrange("(t p) n -> p t n", p=P)
                    return [(lambda r: r[:, 0:1024].rearrange("p (t n) -> p t n", t=2),
                             w[:, 2 * p:2 * p + 2, ds(512 * i, 512)])]
                if stage == "cq":
                    w = d["l1_w_in"].rearrange("(t p) n -> p t n", p=P)
                    n = 320 if isinstance(i, int) and i == 2 else 512
                    return [(lambda r: r[:, 0:2 * n].rearrange("p (t n) -> p t n", t=2),
                             w[:, 2 * p:2 * p + 2, ds(512 * i, n)])]
                if stage == "diff":
                    w = d["l1_w_in"][:, C_DIFF:C_DIFF + 4096].rearrange("(t p) (s n) -> p t s n", p=P, s=4)
                    return [(lambda r: r[:, 0:1024].rearrange("p (s n) -> p s n", s=4), w[:, p, :, ds(256 * i, 256)])]
                if stage == "mla":
                    if p < 2:
                        w = d["l1_w_uq"].rearrange("(t p) n -> p t n", p=P)
                        return [(lambda r: r[:, 0:1152].rearrange("p (t n) -> p t n", t=CQ_T),
                                 w[:, :, ds(384 * i + 192 * p, 192)])]
                    if p < 4:
                        w = d["l1_w_ukv"].rearrange("(t p) n -> p t n", p=P)
                        return [(lambda r: r[:, 0:1024].rearrange("p (t n) -> p t n", t=CKV_T),
                                 w[:, :, ds(512 * i + 256 * (p - 2), 256)])]
                    w = d["l1_w_in"].rearrange("(t p) n -> p t n", p=P)
                    return [(lambda r: r[:, 0:1024].rearrange("p (t n) -> p t n", t=4),
                             w[:, 4 * (p - 4):4 * (p - 4) + 4, ds(256 * i + C_MG, 256)])]
                if stage == "ret":
                    w = d["ev_w_in_2"].rearrange("o (t p) n -> p (o t) n", p=P)
                    qk = w[:, :, 0:2048].rearrange("p t (s n) -> p t s n", s=2)
                    vg = w[:, :, 2048:6144].rearrange("p t (s n) -> p t s n", s=2)
                    return [(lambda r: r[:, 0:256].rearrange("p (s n) -> p s n", s=2), qk[:, p, :, ds(128 * i, 128)]),
                            (lambda r: r[:, 256:768].rearrange("p (s n) -> p s n", s=2), vg[:, p, :, ds(256 * i, 256)])]
                if stage == "four":
                    w = d["ev_w_in_2"].rearrange("o (t p) n -> p (o t) n", p=P)[:, :, 6144:10240]\
                        .rearrange("p t (s n) -> p t s n", s=2)
                    return [two_blocks(t, w[:, 2 * p + t, :, ds(256 * i, 256)]) for t in range(2)]
                w = d["od_w_in_2"].rearrange("o (t p) (s n) -> p (o t) s n", p=P, s=4)
                return [(lambda r: r[:, 0:1024].rearrange("p (s n) -> p s n", s=4), w[:, p, :, ds(256 * i, 256)])]

            def load_ada(stage, group, q):
                u, n = ADA0[stage] + group, ADA_COLS[stage]
                a = u * 8 + q
                if not isinstance(a, int) or a >= ADA_RING:
                    sp.wait_ge(s_au, a - (ADA_RING - 1))
                w = d["ada_w_2"].rearrange("l (t p) n -> p l t n", p=P)
                sp.dma_start(ada_buffers(stage)[0][:, q % ADA_RING, :].rearrange("p (t n) -> p t n", t=2),
                             w[:, 1 if stage == "ret" else 0, 2 * q:2 * q + 2, ds((ADA_FIRST[stage] + group) * n, n)])\
                    .then_inc(s_aw[q % ADA_RING], 16)

            def unit(stage):
                def load(i, hook):
                    for p in range(PIECES[stage]):
                        g = PIECE0[stage] + PIECES[stage] * i + p
                        if not isinstance(g, int) or g >= RING:
                            sp.wait_ge(s_lo, g - (RING - 1))
                        for dst, src in sources(stage, i, p):
                            sp.dma_start(dst(w_raw[:, p % RING, :]), src).then_inc(s_w[p % RING], 16)
                        if stage in ADA0 and p % 8 in ADA_AT:
                            group = i * (PIECES[stage] // 8) + p // 8
                            if stage == "ret" and isinstance(group, int) and group == 0 and p == ADA_AT[0]:
                                sp.wait_ge(s_n["psum"], NORM_BANKS[3] + 8)
                            q = 2 * (p % 8 - ADA_AT[0])
                            load_ada(stage, group, q)
                            load_ada(stage, group, q + 1)
                return load

            for stage in last:
                if stage == "cq":
                    with sp.Fori(0, 2) as i:
                        unit(stage)(i, nothing)
                    unit(stage)(2, nothing)
                elif stage == "ret":
                    sp.wait_ge(s_yl, 8)
                    sp.dma_start(gain_bc, d["final_norm_gain"].partition_broadcast(P)).then_inc(s_gain, 16)
                    sp.dma_start(ctx_sb, d["ctx_2"].rearrange("o (t p) n -> p (o t) n", p=P)).then_inc(s_ctx, 16)
                    sp.wait_ge(s_free, BANK0["ret"])
                    sp.dma_start(const_b[:, :], d["const_b"]).then_inc(s_cb, 16)
                    stage_loop(sp, stage, unit(stage), lambda p, i: None, nothing)
                else:
                    stage_loop(sp, stage, unit(stage), lambda p, i: None, nothing)
            if stop_after is None:
                sp.wait_ge(s_yl, 24)
                sp.dma_start(gain_bc, d["final_norm_w_2"].partition_broadcast(P)).then_inc(s_gain, 16)
                for t in range(TT):
                    sp.wait_ge(s_fin, TT + t + 1)
                    sp.dma_start(out[0, t * P:(t + 1) * P, :], x[:, t, :]).then_inc(s_out, 16)
                sp.wait_ge(s_out, 16 * TT)

        def view(ap, *dims):
            names = " ".join("abc"[:len(dims)])
            return ap.rearrange(f"p ({names}) -> p {names}", **dict(zip("abc", dims)))

        lru_x = view(scr_a[:, 0:518], 2, 259)
        lru_xc, lru_g, lru_gi, lru_gr, lru_r, lru_u, lru_sg = (
            scr_a[:, 518 + 512 * n:1030 + 512 * n] for n in range(7))
        gate_w = scr_a[:, 4102:4614].rearrange("p (b w n) -> p b w n", b=2, w=2)
        swa_q, swa_g = scr_a[:, 0:512], scr_a[:, 512:1024]
        swa_k, swa_v = scr_a[:, 1024:1280], view(scr_a[:, 1280:1408], TT, 64)
        swa_s, swa_t = scr_a[:, 1408:2944], scr_a[:, 2944:4480]
        at_q, at_k, at_v, at_g = (scr_a[:, 512 * n:512 * n + 512] for n in range(4))
        dif_s, dif_t = scr_a[:, 2048:3584], scr_a[:, 3584:4352]
        dif_o, dif_sq, dif_r = scr_a[:, 2048:2560], scr_a[:, 2560:3072], scr_a[:, 3072:3584]
        cq_r = view(scr_a[:, 3584:4096], 2, T)
        cq_sq = view(y[:, 0:(CQ_T + CKV_T) * T], CQ_T + CKV_T, T)
        mla_s, mla_t = scr_a[:, 2048:2816], scr_a[:, 2816:3584]
        mla_qr0, mla_qr = scr_a[0:64, 3584:4096], scr_a[0:64, 4096:4608]
        ret_qk, ret_tmp, ret_v, ret_g, ret_kc, ret_vc, ret_S, ret_D, ret_xi = (
            scr_b[:, 512 * n:512 * n + 512] for n in range(9))
        ret_sq, ret_r = ret_kc, ret_vc[:, 0:T]
        four_u, four_g = scr_b[:, 0:512], scr_b[:, 512:1024]
        four_c, four_f = view(scr_b[:, 1024:2048], 2, 512), view(scr_b[:, 2048:2560], 2, T)
        conv_x, conv_g, conv_b, conv_y = (scr_b[:, 512 * n:512 * n + 512] for n in range(4))
        conv_c = scr_b[:, 2576:3088]
        conv_z = scr_b[:, 2048:2576].rearrange("p (b r n) -> p b r n", b=2, r=4)
        gate_rows = scr_b[:, 2560:4608]
        gate_diag = view(scr_b[:, 0:2048], 16, P)
        out_t = view(scr_b[:, 0:1024], TT, 512)

        def pcol(which, n, width=1):
            tile, first = which
            return pc[:, tile, ds(first + n, width)]

        def landed(eng, stage, i, p):
            per = 16 * DMAS[stage]
            eng.wait_ge(s_w[p % RING], LAND0[stage] + per * (i * (PIECES[stage] // RING) + p // RING + 1))

        def width(stage, i):
            return {"kv": 768, "ret": 768, "mla": None}.get(stage, 1024)

        def cols(stage, i, p):
            if stage == "mla":
                return 1152 if p < 2 else 1024
            if stage == "cq" and isinstance(i, int) and i == 2:
                return 640
            return width(stage, i)

        def bank_count(stage, i, n):
            return BANK0[stage] + len(BANKS[stage]) * i + n

        def all_left(stage, i):
            return bank_count(stage, i, len(BANKS[stage]))

        def pieces_before(stage, i):
            return PIECE0[stage] + PIECES[stage] * i

        def full(eng, stage, i, n):
            if n == len(BANKS[stage]):
                eng.wait_ge(s_used, pieces_before(stage, i) + PIECES[stage])
            elif stage == "mla":
                eng.wait_ge(s_used, pieces_before(stage, i) + 4)
            else:
                eng.wait_ge(s_full, FULL0[stage] + FULLS[stage] * i + n)

        MIX_KT = {"out0": 16, "out1": 16, "out2": 32, "out3": 32}
        MIX0 = {"out0": 0, "out1": 4, "out2": 8, "out3": 16}
        SUMS = {0: 0, 1: 1, 2: 2, 3: 3, 4: 4, 5: 5, 6: 6}
        DIAGS = {0: 0, 1: 1, 3: 2, 4: 3, 5: 4}

        def mix_dst(kt):
            return (act if kt < KT else act2), kt % KT

        @block.gpsimd
        def _(pool):
            nc.gpsimd.memset(y[:, 0:3 * P], 0.0)
            nc.gpsimd.memset(ones[:, :], 1.0).then_inc(s_set, 1)
            gx = d["l0_gate_x_w"].rearrange("b k n -> k b n")
            ga = d["l0_gate_a_w"].rearrange("b k n -> k b n")

            def gates(i):
                pool.dma_start(gate_w[:, :, 0, :], gx[:, ds(2 * i, 2), :]).then_inc(s_gw, 16)
                pool.dma_start(gate_w[:, :, 1, :], ga[:, ds(2 * i, 2), :]).then_inc(s_gw, 16)

            gates(0)
            with pool.Fori(1, COUNT["lru"]) as i:
                pool.wait_ge(S["lru"]["gates"], i)
                gates(i)
            if wanted("four"):
                f = d["fno_w_2"].rearrange("o g (c p) n -> p (o g) c n", p=P)
                pool.wait_ge(s_cb, 16)
                pool.dma_start(fno[:, :, :], f[:, 0, :, :]).then_inc(s_fno, 16)
                with pool.Fori(1, COUNT["four"]) as i:
                    pool.wait_ge(S["four"]["o"], i)
                    pool.dma_start(fno[:, :, :], f[:, ds(i, 1), :, :].rearrange("p g c n -> p (g c) n"))\
                        .then_inc(s_fno, 16)

        @block.scalar
        def _(sc):
            def split(stage):
                def run(i, hook):
                    for p in range(PIECES[stage]):
                        g = pieces_before(stage, i) + p
                        n = cols(stage, i, p)
                        landed(sc, stage, i, p)
                        if not isinstance(g, int) or g >= RING:
                            sc.wait_ge(s_used, g - (RING - 1))
                        nc.scalar.activation(w_hi[:, p % RING, 0:n], w_raw[:, p % RING, 0:n], ACT.Copy)\
                            .then_inc(s_hi, 1)
                        hook(p)
                return run

            def copy(dst, src, **k):
                return nc.scalar.activation(dst, src, ACT.Copy, **k)

            def norm(k, src, ready, dst):
                ready()
                for t in range(TT):
                    nc.scalar.drain()
                    last = nc.scalar.activation(junk, src[:, t, :], ACT.Square, accum_out=stat[:, 0, t:t + 1])
                last.then_inc(s_n["sum"], 1)
                sc.wait_ge(s_n["mean"], SUMS[k] + 1)
                nc.scalar.activation(stat[:, 2, :], stat[:, 1, :], ACT.Sqrt).then_inc(s_n["root"], 1)
                if dst is None:
                    return
                scratch = scr_a if k < 2 else scr_b
                for b in range(8):
                    sc.wait_ge(s_n["tile"], NORM_BANKS[k] + b + 1)
                    copy(dst[:, 2 * b:2 * b + 2, 0:T], halves(scratch[:, (b % 4) * 512:(b % 4 + 1) * 512]))\
                        .then_inc(s_n["hi"], 1)

            def mix(stage):
                for q in range(MIX_KT[stage] // 4):
                    dst, kt = mix_dst(4 * q)
                    copy(dst[:, kt:kt + 4, 0:T], yt[:, 4 * q:4 * q + 4, :]).then_inc(s_yh, 1)

            def lru(p, i):
                s = S["lru"]
                if p == 2:
                    sc.wait_ge(s["y"], i + 1)
                    full(sc, "lru", i, 1)
                    copy(lru_x[:, :, 3:259], halves(bank(A))).then_inc(s_free, 1)
                    full(sc, "lru", i, 2)
                    copy(lru_g, bank(B))
                    nc.scalar.activation(lru_sg, bank(B), ACT.Sigmoid).then_inc(s_free, 1)
                if p == 5:
                    sc.wait_ge(s["gates"], i + 1)
                    for b in range(2):
                        nc.scalar.activation(halves(lru_gi)[:, b, :], halves(bank(4))[:, b, :], ACT.Sigmoid,
                                             bias=pcol(GX_B, 2 * i + b))
                        nc.scalar.activation(halves(lru_gr)[:, b, :], halves(bank(5))[:, b, :], ACT.Sigmoid,
                                             bias=pcol(GA_B, 2 * i + b))
                    nc.scalar.drain()
                    for b in range(2):
                        nc.scalar.activation(halves(lru_gr)[:, b, :], halves(lru_gr)[:, b, :], ACT.Tanh,
                                             scale=lru_c[:, 0, ds(2 * i + b, 1)])
                    nc.scalar.drain()
                    nc.scalar.activation(lru_u, lru_gr, ACT.Sqrt, scale=-1.0).then_inc(s["sig"], 1)

            def kv(p, i=0):
                if p == 2:
                    full(sc, "kv", 0, 2)
                    for h in range(4):
                        last = copy(kT4[:, h, :], halves(bank(A))[:, h // 2, :])
                    last.then_inc(s_free, 1)
                    for h in range(4):
                        last = copy(v4[:, h, :, :], bank(B)[:, 0:256].rearrange("p (t g n) -> p t g n", t=2, g=2)
                                    [:, :, h // 2, :])
                    last.then_inc(s_free, 1)

            def exps(s_tile, n, ready, done, sink):
                ready()
                if sink:
                    nc.scalar.activation(soft[:, 3, :], soft[:, 3, :], ACT.Exp)
                v = s_tile.rearrange("p (h c) -> p h c", c=384)
                for h in range(n):
                    for b, (lo, hi) in enumerate(((0, 128), (128, 384))):
                        last = nc.scalar.activation(v[:, h, lo:hi], v[:, h, lo:hi], ACT.Exp,
                                                    bias=soft[:, 1, 2 * h + b:2 * h + b + 1],
                                                    accum_out=soft[:, 2, 2 * h + b:2 * h + b + 1])
                last.then_inc(done, 1)

            def swa(p, i):
                s = S["swa"]
                if p == 2:
                    if isinstance(i, int) and i == 0:
                        sc.wait_ge(S["lru"]["y"], COUNT["lru"] + 1)
                    sc.wait_ge(s["y"], i + 1)
                    full(sc, "swa", i, 1)
                    copy(swa_q, bank(A), scale=SWA_D ** -0.5).then_inc(s_free, 1)
                    copy(swa_k, kT4[:, ds(i, 1), :].rearrange("p a n -> p (a n)"))
                    copy(swa_v, v4[:, ds(i, 1), :, :].rearrange("p a t n -> p (a t) n"))
                    full(sc, "swa", i, 2)
                    nc.scalar.activation(swa_g, bank(B), ACT.Silu).then_inc(s_free, 1)
                if p == 4:
                    exps(swa_s, 4, lambda: sc.wait_ge(s["max"], i + 1), s["exp"], True)
                if p == 6:
                    sc.wait_ge(s["probT"], i + 1)
                    copy(view(swa_t, 4, 384), PS[:, 4:8, 0:384]).then_inc(s["probT_sb"], 1)

            def cq_evac(i, last):
                full(sc, "cq", i, 1)
                if not last:
                    copy(zc[:, ds(4 * i, 2), :], halves(bank(A))).then_inc(s_free, 1)
                    full(sc, "cq", i, 2)
                    copy(zc[:, ds(4 * i + 2, 2), :], halves(bank(B))).then_inc(s_free, 1)
                else:
                    copy(zc[:, 8:10, :], halves(bank(A))).then_inc(s_free, 1)
                    full(sc, "cq", i, 2)
                    copy(k_raw[:, :], PS[0:64, B, 0:T]).then_inc(s_free, 1)

            def cq(p, i):
                if p == 2:
                    cq_evac(i, False)

            def cq_end(p, i=2):
                s = S["cq"]
                if p == 2:
                    cq_evac(2, True)
                    nc.scalar.drain()
                    nc.scalar.activation(cq_sq, zc, ACT.Square).then_inc(s["squares"], 1)
                if p == 6:
                    sc.wait_ge(s["mean"], 1)
                    nc.scalar.activation(cq_r, cq_r, ACT.Sqrt).then_inc(s["root"], 1)
                if p == 8:
                    sc.wait_ge(s["gained"], 1)
                    copy(cn[:, :, 0:T], zc).then_inc(s["hi"], 1)

            def diff(p, i):
                s = S["diff"]
                if p == 2:
                    if isinstance(i, int) and i == 0:
                        sc.wait_ge(S["cq"]["lo"], 1)
                    sc.wait_ge(s["y"], i + 1)
                    full(sc, "diff", i, 1)
                    copy(at_q, bank(A), scale=64 ** -0.5).then_inc(s_free, 1)
                    full(sc, "diff", i, 2)
                    copy(at_k, bank(B)).then_inc(s_free, 1)
                    full(sc, "diff", i, 3)
                    nc.scalar.activation(at_g, bank(C), ACT.Silu).then_inc(s_free, 1)
                    full(sc, "diff", i, 4)
                    copy(at_v, bank(3)).then_inc(s_free, 1)
                if p == 6:
                    exps(dif_s, 4, lambda: sc.wait_ge(s["max"], i + 1), s["exp"], False)
                if p == 10:
                    sc.wait_ge(s["probT"], i + 1)
                    copy(view(dif_t, 2, 384), PS[:, 4:6, 0:384]).then_inc(s["probT_sb"], 1)
                if p == 12:
                    sc.wait_ge(s["o"], i + 1)
                    copy(dif_o, bank(6))
                    nc.scalar.activation(dif_sq, bank(6), ACT.Square).then_inc(s["sq"], 1)
                if p == 14:
                    sc.wait_ge(s["mean"], i + 1)
                    nc.scalar.activation(dif_r, dif_r, ACT.Sqrt).then_inc(s["root"], 1)

            def mla(p, i):
                s = S["mla"]
                if p == 2:
                    if isinstance(i, int) and i == 0:
                        sc.wait_ge(S["diff"]["y"], COUNT["diff"] + 1)
                    sc.wait_ge(s["y"], i + 1)
                    full(sc, "mla", i, 4)
                    copy(at_q, bank(A), scale=MLA_SCALE).then_inc(s_free, 1)
                    copy(mla_qr0, PS[0:64, 4, :], scale=MLA_SCALE).then_inc(s_free, 1)
                    copy(at_k, bank(B)).then_inc(s_free, 1)
                    copy(at_v, bank(3)).then_inc(s_free, 1)
                    full(sc, "mla", i, 5)
                    nc.scalar.activation(at_g, bank(C), ACT.Silu).then_inc(s_free, 1)
                if p == 4:
                    exps(mla_s, 2, lambda: sc.wait_ge(s["max"], i + 1), s["exp"], False)
                if p == 6:
                    sc.wait_ge(s["probT"], i + 1)
                    copy(view(mla_t, 2, 384), PS[:, 5:7, 0:384]).then_inc(s["probT_sb"], 1)

            def ret(p, i):
                s = S["ret"]
                if p == 1:
                    sc.wait_ge(s["arg"], i + 1)
                    nc.scalar.activation(ret_D, ret_D, ACT.Exp)
                    nc.scalar.activation(ret_xi[:, 0:T], pow_up, ACT.Exp, scale=lg[:, ds(i, 1)])
                    nc.scalar.activation(ret_xi[:, T:], pow_dn, ACT.Exp, scale=lg[:, ds(i + RET_H, 1)])\
                        .then_inc(s["tables"], 1)
                if p == 2:
                    sc.wait_ge(s["y"], i + 1)
                    full(sc, "ret", i, 1)
                    copy(ret_qk, bank(A)).then_inc(s_free, 1)
                    full(sc, "ret", i, 2)
                    nc.scalar.activation(ret_g, bank(B), ACT.Silu).then_inc(s_free, 1)
                    full(sc, "ret", i, 3)
                    copy(ret_v, bank(C)).then_inc(s_free, 1)
                    for t in range(TT):
                        full(sc, "ret", i, 4 + t)
                        ctx_k, ctx_v = PS[:, 3 + t, 0:P], PS[:, 3 + t, P:384]
                        for n in range(2):
                            wcol = state_w[:, ds(i, 1), 2 * n + t:2 * n + t + 1].rearrange("p a b -> p (a b)")
                            copy(ret_kc[:, (2 * n + t) * P:(2 * n + t + 1) * P], ctx_k, scale=wcol)
                        copy(ret_vc[:, t * T:(t + 1) * T], ctx_v).then_inc(s_free, 1)
                if p == 4:
                    sc.wait_ge(s["state"], i + 1)
                    copy(ret_S, bank(6)).then_inc(s["state_sb"], 1)
                if p == 11:
                    sc.wait_ge(s["o"], i + 1)
                    nc.scalar.activation(ret_sq, bank(5), ACT.Square).then_inc(s["sq"], 1)
                if p == 13:
                    sc.wait_ge(s["mean"], i + 1)
                    nc.scalar.activation(ret_r, ret_r, ACT.Sqrt).then_inc(s["root"], 1)

            def four(p, i):
                s = S["four"]
                if p == 2:
                    if isinstance(i, int) and i == 0:
                        sc.wait_ge(S["ret"]["y"], COUNT["ret"] + 1)
                    sc.wait_ge(s["y"], i + 1)
                    full(sc, "four", i, 1)
                    copy(four_u, bank(A)).then_inc(s_free, 1)
                    full(sc, "four", i, 2)
                    nc.scalar.activation(four_g, bank(B), ACT.Silu).then_inc(s_free, 1)
                if p == 4:
                    sc.wait_ge(s["cols"], i + 1)
                    copy(four_c, PS[:, 4:6, :]).then_inc(s["cols_sb"], 1)
                if p == 6:
                    sc.wait_ge(s["rows"], i + 1)
                    copy(four_f, halves(bank(6))).then_inc(s["rows_sb"], 1)

            def conv(p, i):
                s = S["conv"]
                if p == 2:
                    sc.wait_ge(s["y"], i + 1)
                    full(sc, "conv", i, 1)
                    copy(conv_b, bank(A)).then_inc(s_free, 1)
                    full(sc, "conv", i, 2)
                    copy(conv_x, bank(B)).then_inc(s_free, 1)
                    full(sc, "conv", i, 3)
                    copy(conv_c, bank(C)).then_inc(s_free, 1)
                    full(sc, "conv", i, 4)
                    nc.scalar.activation(conv_g, bank(3), ACT.Silu).then_inc(s_free, 1)

            def gate_rows_copy(n):
                sc.wait_ge(s_gb, n)
                copy(view(gate_rows, 4, 512), PS[:, 4:8, :]).then_inc(s_gr, 1)

            def none(p, i):
                pass

            sc.wait_ge(s_pc, 1)
            nc.scalar.activation(silu_c[:, 0, :], pc[:, 1, C_X[1]:C_X[1] + KT], ACT.Silu)
            nc.scalar.activation(silu_c[:, 1, :], pc[:, 2, C_CTX[1]:C_CTX[1] + KT], ACT.Silu)
            nc.scalar.activation(lru_c[:, 1, :], pc[:, 0, LAM[1]:LAM[1] + 8], ACT.Abs)
            nc.scalar.drain()
            nc.scalar.activation(lru_c[:, 1, :], lru_c[:, 1, :], ACT.Exp, scale=-1.0)
            nc.scalar.activation(lg[:, :], lg[:, :], ACT.Exp)
            nc.scalar.activation(nlam[:, :], nlam[:, :], ACT.Exp).then_inc(s_pe_, 1)

            norm(0, x, lambda: sc.wait_ge(s_x, 16), act)
            stage_loop(sc, "lru", split("lru"), lru, nothing)
            if wanted("kv"):
                split("kv")(0, lambda p: lru(p, COUNT["lru"] - 1))
                stage_loop(sc, "swa", split("swa"), swa, kv)
                at_end(swa, COUNT["swa"] - 1, 8)
            if wanted("out0"):
                sc.wait_ge(S["swa"]["y"], COUNT["swa"] + 1)
                sc.wait_ge(s_used, pieces_before("out0", 0))
                mix("out0")
                stage_loop(sc, "out0", split("out0"), none, nothing)
            if wanted("cq"):
                norm(1, x, lambda: sc.wait_ge(s_free, BANK0["cq"]), act)
                split("cq")(0, nothing)
                with sc.Fori(1, 2) as i:
                    split("cq")(i, lambda p: cq(p, i - 1))
                split("cq")(2, lambda p: cq(p, 1))
            if wanted("diff"):
                stage_loop(sc, "diff", split("diff"), diff, cq_end)
                at_end(diff, COUNT["diff"] - 1, 16)
                stage_loop(sc, "mla", split("mla"), mla, nothing)
                at_end(mla, COUNT["mla"] - 1, 8)
            if wanted("out1"):
                sc.wait_ge(S["mla"]["y"], COUNT["mla"] + 1)
                sc.wait_ge(s_used, pieces_before("out1", 0))
                mix("out1")
                stage_loop(sc, "out1", split("out1"), none, nothing)
            if wanted("ret"):
                norm(2, x, lambda: sc.wait_ge(s_free, BANK0["ret"]), None)
                sc.wait_ge(s_dec, 1)
                nc.scalar.activation(state_w[:, :, :], state_w[:, :, :], ACT.Exp).then_inc(s_stw, 1)
                norm(3, ctx_sb, lambda: sc.wait_ge(s_ctx, 16), act2)
                norm(4, x, lambda: sc.wait_ge(s_fin, TT), act)
                sc.wait_ge(s_stw, 2)
                stage_loop(sc, "ret", split("ret"), ret, nothing)
            if wanted("four"):
                stage_loop(sc, "four", split("four"), four, squeezed(ret, COUNT["ret"] - 1))
                at_end(four, COUNT["four"] - 1, 8)
            if wanted("out2"):
                sc.wait_ge(S["four"]["y"], COUNT["four"] + 1)
                sc.wait_ge(s_used, pieces_before("out2", 0))
                mix("out2")
                gate_rows_copy(1)
                stage_loop(sc, "out2", split("out2"), none, nothing)
            if wanted("conv"):
                norm(5, x, lambda: sc.wait_ge(s_added, COUNT["out2"]), act)
                stage_loop(sc, "conv", split("conv"), conv, nothing)
                at_end(conv, COUNT["conv"] - 1, 16)
            if wanted("out3"):
                sc.wait_ge(S["conv"]["y"], COUNT["conv"] + 1)
                sc.wait_ge(s_used, pieces_before("out3", 0))
                mix("out3")
                gate_rows_copy(2)
                stage_loop(sc, "out3", split("out3"), none, nothing)
                norm(6, x, lambda: sc.wait_ge(s_added, COUNT["out2"] + COUNT["out3"]), None)

        @block.vector
        def _(ve):
            drain = nc.vector.drain
            tt = nc.vector.tensor_tensor
            stt = nc.vector.scalar_tensor_tensor
            ts = nc.vector.tensor_scalar

            def ada_column(slab, sums):
                stage, group = slab
                n = ADA_COLS[stage] // P
                first = n * (ADA_FIRST[stage] + group) + (48 if stage == "ret" else 0)
                ve.wait_ge(s_aps, ADA0[stage] + group + 1)
                r = tt(ada_x[:, ds(first, n)], sums[:, 0:n], pcol(ADA_B, first, n), ALU.add)
                if ada_context(stage):
                    r = tt(ada_c[:, ds(first, n)], sums[:, 3:3 + n], pcol(ADA_B, first, n), ALU.add)
                r.then_inc(s_acol, 1)

            def ada_piece(stage, group, q):
                ring, total = ada_buffers(stage)
                n = ADA_COLS[stage]
                ve.wait_ge(s_aw[q % ADA_RING], 16 * ((ADA0[stage] + group) * 2 + q // ADA_RING + 1))
                for t in range(2):
                    kt = 2 * q + t
                    w = ring[:, q % ADA_RING, t * n:(t + 1) * n]
                    for c, acc in ((1, acc_c), (0, total)) if ada_context(stage) else ((0, total),):
                        cond = silu_c[:, c, kt:kt + 1]
                        if kt == 0:
                            last = ts(acc[:, :], w, cond, None, ALU.mult)
                        else:
                            last = stt(acc[:, :], w, cond, acc[:, :], ALU.mult, ALU.add)
                    if t == 0:
                        drain()
                last.then_inc(s_au, 1)
                drain()

            def split(stage):
                def run(i, hook):
                    for p in range(PIECES[stage]):
                        g = pieces_before(stage, i) + p
                        n = cols(stage, i, p)
                        ve.wait_ge(s_hi, g + 1)
                        tt(w_lo[:, p % RING, 0:n], w_raw[:, p % RING, 0:n], w_hi[:, p % RING, 0:n].bitcast(F32),
                           ALU.subtract).then_inc(s_lo, 1)
                        hook(p)
                        if p % 8 == ADA_AT[0]:
                            slab = ada_slab(stage, i, p)
                            if slab:
                                ada_column(slab, ada_cols(stage, p // 8))
                        if stage in ADA0 and p % 8 in ADA_AT:
                            group = i * (PIECES[stage] // 8) + p // 8
                            q = 2 * (p % 8 - ADA_AT[0])
                            ada_piece(stage, group, q)
                            ada_piece(stage, group, q + 1)
                return run

            def root(k):
                ve.wait_ge(s_n["sum"], SUMS[k] + 1)
                ts(stat[:, 1, :], stat[:, 0, :], 1.0 / D, EPS, ALU.mult, ALU.add).then_inc(s_n["mean"], 1)
                ve.wait_ge(s_n["root"], SUMS[k] + 1)
                nc.vector.reciprocal(stat[:, 3, :], stat[:, 2, :])
                drain()
                tt(stat[:, 2, :], stat[:, 3, :], stat[:, 3, :], ALU.mult)
                drain()
                tt(stat[:, 2, :], stat[:, 2, :], stat[:, 1, :], ALU.mult)
                drain()
                ts(stat[:, 2, :], stat[:, 2, :], -0.5, 1.5, ALU.mult, ALU.add)
                drain()
                tt(stat[:, 3, :], stat[:, 3, :], stat[:, 2, :], ALU.mult)
                drain()

            def norm(k, gain, bias, dst, scratch):
                root(k)
                diag = view(scratch[:, 2048:2304], TT, P)
                for t in range(TT):
                    last = ts(diag[:, t, :], ident[:, :], stat[:, 3, t:t + 1], None, ALU.mult)
                last.then_inc(s_n["diag"], 1)
                def low(b):
                    tmp = scratch[:, (b % 4) * 512:(b % 4 + 1) * 512]
                    ve.wait_ge(s_n["hi"], NORM_BANKS[k] + b + 1)
                    tt(dst[:, 2 * b:2 * b + 2, T:2 * T], halves(tmp), dst[:, 2 * b:2 * b + 2, 0:T].bitcast(F32),
                       ALU.subtract).then_inc(s_n["lo"], 1)

                for b in range(8):
                    tmp = scratch[:, (b % 4) * 512:(b % 4 + 1) * 512]
                    ve.wait_ge(s_n["psum"], NORM_BANKS[k] + b + 1)
                    for h, f in enumerate((2 * b, 2 * b + 1)):
                        last = ts(tmp[:, h * T:(h + 1) * T], PS[:, b, h * T:(h + 1) * T], gain(f),
                                  0.0 if bias is None else bias(f), ALU.mult, ALU.add)
                    last.then_inc(s_n["tile"], 1)
                    if b > 0:
                        low(b - 1)
                drain()
                low(7)

            def scaled(k, n):
                root(k)
                ve.wait_ge(s_gain, 16 * n)
                for t in range(TT):
                    stt(x[:, t, :], x[:, t, :], stat[:, 3, t:t + 1], gain_bc, ALU.mult, ALU.mult)\
                        .then_inc(s_fin, 1)

            def mix(stage):
                for q in range(MIX_KT[stage] // 4):
                    dst, kt = mix_dst(4 * q)
                    ve.wait_ge(s_yh, MIX0[stage] + q + 1)
                    tt(dst[:, kt:kt + 4, T:2 * T], yt[:, 4 * q:4 * q + 4, :], dst[:, kt:kt + 4, 0:T].bitcast(F32),
                       ALU.subtract).then_inc(s_yl, 1)

            def lru(p, i):
                s = S["lru"]
                if p == 3:
                    ve.wait_ge(s_free, all_left("lru", i))
                    xc = halves(lru_xc)
                    for b in range(2):
                        ts(xc[:, b, :], lru_x[:, b, 3:259], pcol(CONV_W, 24 + 2 * i + b),
                           pcol(CONV_B, 2 * i + b), ALU.mult, ALU.add)
                    for tap in range(3):
                        drain()
                        for b in range(2):
                            last = stt(xc[:, b, :], lru_x[:, b, tap:tap + T], pcol(CONV_W, 8 * tap + 2 * i + b),
                                       xc[:, b, :], ALU.mult, ALU.add)
                    last.then_inc(s["conv"], 1)
                if p == 6:
                    ve.wait_ge(s["sig"], i + 1)
                    ts(lru_r, lru_gr, -1.0, 1.0, ALU.mult, ALU.add)
                    drain()
                    nc.vector.reciprocal(lru_r, lru_r)
                    drain()
                    stt(lru_u, lru_u, 2.0, lru_r, ALU.mult, ALU.mult)
                    stt(lru_gr, lru_gr, 1.0, lru_r, ALU.add, ALU.mult)
                    drain()
                    tt(lru_u, lru_u, lru_gi, ALU.mult)
                    drain()
                    tt(lru_u, lru_u, lru_xc, ALU.mult)
                    drain()
                    for b in range(2):
                        nc.vector.tensor_tensor_scan(halves(lru_gi)[:, b, :], halves(lru_gr)[:, b, :],
                                                     halves(lru_u)[:, b, :], 0.0, ALU.mult, ALU.add)
                    drain()
                    tt(lru_gi, lru_gi, lru_g, ALU.mult)
                    drain()
                    tt(yt[:, ds(2 * i, 2), :], halves(lru_gi), halves(lru_sg), ALU.mult).then_inc(s["y"], 1)

            def kv(p, i=0):
                pass

            def scores_max(s_tile, n, mask, first_bank, done, sink):
                v = s_tile.rearrange("p (h c) -> p h c", c=384)
                tt(v, PS[:, first_bank:first_bank + n, 0:384], mask.unsqueeze(1).broadcast_to([P, n, 384]), ALU.add)
                drain()
                mx = soft[:, 0, 0:2 * n].rearrange("p (h b) -> p h b", b=2)
                nc.vector.tensor_reduce(mx[:, :, 0], v[:, :, 0:128], AX, ALU.max)
                nc.vector.tensor_reduce(mx[:, :, 1], v[:, :, 128:384], AX, ALU.max)
                drain()
                if sink is not None:
                    tt(mx, mx, sink, ALU.max)
                    drain()
                    tt(soft[:, 3, :].rearrange("p (h b) -> p h b", b=2), sink, mx, ALU.subtract)
                ts(soft[:, 1, 0:2 * n], soft[:, 0, 0:2 * n], -1.0, None, ALU.mult).then_inc(done, 1)

            def normalise(s_tile, n, weight):
                v = s_tile.rearrange("p (h c) -> p h c", c=384)
                r = soft[:, 4, 0:2 * n].rearrange("p (h b) -> p h b", b=2)
                nc.vector.reciprocal(soft[:, 4, 0:2 * n], soft[:, 2, 0:2 * n])
                drain()
                if weight is not None:
                    weight(soft[:, 4, 0:2 * n])
                    drain()
                tt(v[:, :, 0:128], v[:, :, 0:128], r[:, :, 0:1].broadcast_to([P, n, 128]), ALU.mult)
                return tt(v[:, :, 128:384], v[:, :, 128:384], r[:, :, 1:2].broadcast_to([P, n, 256]), ALU.mult)

            def swa(p, i):
                s = S["swa"]
                if p == 4:
                    ve.wait_ge(s["scores"], i + 1)
                    sink = sinks[:, ds(4 * i, 4)].unsqueeze(2).broadcast_to([P, 4, 2])
                    scores_max(swa_s, 4, band, 4, s["max"], sink)
                if p == 5:
                    ve.wait_ge(s["exp"], i + 1)
                    tt(soft[:, 2, :], soft[:, 2, :], soft[:, 3, :], ALU.add)
                    drain()
                    normalise(swa_s, 4, None).then_inc(s["prob"], 1)
                if p == 7:
                    ve.wait_ge(s["o"], i + 1)
                    tt(yt[:, ds(2 * i + 8, 2), :], halves(bank(4)), halves(swa_g), ALU.mult).then_inc(s["y"], 1)

            def cq_end(p, i=2):
                s = S["cq"]
                if p == 6:
                    ve.wait_ge(s["sums"], 1)
                    ts(cq_r[:, 0, :], PS[:, 5, 0:T], 1.0 / Q_RANK, EPS, ALU.mult, ALU.add)
                    ts(cq_r[:, 1, :], PS[:, 7, 0:T], 1.0 / KV_RANK, EPS, ALU.mult, ALU.add).then_inc(s["mean"], 1)
                    rot = at_q[0:64, 0:T]
                    tt(rot, PS[0:64, 4, 0:T], sin64, ALU.mult)
                    tt(k_rot[:, :], k_raw[:, :], cos64, ALU.mult)
                    drain()
                    tt(k_rot[:, :], k_rot[:, :], rot, ALU.add)
                if p == 7:
                    ve.wait_ge(s["root"], 1)
                    nc.vector.reciprocal(cq_r, cq_r)
                    drain()
                    for t in range(CQ_T + CKV_T):
                        gain = pcol(G_Q, t) if t < CQ_T else pcol(G_KV, t - CQ_T)
                        last = stt(zc[:, t, :], zc[:, t, :], gain, cq_r[:, 0 if t < CQ_T else 1, :],
                                   ALU.mult, ALU.mult)
                    last.then_inc(s["gained"], 1)
                if p == 9:
                    ve.wait_ge(s["hi"], 1)
                    tt(cn[:, :, T:2 * T], zc, cn[:, :, 0:T].bitcast(F32), ALU.subtract).then_inc(s["lo"], 1)

            def diff(p, i):
                s = S["diff"]
                if p == 6:
                    ve.wait_ge(s["scores"], i + 1)
                    scores_max(dif_s, 4, causal, 4, s["max"], None)
                if p == 8:
                    ve.wait_ge(s["exp"], i + 1)

                    def second(r):
                        r = r.rearrange("p (h c b) -> p h c b", h=2, c=2)[:, :, 1, :]
                        ts(r, r, nlam[:, 0:1], None, ALU.mult)
                    normalise(dif_s, 4, second)
                    drain()
                    v = dif_s.rearrange("p (h c n) -> p h c n", h=2, c=2)
                    tt(v[:, :, 0, :], v[:, :, 0, :], v[:, :, 1, :], ALU.add).then_inc(s["prob"], 1)
                if p == 14:
                    ve.wait_ge(s["sum"], i + 1)
                    ts(dif_r, bank(4), 1.0 / 128, EPS, ALU.mult, ALU.add).then_inc(s["mean"], 1)
                if p == 15:
                    ve.wait_ge(s["root"], i + 1)
                    nc.vector.reciprocal(dif_r, dif_r)
                    drain()
                    stt(dif_o, dif_o, sub_g[:, :], dif_r, ALU.mult, ALU.mult)
                    drain()
                    tt(yt[:, ds(2 * i + 8, 2), :], halves(dif_o), halves(at_g), ALU.mult).then_inc(s["y"], 1)

            def mla(p, i):
                s = S["mla"]
                if p == 3:
                    ve.wait_ge(s["rot"], i + 1)
                    v0, v1 = halves(mla_qr0), halves(mla_qr)
                    tt(v1, halves(PS[0:64, 5, :]), sin64.unsqueeze(1).broadcast_to([64, 2, T]), ALU.mult)
                    tt(v0, v0, cos64.unsqueeze(1).broadcast_to([64, 2, T]), ALU.mult)
                    drain()
                    tt(v1, v1, v0, ALU.add).then_inc(s["rope"], 1)
                if p == 4:
                    ve.wait_ge(s["scores"], i + 1)
                    scores_max(mla_s, 2, causal, 5, s["max"], None)
                if p == 5:
                    ve.wait_ge(s["exp"], i + 1)
                    normalise(mla_s, 2, None).then_inc(s["prob"], 1)
                if p == 7:
                    ve.wait_ge(s["o"], i + 1)
                    tt(yt[:, ds(2 * i, 2), :], halves(bank(5)), halves(at_g), ALU.mult).then_inc(s["y"], 1)

            def ret(p, i):
                s = S["ret"]
                if p == 0:
                    ts(ret_D, rel_up, lg[:, ds(i, 1)], None, ALU.mult)
                    drain()
                    stt(ret_D, rel_dn, lg[:, ds(i + RET_H, 1)], ret_D, ALU.mult, ALU.add).then_inc(s["arg"], 1)
                if p == 4:
                    ve.wait_ge(s["rot"], i + 1)
                    tt(halves(ret_tmp), halves(bank(5)), sin128.unsqueeze(1).broadcast_to([P, 2, T]), ALU.mult)
                    tt(halves(ret_qk), halves(ret_qk), cos128.unsqueeze(1).broadcast_to([P, 2, T]), ALU.mult)
                    drain()
                    tt(ret_qk, ret_qk, ret_tmp, ALU.add).then_inc(s["rope"], 1)
                if p == 5:
                    drain()
                    ve.wait_ge(s["tables"], i + 1)
                    q2 = ret_qk[:, 0:T].unsqueeze(1).broadcast_to([P, 2, T])
                    tt(halves(ret_xi), halves(ret_xi), q2, ALU.mult).then_inc(s["scaled"], 1)
                if p == 8:
                    ve.wait_ge(s["scores"], i + 1)
                    stt(ret_tmp, bank(7), K_SCALE, ret_D, ALU.mult, ALU.mult).then_inc(s["decayed"], 1)
                if p == 13:
                    ve.wait_ge(s["sum"], i + 1)
                    ts(ret_r, PS[:, 6, 0:T], 1.0 / T, EPS, ALU.mult, ALU.add).then_inc(s["mean"], 1)
                if p == 14:
                    ve.wait_ge(s["root"], i + 1)
                    nc.vector.reciprocal(ret_r, ret_r)
                    drain()
                    r2 = ret_r.unsqueeze(1).broadcast_to([P, 2, T])
                    tt(halves(ret_v), halves(bank(5)), r2, ALU.mult)
                    drain()
                    tt(yt[:, ds(2 * i, 2), :], halves(ret_v), halves(ret_g), ALU.mult).then_inc(s["y"], 1)

            def four(p, i):
                s = S["four"]
                if p == 7:
                    ve.wait_ge(s["o"], i + 1)
                    tt(yt[:, ds(2 * i + 16, 2), :], halves(bank(7)), halves(four_g), ALU.mult).then_inc(s["y"], 1)

            def conv(p, i):
                s = S["conv"]
                if p == 3:
                    ve.wait_ge(s_free, all_left("conv", i))
                    rows = "p (b r n) -> p b r n"
                    z, v = conv_z, conv_y.rearrange(rows, b=2, r=4)
                    tt(z[:, :, :, 1:65], conv_c.rearrange(rows, b=2, r=4), conv_x.rearrange(rows, b=2, r=4),
                       ALU.mult)
                    drain()
                    for tap in (1, 0, 2):
                        for b in range(2):
                            w = pcol(CONV3_W, 32 * tap + 2 * i + b)
                            zs = z[:, b, :, tap:tap + 64]
                            if tap == 1:
                                ts(v[:, b, :, :], zs, w, None, ALU.mult)
                            else:
                                stt(v[:, b, :, :], zs, w, v[:, b, :, :], ALU.mult, ALU.add)
                        drain()
                    tt(conv_y, conv_y, conv_b, ALU.mult)
                    drain()
                    tt(yt[:, ds(2 * i, 2), :], halves(conv_y), halves(conv_g), ALU.mult).then_inc(s["y"], 1)

            def out_of(stage):
                def add(p, i):
                    if p != 2:
                        return
                    if stage in ("out0", "out1"):
                        for t in range(TT):
                            full(ve, stage, i, t + 1)
                            xs = x[:, t, ds(512 * i, 512)]
                            tt(xs, xs, bank(A + t), ALU.add).then_inc(s_free, 1)
                        return
                    for t in range(TT):
                        full(ve, stage, i, t + 1)
                        tt(out_t[:, t, :], bank(A + t), gate_rows[:, ds(512 * i, 512)], ALU.mult)\
                            .then_inc(s_free, 1)
                    drain()
                    xs = x[:, :, ds(512 * i, 512)]
                    tt(xs, xs, out_t, ALU.add).then_inc(s_added, 1)
                return add

            def gate_diags(n, first):
                for q in range(16):
                    ts(gate_diag[:, q, :], ident[:, :], ada_x[:, first + q:first + q + 1], None, ALU.mult)\
                        .then_inc(s_gd, 1)
                ve.wait_ge(s_gr, n)

            def mod_gain(k, norm_col, scale):
                stt(modc[:, k, :], scale, 1.0, norm_col, ALU.add, ALU.mult)
                drain()

            for stage in ("lru", "swa", "diff", "mla", "ret", "four", "conv"):
                ve.sem_inc(S[stage]["y"], 1)
            ve.wait_ge(s_pps, 1)
            nc.vector.tensor_copy(pc[:, :, :], PS[:, 0, 0:3 * P].rearrange("p (t n) -> p t n", t=3))
            for n in range(2):
                prod = lam_rows[:, 2 * n, :]
                tt(prod, prod, lam_rows[:, 2 * n + 1, :], ALU.mult)
            drain()
            for n in range(2):
                nc.vector.tensor_reduce(nlam[:, n:n + 1], lam_rows[:, 2 * n, :], AX, ALU.add)
            drain()
            ts(sub_g[:, :], pcol(G_SUB, 0), 1.0 - LAMBDA_INIT, None, ALU.mult).then_inc(s_pc, 1)
            ve.wait_ge(s_pe_, 1)
            ts(lg[:, :], lg[:, :], -1.0, None, ALU.mult)
            tt(nlam[:, 0:1], nlam[:, 1:2], nlam[:, 0:1], ALU.subtract)
            e, z, z2, acc = (lru_c[:, k, :] for k in (1, 2, 3, 0))
            ts(z, e, 2.0, None, ALU.add)
            drain()
            ts(nlam[:, 0:1], nlam[:, 0:1], -LAMBDA_INIT, None, ALU.add)
            nc.vector.reciprocal(z, z)
            drain()
            tt(z, z, e, ALU.mult)
            drain()
            tt(z2, z, z, ALU.mult)
            drain()
            ts(acc, z2, 1.0 / 17, None, ALU.mult)
            for k in range(15, 1, -2):
                drain()
                stt(acc, acc, 1.0 / k, z2, ALU.add, ALU.mult)
            drain()
            stt(acc, acc, 1.0, z, ALU.add, ALU.mult)
            ts(e, pc[:, 0, LAM[1]:LAM[1] + 8], -1.0, 0.0, ALU.mult, ALU.max)
            drain()
            ts(acc, acc, 2.0, None, ALU.mult)
            drain()
            tt(acc, acc, e, ALU.add)
            drain()
            ts(acc, acc, -4.0, None, ALU.mult).then_inc(s_pc, 1)

            def none(p, i):
                pass

            ve.wait_ge(s_x, 16)
            norm(0, lambda f: pcol(G_L0, f), None, act, scr_a)
            drain()
            nc.vector.memset(lru_x, 0.0)
            drain()
            stage_loop(ve, "lru", split("lru"), lru, nothing)
            if wanted("kv"):
                split("kv")(0, lambda p: lru(p, COUNT["lru"] - 1))
                stage_loop(ve, "swa", split("swa"), swa, kv)
                at_end(swa, COUNT["swa"] - 1, 8)
            if wanted("out0"):
                mix("out0")
                add = out_of("out0")
                stage_loop(ve, "out0", split("out0"), add, nothing)
                add(2, COUNT["out0"] - 1)
            if wanted("cq"):
                drain()
                norm(1, lambda f: pcol(G_L1, f), None, act, scr_a)
                split("cq")(0, nothing)
                with ve.Fori(1, 2) as i:
                    split("cq")(i, nothing)
                split("cq")(2, nothing)
            if wanted("diff"):
                stage_loop(ve, "diff", split("diff"), diff, cq_end)
                at_end(diff, COUNT["diff"] - 1, 16)
                stage_loop(ve, "mla", split("mla"), mla, nothing)
                at_end(mla, COUNT["mla"] - 1, 8)
            if wanted("out1"):
                mix("out1")
                add = out_of("out1")
                stage_loop(ve, "out1", split("out1"), add, nothing)
                add(2, COUNT["out1"] - 1)
                ada_column(("out1", COUNT["out1"] - 1), ada_cols("out1", 0))
            if wanted("ret"):
                drain()
                scaled(2, 1)
                mod_gain(0, pc[:, 0, G_MOD[1]:G_MOD[1] + KT], ada_c[:, KT:2 * KT])
                mod_gain(1, pc[:, 0, G_MOD[1]:G_MOD[1] + KT], ada_x[:, KT:2 * KT])
                ve.wait_ge(s_cb, 16)
                for n in range(2):
                    tt(state_w[:, :, 2 * n:2 * n + 2],
                       lg[:, RET_H * n:RET_H * (n + 1)].unsqueeze(2).broadcast_to([P, RET_H, 2]),
                       pow_left[:, 2 * n:2 * n + 2].unsqueeze(1).broadcast_to([P, RET_H, 2]), ALU.mult)
                drain().then_inc(s_dec, 1)
                ve.wait_ge(s_stw, 1)
                ts(state_w[:, :, :], state_w[:, :, :], K_SCALE, None, ALU.mult).then_inc(s_stw, 1)
                norm(3, lambda f: modc[:, 0, f:f + 1], lambda f: ada_c[:, f:f + 1], act2, scr_b)
                drain()
                norm(4, lambda f: modc[:, 1, f:f + 1], lambda f: ada_x[:, f:f + 1], act, scr_b)
                drain()
                stage_loop(ve, "ret", split("ret"), ret, nothing)
            if wanted("four"):
                stage_loop(ve, "four", split("four"), four, squeezed(ret, COUNT["ret"] - 1))
                at_end(four, COUNT["four"] - 1, 8)
            if wanted("out2"):
                mix("out2")
                gate_diags(1, 32)
                add = out_of("out2")
                stage_loop(ve, "out2", split("out2"), add, nothing)
                add(2, COUNT["out2"] - 1)
            if wanted("conv"):
                mod_gain(2, pc[:, 0, G_MOD[1] + KT:G_MOD[1] + 2 * KT], ada_x[:, 64:80])
                norm(5, lambda f: modc[:, 2, f:f + 1], lambda f: ada_x[:, 48 + f:49 + f], act, scr_b)
                drain()
                nc.vector.memset(conv_z, 0.0)
                drain()
                stage_loop(ve, "conv", split("conv"), conv, nothing)
                at_end(conv, COUNT["conv"] - 1, 16)
            if wanted("out3"):
                mix("out3")
                gate_diags(2, 80)
                add = out_of("out3")
                stage_loop(ve, "out3", split("out3"), add, nothing)
                add(2, COUNT["out3"] - 1)
                drain()
                scaled(6, 2)

        @block.tensor
        def _(te):
            mm = nc.tensor.matmul

            def features(out, slot, c, a, kt, start, stop, m=P):
                hi, lo = w_hi[:, slot, c:c + m], w_lo[:, slot, c:c + m]
                mm(out, hi, a[:, kt, 0:T], start=start, stop=False, skip_group_check=True)
                mm(out, hi, a[:, kt, T:2 * T], start=False, stop=False, skip_group_check=True)
                return mm(out, lo, a[:, kt, 0:T], start=False, stop=stop, skip_group_check=True)

            def tokens(out, slot, c, n, a, kt, t, start, stop):
                hi, lo = w_hi[:, slot, c:c + n], w_lo[:, slot, c:c + n]
                ah, al = a[:, kt, t * P:(t + 1) * P], a[:, kt, T + t * P:T + (t + 1) * P]
                mm(out, ah, hi, start=start, stop=False, skip_group_check=True)
                mm(out, ah, lo, start=False, stop=False, skip_group_check=True)
                return mm(out, al, hi, start=False, stop=stop, skip_group_check=True)

            def enter(stage, i, n):
                v = bank_count(stage, i - 1, n) if not isinstance(i, int) or i > 0 else BANK0[stage]
                if not isinstance(v, int) or v > 0:
                    te.wait_ge(s_free, v)

            def half(b, n):
                return PS[:, b, n * T:(n + 1) * T]

            def project(stage, i, p):
                slot = p % RING
                first, last = p == 0, p == PIECES[stage] - 1

                def filled(r):
                    return r.then_inc(s_full, 1)

                if stage in ("lru", "swa", "cq", "four"):
                    partial = stage == "cq" and isinstance(i, int) and i == 2
                    n = 320 if partial else 512
                    for q in range(4 if not partial else 3):
                        m = 64 if n - q * P < P else P
                        if first and q % 2 == 0:
                            enter(stage, i, 1 + q // 2)
                        out = PS[0:m, A + q // 2, (q % 2) * T:(q % 2 + 1) * T]
                        for t in range(2):
                            r = features(out, slot, t * n + q * P, act, 2 * p + t,
                                         first and t == 0 and q % 2 == 0, last and t == 1, m)
                        if last and q == 1:
                            filled(r)
                    return r
                if stage == "kv":
                    if first:
                        enter(stage, i, 2)
                    for t in range(2):
                        st, sp_ = first and t == 0, last and t == 1
                        for q in range(2):
                            r = features(half(A, q), slot, t * 384 + q * P, act, 2 * p + t, st and q == 0, sp_)
                        if sp_:
                            filled(r)
                        for k in range(TT):
                            r = tokens(PS[:, B, k * P:(k + 1) * P], slot, t * 384 + 256, P, act, 2 * p + t, k,
                                       st and k == 0, sp_)
                    return r
                if stage in MIX_KT:
                    for k in range(TT):
                        if first:
                            enter(stage, i, 1 + k)
                        for t in range(2):
                            a, kt = mix_dst(2 * p + t)
                            r = tokens(bank(A + k), slot, t * 512, 512, a, kt, k, first and t == 0, last and t == 1)
                        if last and k < TT - 1:
                            filled(r)
                    return r
                if stage == "diff":
                    for b, c in ((A, 0), (B, 256), (C, 768)):
                        if first:
                            enter(stage, i, 1 + b)
                        for q in range(2):
                            r = features(half(b, q), slot, c + q * P, act, p, first and q == 0, last)
                        if last:
                            filled(r)
                    if first:
                        enter(stage, i, 4)
                    for k in range(TT):
                        r = tokens(half(3, k), slot, 512, 256, act, p, k, first and k == 0, last)
                    return r
                if stage == "mla":
                    if p < 2:
                        if first:
                            enter(stage, i, 2)
                        for t in range(CQ_T):
                            st, sp_ = t == 0, t == CQ_T - 1
                            r = features(half(A, p), slot, t * 192, cn, t, st and p == 0, sp_)
                            r = features(PS[0:64, 4, p * T:(p + 1) * T], slot, t * 192 + P, cn, t,
                                         st and p == 0, sp_, 64)
                        return r
                    if p < 4:
                        h = p - 2
                        if h == 0:
                            enter(stage, i, 4)
                        for t in range(CKV_T):
                            st, sp_ = t == 0, t == CKV_T - 1
                            r = features(half(B, h), slot, t * 256, cn, CQ_T + t, st and h == 0, sp_)
                            for k in range(TT):
                                r = tokens(PS[:, 3, k * T + h * P:k * T + (h + 1) * P], slot, t * 256 + P, P, cn,
                                           CQ_T + t, k, st and h == 0 and k == 0, sp_)
                        return r
                    if p == 4:
                        enter(stage, i, 5)
                    for t in range(4):
                        for q in range(2):
                            r = features(half(C, q), slot, t * 256 + q * P, act, 4 * (p - 4) + t,
                                         p == 4 and t == 0 and q == 0, last and t == 3)
                    return r
                if stage == "ret":
                    for b, c in ((A, 0), (B, 512)):
                        if first:
                            enter(stage, i, 1 + b)
                        for q in range(2):
                            r = features(half(b, q), slot, c + q * P, act, p, first and q == 0, last)
                        if last:
                            filled(r)
                    if first:
                        enter(stage, i, 3)
                    for k in range(TT):
                        r = tokens(half(C, k), slot, 256, 256, act, p, k, first and k == 0, last)
                    if last:
                        filled(r)
                    for k in range(TT):
                        if first:
                            enter(stage, i, 4 + k)
                        r = tokens(PS[:, 3 + k, 0:384], slot, 128, 384, act2, p, k, first, last)
                        if last and k < TT - 1:
                            filled(r)
                    return r
                for b in range(4):
                    if first:
                        enter(stage, i, 1 + b)
                    for q in range(2):
                        r = features(half(b, q), slot, 256 * b + q * P, act, p, first and q == 0, last)
                    if last and b < 3:
                        filled(r)
                return r

            def ada_sums(slab, sums):
                stage, group = slab
                total = ada_buffers(stage)[1]
                te.wait_ge(s_au, 8 * (ADA0[stage] + group + 1))
                for b in range(ADA_COLS[stage] // P):
                    last = mm(sums[:, b:b + 1], total[:, b * P:(b + 1) * P], ones[:, 0:1], start=True, stop=True,
                              skip_group_check=True)
                    if ada_context(stage):
                        last = mm(sums[:, 3 + b:4 + b], acc_c[:, b * P:(b + 1) * P], ones[:, 0:1], start=True,
                                  stop=True, skip_group_check=True)
                last.then_inc(s_aps, 1)

            def run(stage):
                def unit(i, hook):
                    for p in range(PIECES[stage]):
                        slab = ada_slab(stage, i, p) if p % 8 == 0 else None
                        if slab:
                            ada_sums(slab, ada_cols(stage, p // 8))
                        if stage in MIX_KT and p % 2 == 0 and isinstance(i, int) and i == 0:
                            te.wait_ge(s_yl, MIX0[stage] + p // 2 + 1)
                        te.wait_ge(s_lo, pieces_before(stage, i) + p + 1)
                        project(stage, i, p).then_inc(s_used, 1)
                        hook(p)
                return unit

            def norm(k, src, scratch):
                te.wait_ge(s_n["diag"], DIAGS[k] + 1)
                diag = view(scratch[:, 2048:2304], TT, P)
                for b in range(8):
                    for f in (2 * b, 2 * b + 1):
                        for t in range(TT):
                            r = mm(PS[:, b, (f % 2) * T + t * P:(f % 2) * T + (t + 1) * P],
                                   src[:, t, f * P:(f + 1) * P], diag[:, t, :], start=True, stop=True,
                                   skip_group_check=True)
                    r.then_inc(s_n["psum"], 1)

            def normed(k):
                te.wait_ge(s_n["lo"], NORM_BANKS[k] + 8)

            def lru(p, i):
                s = S["lru"]
                if p == 2:
                    te.wait_ge(s["conv"], i + 1)
                    te.wait_ge(s_gw, 32 * i + 32)
                    te.wait_ge(s["y"], i + 1)
                    for b in range(2):
                        for w in range(2):
                            r = mm(half(4 + w, b), gate_w[:, b, w, :], halves(lru_xc)[:, b, :], start=True, stop=True,
                                   skip_group_check=True)
                    r.then_inc(s["gates"], 1)

            def kv(p, i=0):
                pass

            def sets_scores(pairs, first_bank):
                for n, terms in enumerate(pairs):
                    for lo, hi, q0, keys in ((0, 128, 0, P), (128, 384, P, T)):
                        for m, (q, k) in enumerate(terms):
                            r = mm(PS[:, first_bank + n, lo:hi], q[:, q0:q0 + P], k[:, 0:keys], start=m == 0,
                                   stop=m == len(terms) - 1, skip_group_check=True)
                return r

            def transposes(tiles, first_bank):
                for n, tile in enumerate(tiles):
                    for b in range(3):
                        r = nc.tensor.transpose(PS[:, first_bank + n, b * P:(b + 1) * P], tile[:, b * P:(b + 1) * P],
                                                ident[:, :])
                return r

            def values(out, v, pT):
                mm(out[:, 0:P], v(0), pT[:, 0:P], start=True, stop=True, skip_group_check=True)
                mm(out[:, P:T], v(0), pT[:, P:2 * P], start=True, stop=False, skip_group_check=True)
                return mm(out[:, P:T], v(1), pT[:, 2 * P:3 * P], start=False, stop=True, skip_group_check=True)

            def swa(p, i):
                s = S["swa"]
                if p == 1:
                    te.wait_ge(s_free, all_left("swa", i))
                    te.wait_ge(s["y"], i + 1)
                    q = halves(swa_q)
                    pairs = [[(q[64 * (h % 2):64 * (h % 2) + 64, h // 2, :], swa_k[64 * (h % 2):64 * (h % 2) + 64, :])]
                             for h in range(4)]
                    sets_scores(pairs, 4).then_inc(s["scores"], 1)
                if p == 4:
                    te.wait_ge(s["prob"], i + 1)
                    v = view(swa_s, 4, 384)
                    transposes([v[:, h, :] for h in range(4)], 4).then_inc(s["probT"], 1)
                if p == 6:
                    te.wait_ge(s["probT_sb"], i + 1)
                    v = view(swa_t, 4, 384)
                    for h in range(4):
                        r = values(PS[64 * (h % 2):64 * (h % 2) + 64, 4, (h // 2) * T:(h // 2 + 1) * T],
                                   lambda t: swa_v[:, t, :], v[:, h, :])
                    r.then_inc(s["o"], 1)

            def cq_end(p, i=2):
                s = S["cq"]
                if p == 1:
                    te.wait_ge(s["squares"], 1)
                    mm(half(4, 0), rot64, k_raw[:, :], start=True, stop=True, skip_group_check=True)
                    for t in range(CQ_T + CKV_T):
                        q = t < CQ_T
                        r = mm(PS[:, 5 if q else 7, 0:T], ones[:, :], cq_sq[:, t, :], start=t in (0, CQ_T),
                               stop=t in (CQ_T - 1, CQ_T + CKV_T - 1), skip_group_check=True)
                    r.then_inc(s["sums"], 1)
                if p == 7:
                    te.wait_ge(s["gained"], 1)

            def diff(p, i):
                s = S["diff"]
                q, k = halves(at_q), halves(at_k)
                if p == 1:
                    te.wait_ge(s_free, all_left("diff", i))
                    te.wait_ge(s["y"], i + 1)
                    if not isinstance(i, int) or i < COUNT["diff"] - 1:
                        te.wait_ge(s_acol, ADA0["diff"] + 2 * i + 2)
                    pairs = [[(q[64 * c:64 * c + 64, h, :], k[64 * c:64 * c + 64, h, :])]
                             for h in range(2) for c in range(2)]
                    sets_scores(pairs, 4).then_inc(s["scores"], 1)
                if p == 7:
                    te.wait_ge(s["prob"], i + 1)
                    v = dif_s.rearrange("p (h c n) -> p h c n", h=2, c=2)
                    transposes([v[:, h, 0, :] for h in range(2)], 4).then_inc(s["probT"], 1)
                if p == 9:
                    te.wait_ge(s["probT_sb"], i + 1)
                    v, t2 = halves(at_v), view(dif_t, 2, 384)
                    for h in range(2):
                        r = values(half(6, h), lambda t: v[:, t, h * P:(h + 1) * P], t2[:, h, :])
                    r.then_inc(s["o"], 1)
                if p == 11:
                    te.wait_ge(s["sq"], i + 1)
                    mm(bank(4), ones[:, :], dif_sq, start=True, stop=True, skip_group_check=True)\
                        .then_inc(s["sum"], 1)

            def mla(p, i):
                s = S["mla"]
                q, k, qr = halves(at_q), halves(at_k), halves(mla_qr)
                if p == 1:
                    te.wait_ge(s_free, all_left("mla", i))
                    te.wait_ge(s["y"], i + 1)
                    mm(bank(5), rot64, mla_qr0, start=True, stop=True, skip_group_check=True)\
                        .then_inc(s["rot"], 1)
                if p == 2:
                    te.wait_ge(s["rope"], i + 1)
                    pairs = [[(q[:, h, :], k[:, h, :]), (qr[:, h, :], k_rot[:, :])] for h in range(2)]
                    sets_scores(pairs, 5).then_inc(s["scores"], 1)
                if p == 4:
                    te.wait_ge(s["prob"], i + 1)
                    v = view(mla_s, 2, 384)
                    transposes([v[:, h, :] for h in range(2)], 5).then_inc(s["probT"], 1)
                if p == 6:
                    te.wait_ge(s["probT_sb"], i + 1)
                    v, t2 = halves(at_v), view(mla_t, 2, 384)
                    for h in range(2):
                        r = values(half(5, h), lambda t: v[:, t, h * P:(h + 1) * P], t2[:, h, :])
                    r.then_inc(s["o"], 1)

            def ret(p, i):
                s = S["ret"]
                if p == 1:
                    te.wait_ge(s_free, all_left("ret", i))
                    te.wait_ge(s["y"], i + 1)
                    mm(bank(5), rot128, ret_qk, start=True, stop=True, skip_group_check=True).then_inc(s["rot"], 1)
                    kc, vc = view(ret_kc, 4, P), halves(ret_vc)
                    for n in range(2):
                        for t in range(TT):
                            r = mm(half(6, n), kc[:, 2 * n + t, :], vc[:, t, :], start=t == 0, stop=t == TT - 1,
                                   skip_group_check=True)
                    r.then_inc(s["state"], 1)
                if p == 5:
                    te.wait_ge(s["rope"], i + 1)
                    te.wait_ge(s_acol, ADA0["ret"] + 2 * i + 2)
                    for j in range(TT):
                        r = mm(half(7, j), ret_qk[:, T + j * P:T + (j + 1) * P], ret_qk[:, 0:T], start=True, stop=True,
                               skip_group_check=True)
                    r.then_inc(s["scores"], 1)
                if p == 7:
                    te.wait_ge(s["decayed"], i + 1)
                    te.wait_ge(s["scaled"], i + 1)
                    te.wait_ge(s["state_sb"], i + 1)
                    v, sd, xi = halves(ret_v), halves(ret_tmp), halves(ret_xi)
                    for e in range(2):
                        terms = [(v[:, j, e * P:(e + 1) * P], sd[:, j, :]) for j in range(TT)]
                        terms += [(ret_S[:, n * T + e * P:n * T + (e + 1) * P], xi[:, n, :]) for n in range(2)]
                        for m, (a, b) in enumerate(terms):
                            r = mm(half(5, e), a, b, start=m == 0, stop=m == 3, skip_group_check=True)
                    r.then_inc(s["o"], 1)
                if p == 10:
                    te.wait_ge(s["sq"], i + 1)
                    for e in range(2):
                        r = mm(PS[:, 6, 0:T], ones[:, :], halves(ret_sq)[:, e, :], start=e == 0, stop=e == 1,
                               skip_group_check=True)
                    r.then_inc(s["sum"], 1)

            def four(p, i):
                s = S["four"]
                if p == 1:
                    te.wait_ge(s_free, all_left("four", i))
                    if isinstance(i, int) and i == 0:
                        te.wait_ge(S["ret"]["y"], COUNT["ret"] + 1)
                    te.wait_ge(s["y"], i + 1)
                    u = halves(four_u)
                    for t in range(TT):
                        for c in range(2):
                            r = mm(bank(4 + t), u[:, c, t * P:(t + 1) * P], dft[:, c, :], start=c == 0, stop=c == 1,
                                   skip_group_check=True)
                    r.then_inc(s["cols"], 1)
                if p == 3:
                    te.wait_ge(s["cols_sb"], i + 1)
                    for e in range(2):
                        for t in range(TT):
                            mm(half(6, e), four_c[:, t, e * P:(e + 1) * P], dft[:, t, 0:T], start=t == 0, stop=False,
                               skip_group_check=True)
                            r = mm(half(6, e), four_c[:, t, T + e * P:T + (e + 1) * P], dft_ns[:, t, :], start=False,
                                   stop=t == 1, skip_group_check=True)
                    r.then_inc(s["rows"], 1)
                if p == 5:
                    te.wait_ge(s["rows_sb"], i + 1)
                    te.wait_ge(s_fno, 16 * i + 16)
                    for e in range(2):
                        for c in range(2):
                            r = mm(half(7, e), fno[:, c, e * P:(e + 1) * P], four_f[:, c, :], start=c == 0,
                                   stop=c == 1, skip_group_check=True)
                    r.then_inc(s["o"], 1)

            def gates_rows(n):
                for q in range(16):
                    te.wait_ge(s_gd, 16 * (n - 1) + q + 1)
                    r = mm(PS[:, 4 + q // 4, (q % 4) * P:(q % 4 + 1) * P], ones[:, :],
                           gate_diag[:, q, :], start=True, stop=True, skip_group_check=True)
                r.then_inc(s_gb, 1)

            def none(p, i):
                pass

            te.wait_ge(s_set, 1)
            te.wait_ge(s_par, 16 * N_PARAM)
            for t in range(3):
                r = nc.tensor.transpose(PS[:, 0, t * P:(t + 1) * P], prow[:, t, :], ident[:, :])
            r.then_inc(s_pps, 1)
            norm(0, x, scr_a)
            normed(0)
            stage_loop(te, "lru", run("lru"), lru, nothing)
            if wanted("kv"):
                run("kv")(0, lambda p: lru(p, COUNT["lru"] - 1))
                stage_loop(te, "swa", run("swa"), swa, kv)
                at_end(swa, COUNT["swa"] - 1, 8)
            if wanted("out0"):
                stage_loop(te, "out0", run("out0"), none, nothing)
            if wanted("cq"):
                norm(1, x, scr_a)
                normed(1)
                run("cq")(0, nothing)
                with te.Fori(1, 2) as i:
                    run("cq")(i, nothing)
                run("cq")(2, nothing)
            if wanted("diff"):
                stage_loop(te, "diff", run("diff"), diff, cq_end)
                at_end(diff, COUNT["diff"] - 1, 16)
                stage_loop(te, "mla", run("mla"), mla, nothing)
                at_end(mla, COUNT["mla"] - 1, 8)
            if wanted("out1"):
                stage_loop(te, "out1", run("out1"), none, nothing)
                ada_sums(("out1", COUNT["out1"] - 1), ada_cols("out1", 0))
            if wanted("ret"):
                norm(3, ctx_sb, scr_b)
                normed(3)
                norm(4, x, scr_b)
                normed(4)
                te.wait_ge(s_cb, 16)
                stage_loop(te, "ret", run("ret"), ret, nothing)
            if wanted("four"):
                stage_loop(te, "four", run("four"), four, squeezed(ret, COUNT["ret"] - 1))
                at_end(four, COUNT["four"] - 1, 8)
            if wanted("out2"):
                gates_rows(1)
                stage_loop(te, "out2", run("out2"), none, nothing)
            if wanted("conv"):
                norm(5, x, scr_b)
                normed(5)
                stage_loop(te, "conv", run("conv"), none, nothing)
            if wanted("out3"):
                gates_rows(2)
                stage_loop(te, "out3", run("out3"), none, nothing)


_INS = ["x", "norm_gains", "final_norm_gain", "l0_w_in", "l0_conv_w", "l0_conv_b", "l0_gate_x_w", "l0_gate_x_b",
        "l0_gate_a_w", "l0_gate_a_b", "l0_lru_lambda", "l0_sinks", "l0_w_out", "l1_w_in", "l1_q_norm", "l1_w_uq",
        "l1_kv_norm", "l1_w_ukv", "l1_lambda_q1", "l1_lambda_k1", "l1_lambda_q2", "l1_lambda_k2", "l1_subln",
        "l1_w_out", "c_2", "ctx_2", "c_ctx_2", "ada_w_2", "ada_b_2", "norm_w_2", "ev_w_in_2", "ret_decay_logit_2",
        "fno_w_2", "ev_w_out_2", "od_w_in_2", "conv_w_2", "od_w_out_2", "final_norm_w_2"]


def kernel(**inputs):
    import concourse.bacc as bacc
    from concourse.bass_utils import run_bass_kernel_spmd

    nc = bacc.Bacc("TRN2", target_bir_lowering=False, num_devices=1)
    arrays = {name: np.ascontiguousarray(inputs[name]) for name in _INS}
    arrays["const_a"], arrays["const_b"] = constants()
    drams = {name: nc.dram_tensor(f"in_{name}", a.shape, mybir.dt.from_np(a.dtype), kind="ExternalInput").ap()
             for name, a in arrays.items()}
    out = nc.dram_tensor("out_0", (1, T, D), F32, kind="ExternalOutput").ap()
    build(nc, drams, out)
    r = run_bass_kernel_spmd(nc, [{f"in_{name}": a for name, a in arrays.items()}], core_ids=[0])
    return r.results[0]["out_0"]
```

```python
from contextlib import ExitStack

import numpy as np

import concourse.bass as bass
from concourse import mybir

F32 = mybir.dt.float32
F32R = mybir.dt.float32r
ALU = mybir.AluOpType
ACT = mybir.ActivationFunctionType
AX = mybir.AxisListType.X
ds = bass.ds

P = 128
T = 256
TT = T // P
D = 2048
KT = D // P
EPS = 1e-6
N_PARAM, N_MISC = 15, 7
RING = 4
SLOT = 1152

LRU_W = 1024
SWA_Q, SWA_KV, SWA_D = 1024, 128, 64
C_K = 2 * LRU_W + SWA_Q
C_V = C_K + SWA_KV
C_G = C_V + SWA_KV

Q_RANK, KV_RANK, ROPE_D = 768, 512, 64
CQ_T, CKV_T = Q_RANK // P, KV_RANK // P
C_MG = Q_RANK + KV_RANK + ROPE_D
C_DIFF = C_MG + 1024
MLA_SCALE = float(192) ** -0.5
LAMBDA_INIT = 0.8 - 0.6 * float(np.exp(-0.3))

RET_H = 8
K_SCALE = float(128) ** -0.5
NEG = -1.0e30

STAGES = [("lru", 4, 8), ("kv", 1, 8), ("swa", 4, 8), ("out0", 4, 8),
          ("cq", 3, 8), ("diff", 4, 16), ("mla", 4, 8), ("out1", 4, 8),
          ("ret", 8, 16), ("four", 8, 8), ("out2", 4, 16), ("conv", 16, 16), ("out3", 4, 16)]
DMAS = {"lru": 2, "kv": 5, "swa": 2, "out0": 1, "cq": 1, "diff": 1, "mla": 1, "out1": 1,
        "ret": 2, "four": 2, "out2": 1, "conv": 1, "out3": 1}
COUNT = {s: n for s, n, _ in STAGES}
PIECES = {s: p for s, _, p in STAGES}
BANKS = {"diff": (0, 1, 2, 3), "mla": (2, 4, 0, 1, 3), "ret": (0, 2, 3, 4, 1), "conv": (0, 1, 2, 3)}
BANKS = {s: BANKS.get(s, (0, 1)) for s, _, _ in STAGES}
FULLS = {s: 0 if s == "mla" else len(b) - 1 for s, b in BANKS.items()}
PIECE0, BANK0, FULL0, LAND0 = {}, {}, {}, {}
_g = _b = _f = _l = 0
for _s, _n, _p in STAGES:
    PIECE0[_s], BANK0[_s], FULL0[_s], LAND0[_s] = _g, _b, _f, _l
    _g, _b, _f = _g + _n * _p, _b + _n * len(BANKS[_s]), _f + _n * FULLS[_s]
    _l += _n * _p // RING * 16 * DMAS[_s]

ADA_RING = 4
ADA0 = {"swa": 0, "out0": 1, "cq": 5, "diff": 8, "mla": 16, "out1": 20, "ret": 24}
ADA_FIRST = {"swa": 0, "out0": 1, "cq": 5, "diff": 16, "mla": 8, "out1": 12, "ret": 0}
ADA_COLS = {s: 384 if s == "ret" else 256 for s in ADA0}
ADA_COL = 2
ADA_STEPS = {s: {2: (0,), 3: (1, 2), 4: (3,), 5: (4, 5), 6: (6,), 7: (7,)} for s in ADA0}
ADA_STEPS["diff"] = {2: (0, 1), 3: (2, 3), 4: (4, 5), 5: (6, 7)}
ADA_STEPS["mla"] = {2: (0, 1), 4: (2,), 5: (3, 4), 6: (5, 6), 7: (7,)}

G_L0, G_L1, G_MOD, CONV_W, CONV_B, GX_B, GA_B, LAM = (
    (0, 0), (0, 16), (0, 32), (0, 64), (0, 96), (0, 104), (0, 112), (0, 120))
ADA_B, G_Q, G_KV, G_SUB, C_X = (1, 0), (1, 96), (1, 102), (1, 106), (1, 107)
CONV3_W, C_CTX = (2, 0), (2, 96)


def constants():
    f = np.float32
    ident = np.eye(P, dtype=f)
    i = np.arange(P)[:, None]
    j = np.arange(P)[None, :]
    causal = np.where(j <= i, 0.0, NEG).astype(f)
    before = np.where(j > i, 0.0, NEG).astype(f)
    zero = np.zeros((P, P), f)
    band = np.concatenate([causal, before, causal], 1)
    full = np.concatenate([causal, zero, causal], 1)
    pos = np.arange(T, dtype=f)

    def rotation(half):
        m = np.zeros((P, P), f)
        for d in range(half):
            m[half + d, d] = -1.0
            m[d, half + d] = 1.0
        return m

    def tables(ang):
        c, s = np.cos(ang).astype(f), np.sin(ang).astype(f)
        return np.concatenate([c, c], 0), np.concatenate([s, s], 0)

    freq = (f(10000.0) ** (-np.arange(32, dtype=f) / f(32))).astype(f)
    cos64, sin64 = tables((pos[None, :] * freq[:, None]).astype(f))
    pad = np.zeros((P - 64, T), f)
    first = np.concatenate([ident, band, full, np.concatenate([cos64, pad], 0),
                            np.concatenate([sin64, pad], 0), rotation(32)], 1)

    inv = (f(10000.0) ** (-np.arange(32, dtype=f) / f(32))).astype(f)
    row = (np.arange(T) // 64).astype(f)
    col = (np.arange(T) % 64).astype(f)
    cos128, sin128 = tables(np.concatenate([row[None] * inv[:, None], col[None] * inv[:, None]], 0).astype(f))
    k = np.arange(T)
    ang = 2 * np.pi * ((k[:, None] * k[None, :]) % T) / T
    dc, dsn = (np.cos(ang) / 16).astype(f), (np.sin(ang) / 16).astype(f)
    cs = np.concatenate([dc, dsn], 1).reshape(2, P, 2 * T).transpose(1, 0, 2).reshape(P, -1)
    ns = (-dsn).reshape(2, P, T).transpose(1, 0, 2).reshape(P, -1)
    rel = (k[None, :] - k[:, None]).astype(f).reshape(2, P, T).transpose(1, 0, 2).reshape(P, -1)
    up = np.broadcast_to(pos + 1, (P, T))
    down = np.broadcast_to(T - pos, (P, T))
    left = np.concatenate([(T - 1 - k).reshape(2, P).T, k.reshape(2, P).T], 1).astype(f)
    second = np.concatenate([cs, ns, np.maximum(rel, 0), np.maximum(-rel, 0), cos128, sin128,
                             rotation(64), up, down, left], 1)
    return np.ascontiguousarray(first, dtype=f), np.ascontiguousarray(second, dtype=f)


def build(nc, d, out, stop_after=None):
    ctx = ExitStack()
    with ctx:
        phase = [ctx]

        def sb(name, shape, dt=F32):
            return phase[0].enter_context(nc.sbuf_tensor(name, shape, dt))

        sems = {}

        def sem(name):
            sems[name] = ctx.enter_context(nc.semaphore(name))
            return sems[name]

        w_raw = sb("w_raw", [P, RING, SLOT])
        w_hi = sb("w_hi", [P, RING, SLOT], F32R)
        w_lo = sb("w_lo", [P, RING, SLOT], F32R)
        x = sb("x_res", [P, TT, D])
        act = sb("act_hl", [P, KT, 2 * T], F32R)
        y = sb("y_mix", [P, 32 * T])
        yt = y[:, :].rearrange("p (k n) -> p k n", n=T)
        pc = sb("param_cols", [P, 3, P])
        ident = sb("ident", [P, P])
        ones = sb("ones", [P, P])
        ada_x = sb("ada_x", [P, 96])
        ada_c = sb("ada_c", [P, 32])
        silu_c = sb("silu_c", [P, 2, KT])
        modc = sb("mod_cols", [P, 3, KT])
        lg = sb("log_gamma", [P, 2 * RET_H])
        state_w = sb("state_w", [P, RET_H, 4])
        sinks = sb("sinks", [P, 16])
        nlam = sb("neg_lambda", [P, 2])
        stat = sb("stat", [P, 4, 2])
        parts = sb("square_parts", [P, TT, 4])
        soft = sb("soft", [P, 5, 8])
        lru_c = sb("lru_c", [P, 4, 8])
        sub_g = sb("sub_gain", [P, 1])

        pa = ExitStack()
        phase[0] = pa
        const_a = sb("const_a", [P, 1408])
        ada_ring = sb("ada_ring", [P, ADA_RING, 2 * 256])
        acc_x = sb("acc_x", [P, 2, 256])
        acc_c = sb("acc_c", [P, 2, 256])
        cn = sb("c_norm", [P, CQ_T + CKV_T, 2 * T], F32R)
        k_raw = sb("k_rope_raw", [64, T])
        k_rot = sb("k_rope", [64, T])
        scr_a = sb("scr_a", [P, 4864])
        pa.close()
        pb = ExitStack()
        phase[0] = pb
        act2 = sb("act2_hl", [P, KT, 2 * T], F32R)
        const_b = sb("const_b", [P, 3716])
        fno = sb("fno", [P, 2, T])
        scr_b = sb("scr_b", [P, 4608])
        pb.close()
        phase[0] = ctx

        band = const_a[:, 0:384]
        causal = const_a[:, 384:768]
        cos64 = const_a[0:64, 768:1024]
        sin64 = const_a[0:64, 1024:1280]
        rot64 = const_a[0:64, 1280:1408]
        dft = const_b[:, 0:1024].rearrange("p (k n) -> p k n", k=2)
        dft_ns = const_b[:, 1024:1536].rearrange("p (k n) -> p k n", k=2)
        rel_up = const_b[:, 1536:2048]
        rel_dn = const_b[:, 2048:2560]
        cos128 = const_b[:, 2560:2816]
        sin128 = const_b[:, 2816:3072]
        rot128 = const_b[:, 3072:3200]
        pow_up = const_b[:, 3200:3456]
        pow_dn = const_b[:, 3456:3712]
        pow_left = const_b[:, 3712:3716]

        lam_rows = y[:, 24 * T:25 * T].rearrange("p (v n) -> p v n", v=4)
        kT4 = yt[:, 26:30, :]
        v4 = y[:, 30 * T:32 * T].rearrange("p (h t n) -> p h t n", h=4, t=TT)
        prow = y[:, 0:3 * P].rearrange("p (t n) -> p t n", t=3)
        zc = yt[:, 16:26, :]
        ctx_sb = y[:, 16 * T:32 * T].rearrange("p (t n) -> p t n", t=TT)
        ada_ring2 = y[:, 16 * T:28 * T].rearrange("p (r n) -> p r n", r=ADA_RING)
        acc_x2 = y[:, 28 * T:28 * T + 384].rearrange("p (t n) -> p t n", t=1)
        gain_bc = y[:, 8 * T:16 * T]
        junk = y[:, 0:8 * T]
        gained = ctx_sb

        PS = ctx.enter_context(nc.psum_tensor("banks", [P, 8, 512], F32))

        def bank(n):
            return PS[:, n, :]

        def halves(ap):
            return ap.rearrange("p (k n) -> p k n", k=2)

        A, B, C, E0 = 0, 1, 2, 4

        s_par = sem("params_landed")
        s_misc = sem("small_inputs_landed")
        s_x = [sem(f"x_landed{t}") for t in range(TT)]
        s_w = [sem(f"weights_landed{k}") for k in range(RING)]
        s_hi = sem("piece_hi")
        s_lo = sem("piece_lo")
        s_used = sem("piece_used")
        s_full = sem("proj_banks_full")
        s_free = sem("proj_banks_free")
        s_aw = [sem(f"ada_landed{k}") for k in range(ADA_RING)]
        s_au = sem("ada_piece_used")
        s_aps = sem("ada_cols_in_psum")
        s_acol = sem("ada_cols_read")
        s_gw = sem("gate_w_landed")
        s_fno = sem("fno_landed")
        s_cb = sem("const_b_landed")
        s_ctx = sem("ctx_landed")
        s_gain = sem("gain_landed")
        s_inv = sem("last_root_ready")
        s_first = sem("first_tokens_scaled")
        s_second = sem("last_tokens_scaled")
        s_out = sem("out_stored")
        s_set = sem("cleared")
        s_pps = sem("params_in_psum")
        s_pc = sem("params_ready")
        s_pe_ = sem("setup_exp")
        s_dec = sem("decay_logs")
        s_stw = sem("state_weights")
        s_n = {k: sem(f"norm_{k}") for k in ("sum", "mean", "root", "diag", "rows", "rows_sb", "psum", "tile", "hi", "lo")}
        s_added = sem("residual_added")
        s_fin = sem("tokens_scaled")
        s_yh = sem("mix_hi")
        s_yl = sem("mix_lo")
        s_gb = sem("gate_rows_in_psum")
        s_gr = sem("gate_rows_ready")
        s_gd = sem("gate_diags_ready")
        S = {}
        for stage, names in {
            "lru": ("conv", "gates", "gate", "tanh", "sig", "y"),
            "swa": ("gate", "scores", "max", "exp", "prob", "probT", "probT_sb", "o", "y"),
            "cq": ("squares", "sums", "mean", "root", "gained", "hi", "lo"),
            "diff": ("gate", "scores", "max", "exp", "prob", "probT", "probT_sb", "o", "sq", "sum", "mean", "root", "y"),
            "mla": ("gate", "rot", "rope", "scores", "max", "exp", "prob", "probT", "probT_sb", "o", "y"),
            "ret": ("gate", "arg", "tables", "rot", "rope", "state", "state_sb", "scaled", "scores", "decayed",
                    "o", "sq", "sum", "mean", "root", "y"),
            "four": ("gate", "cols", "cols_sb", "rows", "rows_sb", "o", "y"),
            "conv": ("y",),
        }.items():
            S[stage] = {k: sem(f"{stage}_{k}") for k in names}

        block = ctx.enter_context(nc.Block())
        order = [s for s, _, _ in STAGES]
        last = order if stop_after is None else order[:order.index(stop_after) + 1]

        def wanted(stage):
            return stage in last

        def stage_loop(eng, stage, unit, post, before):
            unit(0, before)
            if COUNT[stage] > 1:
                with eng.Fori(1, COUNT[stage]) as i:
                    unit(i, lambda p: post(p, i - 1))

        def nothing(p):
            pass

        def squeezed(post, i):
            def hook(p):
                post(2 * p, i)
                post(2 * p + 1, i)
            return hook

        def placed(steps):
            def hook(p):
                for step in steps.get(p, ()):
                    step()
            return hook

        NORM_BANKS = {0: 0, 1: 8, 3: 16, 4: 24, 5: 32}

        def ada_cols(stage, group):
            return PS[:, {"diff": (6, 7)[group % 2], "mla": 7, "ret": 7, "four": 7}.get(stage, 2), 500:506]

        def ada_buffers(stage):
            return (ada_ring2, acc_x2) if stage == "ret" else (ada_ring, acc_x)

        def ada_slab(stage, i, p):
            group = i * (PIECES[stage] // 8) + p // 8
            if not isinstance(group, int) or group > 0:
                return (stage, group - 1) if stage in ADA0 and stage != "swa" else None
            if stage == "out0":
                return "swa", 0
            before = {"cq": "out0", "diff": "cq", "mla": "diff", "out1": "mla", "four": "ret"}.get(stage)
            return before and (before, COUNT[before] * (PIECES[before] // 8) - 1)

        def ada_steps(stage, i, p):
            if stage not in ADA0 or stage == "swa" and not (isinstance(i, int) and i == 0):
                return ()
            return ADA_STEPS[stage].get(p % 8, ())

        def ada_context(stage):
            return stage not in ("diff", "ret")

        FOURS = [(4 * q, 4) for q in range(4)]
        GROUPS = {"out0": FOURS, "out1": [FOURS[0], FOURS[2], FOURS[3], FOURS[1]]}
        GROUPS["out2"] = GROUPS["out3"] = [(2 * q, 2) for q in range(8)] + [(KT + f, n) for f, n in FOURS]
        MIX0 = {"out0": 0, "out1": 4, "out2": 8, "out3": 20}

        def out_cols(i):
            return i * -512 + (D - 512)

        NORM_OF = {"lru": 0, "cq": 1, "ret": 4, "conv": 5}

        def out_pair(stage, p):
            return (0, 1, 4, 5, 6, 7, 2, 3)[p] if stage == "out1" else p

        @block.sync
        def _(sp):
            def row_load(ap, tile, first, n):
                sp.dma_start(prow[first:first + n, tile, :], ap).then_inc(s_par, 16)

            sp.wait_ge(s_set, 1)
            sp.dma_start(ident[:, :], d["const_a"][:, 0:P]).then_inc(s_par, 16)
            row_load(d["norm_gains"].rearrange("l (a b) -> (l a) b", b=P), *G_L0, 32)
            row_load(d["norm_w_2"].rearrange("l (a b) -> (l a) b", b=P), *G_MOD, 32)
            row_load(d["l0_conv_w"].rearrange("l (a b) -> (l a) b", b=P), *CONV_W, 32)
            row_load(d["l0_conv_b"].rearrange("(a b) -> a b", b=P), *CONV_B, 8)
            row_load(d["l0_gate_x_b"], *GX_B, 8)
            row_load(d["l0_gate_a_b"], *GA_B, 8)
            row_load(d["l0_lru_lambda"].rearrange("(a b) -> a b", b=P), *LAM, 8)
            row_load(d["ada_b_2"].rearrange("l (a b) -> (l a) b", b=P), *ADA_B, 96)
            row_load(d["l1_q_norm"].rearrange("(a b) -> a b", b=P), *G_Q, 6)
            row_load(d["l1_kv_norm"].rearrange("(a b) -> a b", b=P), *G_KV, 4)
            row_load(d["l1_subln"].rearrange("(a b) -> a b", b=P), *G_SUB, 1)
            row_load(d["c_2"].rearrange("o (a b) -> (o a) b", b=P), *C_X, 16)
            row_load(d["conv_w_2"].rearrange("o l (a b) -> (o l a) b", b=P), *CONV3_W, 96)
            row_load(d["c_ctx_2"].rearrange("(a b) -> a b", b=P), *C_CTX, 16)
            def two_blocks(t, src):
                return lambda r: r[:, 512 * t:512 * t + 512].rearrange("p (s n) -> p s n", s=2), src

            def sources(stage, i, p):
                if stage == "lru":
                    w = d["l0_w_in"][:, 0:2 * LRU_W].rearrange("(t p) (s n) -> p t s n", p=P, s=2)
                    return [two_blocks(t, w[:, 2 * p + t, :, ds(256 * i, 256)]) for t in range(2)]
                if stage == "kv":
                    w = d["l0_w_in"].rearrange("(t p) n -> p t n", p=P)
                    kk = w[:, 2 * p:2 * p + 2, C_K:C_K + SWA_KV].rearrange("p t (g n) -> p t g n", g=2)

                    def dup(t, n):
                        return lambda r: r[:, t * 384:t * 384 + 256].rearrange("p (g u n) -> p g u n", g=2, u=2)\
                            [:, :, n, :]
                    return [(dup(t, n), kk[:, t, :, :]) for t in range(2) for n in range(2)] + [
                        (lambda r: r[:, 0:768].rearrange("p (t c) -> p t c", t=2)[:, :, 256:384],
                         w[:, 2 * p:2 * p + 2, C_V:C_V + SWA_KV])]
                if stage == "swa":
                    w = d["l0_w_in"].rearrange("(t p) n -> p t n", p=P)

                    def part(n):
                        return lambda r: r[:, 0:1024].rearrange("p (t s n) -> p t s n", t=2, s=2)[:, :, n, :]
                    return [(part(0), w[:, 2 * p:2 * p + 2, ds(256 * i + 2 * LRU_W, 256)]),
                            (part(1), w[:, 2 * p:2 * p + 2, ds(256 * i + C_G, 256)])]
                if stage in ("out0", "out1", "out2", "out3"):
                    name = {"out0": "l0_w_out", "out1": "l1_w_out", "out2": "ev_w_out_2", "out3": "od_w_out_2"}[stage]
                    w = d[name]
                    if len(w.shape) == 3:
                        w = w.rearrange("o k n -> (o k) n")
                    w = w.rearrange("(t p) n -> p t n", p=P)
                    return [(lambda r: r[:, 0:1024].rearrange("p (t n) -> p t n", t=2),
                             w[:, 2 * out_pair(stage, p):2 * out_pair(stage, p) + 2, ds(out_cols(i), 512)])]
                if stage == "cq":
                    w = d["l1_w_in"].rearrange("(t p) n -> p t n", p=P)
                    n = 320 if isinstance(i, int) and i == 2 else 512
                    return [(lambda r: r[:, 0:2 * n].rearrange("p (t n) -> p t n", t=2),
                             w[:, 2 * p:2 * p + 2, ds(512 * i, n)])]
                if stage == "diff":
                    w = d["l1_w_in"][:, C_DIFF:C_DIFF + 4096].rearrange("(t p) (s n) -> p t s n", p=P, s=4)
                    return [(lambda r: r[:, 0:1024].rearrange("p (s n) -> p s n", s=4), w[:, p, :, ds(256 * i, 256)])]
                if stage == "mla":
                    if p < 4:
                        w = d["l1_w_in"].rearrange("(t p) n -> p t n", p=P)
                        return [(lambda r: r[:, 0:1024].rearrange("p (t n) -> p t n", t=4),
                                 w[:, 4 * p:4 * p + 4, ds(256 * i + C_MG, 256)])]
                    if p < 6:
                        w = d["l1_w_ukv"].rearrange("(t p) n -> p t n", p=P)
                        return [(lambda r: r[:, 0:1024].rearrange("p (t n) -> p t n", t=CKV_T),
                                 w[:, :, ds(512 * i + 256 * (p - 4), 256)])]
                    w = d["l1_w_uq"].rearrange("(t p) n -> p t n", p=P)
                    return [(lambda r: r[:, 0:1152].rearrange("p (t n) -> p t n", t=CQ_T),
                             w[:, :, ds(384 * i + 192 * (p - 6), 192)])]
                if stage == "ret":
                    w = d["ev_w_in_2"].rearrange("o (t p) n -> p (o t) n", p=P)
                    qk = w[:, :, 0:2048].rearrange("p t (s n) -> p t s n", s=2)
                    vg = w[:, :, 2048:6144].rearrange("p t (s n) -> p t s n", s=2)
                    return [(lambda r: r[:, 0:256].rearrange("p (s n) -> p s n", s=2), qk[:, p, :, ds(128 * i, 128)]),
                            (lambda r: r[:, 256:768].rearrange("p (s n) -> p s n", s=2), vg[:, p, :, ds(256 * i, 256)])]
                if stage == "four":
                    w = d["ev_w_in_2"].rearrange("o (t p) n -> p (o t) n", p=P)[:, :, 6144:10240]\
                        .rearrange("p t (s n) -> p t s n", s=2)
                    return [two_blocks(t, w[:, 2 * p + t, :, ds(256 * i, 256)]) for t in range(2)]
                w = d["od_w_in_2"].rearrange("o (t p) (s n) -> p (o t) s n", p=P, s=4)
                return [(lambda r: r[:, 0:1024].rearrange("p (s n) -> p s n", s=4), w[:, p, :, ds(256 * i, 256)])]

            def load_ada(stage, group, q):
                u, n = ADA0[stage] + group, ADA_COLS[stage]
                a = u * 8 + q
                if not isinstance(a, int) or a >= ADA_RING:
                    sp.wait_ge(s_au, a - (ADA_RING - 1))
                w = d["ada_w_2"].rearrange("l (t p) n -> p l t n", p=P)
                sp.dma_start(ada_buffers(stage)[0][:, q % ADA_RING, :].rearrange("p (t n) -> p t n", t=2),
                             w[:, 1 if stage == "ret" else 0, 2 * q:2 * q + 2, ds((ADA_FIRST[stage] + group) * n, n)])\
                    .then_inc(s_aw[q % ADA_RING], 16)

            def unit(stage):
                def load(i, hook):
                    for p in range(PIECES[stage]):
                        g = PIECE0[stage] + PIECES[stage] * i + p
                        pieces = sources(stage, i, p)
                        if not isinstance(g, int) or g >= RING:
                            sp.wait_ge(s_lo, g - (RING - 1))
                        for dst, src in pieces:
                            sp.dma_start(dst(w_raw[:, p % RING, :]), src).then_inc(s_w[p % RING], 16)
                        for q in ada_steps(stage, i, p):
                            group = i * (PIECES[stage] // 8) + p // 8
                            if stage == "ret" and isinstance(group, int) and group == 0 and q == 0:
                                sp.wait_ge(s_n["psum"], NORM_BANKS[3] + 8)
                            load_ada(stage, group, q)
                return load

            for stage in last:
                if stage == "cq":
                    with sp.Fori(0, 2) as i:
                        unit(stage)(i, nothing)
                    unit(stage)(2, nothing)
                else:
                    stage_loop(sp, stage, unit(stage), lambda p, i: None, nothing)
            if stop_after is None:
                for h in range(2):
                    for t in range(TT):
                        sp.wait_ge((s_first, s_second)[t], h + 1)
                        sp.dma_start(out[0, t * P:(t + 1) * P, h * D // 2:(h + 1) * D // 2],
                                     x[:, t, h * D // 2:(h + 1) * D // 2]).then_inc(s_out, 16)
                sp.wait_ge(s_out, 16 * 2 * TT)

        def view(ap, *dims):
            names = " ".join("abc"[:len(dims)])
            return ap.rearrange(f"p ({names}) -> p {names}", **dict(zip("abc", dims)))

        def norm_scratch(k):
            scratch, n = (scr_a, 4) if k < 2 else (scr_b, 8)
            return (view(scratch[:, 0:512 * n], n, 512), view(scratch[:, 512 * n:512 * n + 256], TT, P),
                    scratch[:, 512 * n + 256:512 * n + 512])

        lru_x = view(scr_a[:, 0:518], 2, 259)
        lru_xc, lru_g, lru_gi, lru_gr, lru_r, lru_u, lru_sg = (
            scr_a[:, 518 + 512 * n:1030 + 512 * n] for n in range(7))
        gate_w = scr_a[:, 4102:4614].rearrange("p (b w n) -> p b w n", b=2, w=2)
        swa_q, swa_g = scr_a[:, 0:512], scr_a[:, 512:1024]
        swa_k, swa_v = scr_a[:, 1024:1280], view(scr_a[:, 1280:1408], TT, 64)
        swa_s, swa_t = scr_a[:, 1408:2944], scr_a[:, 2944:4480]
        at_q, at_k, at_v, at_g = (scr_a[:, 512 * n:512 * n + 512] for n in range(4))
        dif_s, dif_t = scr_a[:, 2048:3584], scr_a[:, 3584:4352]
        dif_o, dif_sq, dif_r = scr_a[:, 2048:2560], scr_a[:, 2560:3072], scr_a[:, 3072:3584]
        cq_r = view(scr_a[:, 3584:4096], 2, T)
        cq_sq = view(y[:, 0:(CQ_T + CKV_T) * T], CQ_T + CKV_T, T)
        mla_s, mla_t = scr_a[:, 2048:2816], scr_a[:, 2816:3584]
        mla_qr0, mla_qr = scr_a[0:64, 3584:4096], scr_a[0:64, 4096:4608]
        ret_qk, ret_tmp, ret_v, ret_g, ret_kc, ret_vc, ret_S, ret_D, ret_xi = (
            scr_b[:, 512 * n:512 * n + 512] for n in range(9))
        ret_sq, ret_r = ret_kc, ret_vc[:, 0:T]
        four_u, four_g = scr_b[:, 0:512], scr_b[:, 512:1024]
        four_c, four_f = view(scr_b[:, 1024:2048], 2, 512), view(scr_b[:, 2048:2560], 2, T)
        conv_x, conv_g, conv_b, conv_y = (scr_b[:, 512 * n:512 * n + 512] for n in range(4))
        conv_c = scr_b[:, 2576:3088]
        conv_z = scr_b[:, 2048:2576].rearrange("p (b r n) -> p b r n", b=2, r=4)
        gate_rows = scr_b[:, 2560:4608]
        gate_diag = view(scr_b[:, 0:2048], 16, P)
        out_t = view(scr_b[:, 0:1024], TT, 512)

        def pcol(which, n, width=1):
            tile, first = which
            return pc[:, tile, ds(first + n, width)]

        def landed(eng, stage, i, p):
            per = 16 * DMAS[stage]
            eng.wait_ge(s_w[p % RING], LAND0[stage] + per * (i * (PIECES[stage] // RING) + p // RING + 1))

        def width(stage, i):
            return {"kv": 768, "ret": 768, "mla": None}.get(stage, 1024)

        def cols(stage, i, p):
            if stage == "mla":
                return 1152 if p >= 6 else 1024
            if stage == "cq" and isinstance(i, int) and i == 2:
                return 640
            return width(stage, i)

        def bank_count(stage, i, n):
            return BANK0[stage] + len(BANKS[stage]) * i + n

        def all_left(stage, i):
            return bank_count(stage, i, len(BANKS[stage]))

        def pieces_before(stage, i):
            return PIECE0[stage] + PIECES[stage] * i

        def full(eng, stage, i, n):
            if n == len(BANKS[stage]):
                eng.wait_ge(s_used, pieces_before(stage, i) + PIECES[stage])
            else:
                eng.wait_ge(s_full, FULL0[stage] + FULLS[stage] * i + n)

        SUMS = {0: 0, 1: 1, 3: 2, 2: 3, 4: 4, 5: 5, 6: 6}
        DIAGS = {0: 0, 1: 1, 3: 2, 4: 3, 5: 4}
        ROWS = {0: 0, 1: 1, 4: 2, 5: 3}

        def mix_dst(stage, kt):
            second = stage in ("out2", "out3") and not (isinstance(kt, int) and kt >= KT)
            return (act2, kt) if second else (act, kt % KT)

        @block.gpsimd
        def _(pool):
            nc.gpsimd.memset(y[:, 0:3 * P], 0.0)
            nc.gpsimd.memset(ones[:, :], 1.0).then_inc(s_set, 1)
            pool.dma_start(const_a[:, :], d["const_a"][:, P:]).then_inc(s_misc, 16)
            pool.dma_start(sinks[:, :], d["l0_sinks"].partition_broadcast(P)).then_inc(s_misc, 16)
            pool.dma_start(lg[:, :], d["ret_decay_logit_2"].rearrange("o a h -> (o a h)").partition_broadcast(P))\
                .then_inc(s_misc, 16)
            for n, name in enumerate(("l1_lambda_q1", "l1_lambda_k1", "l1_lambda_q2", "l1_lambda_k2")):
                pool.dma_start(lam_rows[:, n, :], d[name].partition_broadcast(P)).then_inc(s_misc, 16)
            gx = d["l0_gate_x_w"].rearrange("b k n -> k b n")
            ga = d["l0_gate_a_w"].rearrange("b k n -> k b n")

            def gates(i):
                pool.dma_start(gate_w[:, :, 0, :], gx[:, ds(2 * i, 2), :]).then_inc(s_gw, 16)
                pool.dma_start(gate_w[:, :, 1, :], ga[:, ds(2 * i, 2), :]).then_inc(s_gw, 16)

            gates(0)
            with pool.Fori(1, COUNT["lru"]) as i:
                pool.wait_ge(S["lru"]["gates"], i)
                gates(i)
            if wanted("ret"):
                pool.wait_ge(s_yl, MIX0["out1"] + len(GROUPS["out1"]))
                pool.dma_start(ctx_sb, d["ctx_2"].rearrange("o (t p) n -> p (o t) n", p=P)).then_inc(s_ctx, 16)
                pool.dma_start(gain_bc, d["final_norm_gain"].partition_broadcast(P)).then_inc(s_gain, 16)
                pool.wait_ge(s_acol, ADA0["ret"])
                pool.dma_start(const_b[:, :], d["const_b"]).then_inc(s_cb, 16)
            if wanted("four"):
                f = d["fno_w_2"].rearrange("o g (c p) n -> p (o g) c n", p=P)
                pool.wait_ge(s_cb, 16)
                pool.dma_start(fno[:, :, :], f[:, 0, :, :]).then_inc(s_fno, 16)
                with pool.Fori(1, COUNT["four"]) as i:
                    pool.wait_ge(S["four"]["o"], i)
                    pool.dma_start(fno[:, :, :], f[:, ds(i, 1), :, :].rearrange("p g c n -> p (g c) n"))\
                        .then_inc(s_fno, 16)
            if wanted("out3"):
                pool.wait_ge(s_yl, MIX0["out3"] + len(GROUPS["out3"]))
                pool.dma_start(gain_bc, d["final_norm_w_2"].partition_broadcast(P)).then_inc(s_gain, 16)

        @block.scalar
        def _(sc):
            def split(stage):
                def run(i, hook):
                    for p in range(PIECES[stage]):
                        g = pieces_before(stage, i) + p
                        n = cols(stage, i, p)
                        landed(sc, stage, i, p)
                        if not isinstance(g, int) or g >= RING:
                            sc.wait_ge(s_used, g - (RING - 1))
                        nc.scalar.activation(w_hi[:, p % RING, 0:n], w_raw[:, p % RING, 0:n], ACT.Copy)\
                            .then_inc(s_hi, 1)
                        hook(p)
                return run

            def copy(dst, src, **k):
                return nc.scalar.activation(dst, src, ACT.Copy, **k)

            def norm_sums(k, src, ready):
                for t in range(TT):
                    ready(t)
                    nc.scalar.drain()
                    last = nc.scalar.activation(scr_a[:, 0:D] if k == 0 else junk, src[:, t, :], ACT.Square,
                                                accum_out=stat[:, 0, t:t + 1])
                last.then_inc(s_n["sum"], 1)

            def norm_root(k):
                sc.wait_ge(s_n["mean"], SUMS[k] + 1)
                nc.scalar.activation(stat[:, 2, :], stat[:, 1, :], ACT.Sqrt).then_inc(s_n["root"], 1)

            def norm_hi(k, dst, order, bias=None):
                buffers = norm_scratch(k)[0]
                for n in order:
                    tmp = halves(buffers[:, n % buffers.shape[1], :])
                    sc.wait_ge(s_n["tile"], NORM_BANKS[k] + n + 1)
                    if bias is None:
                        last = copy(dst[:, 2 * n:2 * n + 2, 0:T], tmp)
                    else:
                        for h in range(2):
                            last = nc.scalar.activation(dst[:, 2 * n + h, 0:T], tmp[:, h, :], ACT.Identity,
                                                        bias=bias(2 * n + h))
                    last.then_inc(s_n["hi"], 1)

            def chunk_sums(i):
                for t in range(TT):
                    last = nc.scalar.activation(junk[:, 512 * t:512 * t + 512], x[:, t, ds(out_cols(i), 512)], ACT.Square,
                                                accum_out=parts[:, t, ds(i, 1)])
                return last

            def out_sums(stage):
                def added(i):
                    nc.scalar.drain()
                    if stage in ("out0", "out1"):
                        sc.wait_ge(s_free, all_left(stage, i))
                    else:
                        sc.wait_ge(s_added, (0 if stage == "out2" else COUNT["out2"]) + i + 1)

                def post(p, i):
                    if p == 5:
                        added(i)
                        chunk_sums(i)

                def last():
                    added(COUNT[stage] - 1)
                    chunk_sums(COUNT[stage] - 1).then_inc(s_n["sum"], 1)
                return post, last

            def mix(stage, q):
                kt, n = GROUPS[stage][q]
                dst, at = mix_dst(stage, kt)
                copy(dst[:, at:at + n, 0:T], yt[:, kt:kt + n, :]).then_inc(s_yh, 1)

            def mix_pair(i):
                copy(act2[:, ds(2 * i, 2), 0:T], yt[:, ds(2 * i, 2), :]).then_inc(s_yh, 1)

            def lru(p, i):
                s = S["lru"]
                if p == 2:
                    sc.wait_ge(s["y"], i + 1)
                    full(sc, "lru", i, 1)
                    copy(lru_x[:, :, 3:259], halves(bank(A))).then_inc(s_free, 1)
                    full(sc, "lru", i, 2)
                    copy(lru_g, bank(B)).then_inc(s_free, 1)
                if p == 3:
                    nc.scalar.drain()
                    nc.scalar.activation(lru_sg, lru_g, ACT.Sigmoid).then_inc(s["gate"], 1)
                if p == 4:
                    sc.wait_ge(s["gates"], i + 1)
                    for b in range(2):
                        nc.scalar.activation(halves(lru_gr)[:, b, :], halves(bank(5))[:, b, :], ACT.Sigmoid,
                                             bias=pcol(GA_B, 2 * i + b))
                    for b in range(2):
                        nc.scalar.activation(halves(lru_gi)[:, b, :], halves(bank(4))[:, b, :], ACT.Sigmoid,
                                             bias=pcol(GX_B, 2 * i + b))
                if p == 5:
                    nc.scalar.drain()
                    for b in range(2):
                        last = nc.scalar.activation(halves(lru_gr)[:, b, :], halves(lru_gr)[:, b, :], ACT.Tanh,
                                                    scale=lru_c[:, 0, ds(2 * i + b, 1)])
                    last.then_inc(s["tanh"], 1)
                if p == 6:
                    nc.scalar.drain()
                    nc.scalar.activation(lru_u, lru_gr, ACT.Sqrt, scale=-1.0).then_inc(s["sig"], 1)

            def kv(p, i=0):
                if p == 2:
                    full(sc, "kv", 0, 2)
                    for h in range(4):
                        last = copy(kT4[:, h, :], halves(bank(A))[:, h // 2, :])
                    last.then_inc(s_free, 1)
                    for h in range(4):
                        last = copy(v4[:, h, :, :], bank(B)[:, 0:256].rearrange("p (t g n) -> p t g n", t=2, g=2)
                                    [:, :, h // 2, :])
                    last.then_inc(s_free, 1)

            def exps(s_tile, heads, done, sink=False):
                first, n = heads[0], len(heads)
                if sink:
                    nc.scalar.activation(soft[:, 3, 2 * first:2 * (first + n)], soft[:, 3, 2 * first:2 * (first + n)],
                                         ACT.Exp)
                v = s_tile.rearrange("p (h c) -> p h c", c=384)
                for h in heads:
                    for b, (lo, hi) in enumerate(((0, 128), (128, 384))):
                        last = nc.scalar.activation(v[:, h, lo:hi], v[:, h, lo:hi], ACT.Exp,
                                                    bias=soft[:, 1, 2 * h + b:2 * h + b + 1],
                                                    accum_out=soft[:, 2, 2 * h + b:2 * h + b + 1])
                last.then_inc(done, 1)

            def swa(p, i):
                s = S["swa"]
                if p == 2:
                    sc.wait_ge(s["y"], i + 1)
                    copy(swa_k, kT4[:, ds(i, 1), :].rearrange("p a n -> p (a n)"))
                    copy(swa_v, v4[:, ds(i, 1), :, :].rearrange("p a t n -> p (a t) n"))
                    full(sc, "swa", i, 1)
                    copy(swa_q, bank(A), scale=SWA_D ** -0.5).then_inc(s_free, 1)
                    full(sc, "swa", i, 2)
                    copy(swa_g, bank(B)).then_inc(s_free, 1)
                    nc.scalar.drain()
                    nc.scalar.activation(swa_g, swa_g, ACT.Silu).then_inc(s["gate"], 1)
                if p == 4:
                    for n in range(2):
                        sc.wait_ge(s["max"], 2 * i + n + 1)
                        exps(swa_s, (2 * n, 2 * n + 1), s["exp"], True)
                if p == 6:
                    sc.wait_ge(s["probT"], i + 1)
                    copy(view(swa_t, 4, 384), PS[:, 4:8, 0:384]).then_inc(s["probT_sb"], 1)

            def cq_evac(i, last):
                full(sc, "cq", i, 1)
                if not last:
                    copy(zc[:, ds(4 * i, 2), :], halves(bank(A))).then_inc(s_free, 1)
                    full(sc, "cq", i, 2)
                    copy(zc[:, ds(4 * i + 2, 2), :], halves(bank(B))).then_inc(s_free, 1)
                else:
                    copy(zc[:, 8:10, :], halves(bank(A))).then_inc(s_free, 1)
                    full(sc, "cq", i, 2)
                    copy(k_raw[:, :], PS[0:64, B, 0:T]).then_inc(s_free, 1)

            def cq(p, i):
                if p == 2:
                    cq_evac(i, False)

            def cq_end(p, i=2):
                s = S["cq"]
                if p == 2:
                    cq_evac(2, True)
                    nc.scalar.drain()
                    nc.scalar.activation(cq_sq, zc, ACT.Square).then_inc(s["squares"], 1)
                if p == 6:
                    sc.wait_ge(s["mean"], 1)
                    nc.scalar.activation(cq_r, cq_r, ACT.Sqrt).then_inc(s["root"], 1)
                if p == 8:
                    sc.wait_ge(s["gained"], 1)
                    copy(cn[:, :, 0:T], zc).then_inc(s["hi"], 1)

            def diff(p, i):
                s = S["diff"]
                if p == 2:
                    if isinstance(i, int) and i == 0:
                        sc.wait_ge(S["cq"]["lo"], 1)
                    sc.wait_ge(s["y"], i + 1)
                    full(sc, "diff", i, 1)
                    copy(at_q, bank(A), scale=64 ** -0.5).then_inc(s_free, 1)
                    full(sc, "diff", i, 2)
                    copy(at_k, bank(B)).then_inc(s_free, 1)
                    full(sc, "diff", i, 3)
                    copy(at_g, bank(C)).then_inc(s_free, 1)
                    full(sc, "diff", i, 4)
                    copy(at_v, bank(3)).then_inc(s_free, 1)
                    nc.scalar.drain()
                    nc.scalar.activation(at_g, at_g, ACT.Silu).then_inc(s["gate"], 1)
                if p == 6:
                    sc.wait_ge(s["max"], i + 1)
                    exps(dif_s, range(4), s["exp"])
                if p == 10:
                    sc.wait_ge(s["probT"], i + 1)
                    copy(view(dif_t, 2, 384), PS[:, 4:6, 0:384]).then_inc(s["probT_sb"], 1)
                if p == 12:
                    sc.wait_ge(s["o"], i + 1)
                    copy(dif_o, bank(6))
                    nc.scalar.activation(dif_sq, bank(6), ACT.Square).then_inc(s["sq"], 1)
                if p == 14:
                    sc.wait_ge(s["mean"], i + 1)
                    nc.scalar.activation(dif_r, dif_r, ACT.Sqrt).then_inc(s["root"], 1)

            def mla(p, i):
                s = S["mla"]
                if p == 2:
                    sc.wait_ge(s["y"], i + 1)
                    full(sc, "mla", i, 5)
                    copy(at_g, bank(C)).then_inc(s_free, 1)
                    copy(mla_qr0, PS[0:64, 4, :], scale=MLA_SCALE).then_inc(s_free, 1)
                    copy(at_q, bank(A), scale=MLA_SCALE).then_inc(s_free, 1)
                    copy(at_k, bank(B)).then_inc(s_free, 1)
                    copy(at_v, bank(3)).then_inc(s_free, 1)
                    nc.scalar.drain()
                    nc.scalar.activation(at_g, at_g, ACT.Silu).then_inc(s["gate"], 1)
                if p == 4:
                    sc.wait_ge(s["max"], i + 1)
                    exps(mla_s, range(2), s["exp"])
                if p == 6:
                    sc.wait_ge(s["probT"], i + 1)
                    copy(view(mla_t, 2, 384), PS[:, 5:7, 0:384]).then_inc(s["probT_sb"], 1)

            def ret(p, i):
                s = S["ret"]
                if p == 2:
                    sc.wait_ge(s["y"], i + 1)
                    full(sc, "ret", i, 1)
                    copy(ret_qk, bank(A)).then_inc(s_free, 1)
                    full(sc, "ret", i, 2)
                    copy(ret_v, bank(C)).then_inc(s_free, 1)
                    for t in range(TT):
                        full(sc, "ret", i, 3 + t)
                        ctx_k, ctx_v = PS[:, 3 + t, 0:P], PS[:, 3 + t, P:384]
                        for n in range(2):
                            wcol = state_w[:, ds(i, 1), 2 * n + t:2 * n + t + 1].rearrange("p a b -> p (a b)")
                            copy(ret_kc[:, (2 * n + t) * P:(2 * n + t + 1) * P], ctx_k, scale=wcol)
                        copy(ret_vc[:, t * T:(t + 1) * T], ctx_v).then_inc(s_free, 1)
                    full(sc, "ret", i, 5)
                    copy(ret_g, bank(B)).then_inc(s_free, 1)
                if p == 3:
                    nc.scalar.drain()
                    nc.scalar.activation(ret_g, ret_g, ACT.Silu).then_inc(s["gate"], 1)
                    sc.wait_ge(s["arg"], i + 1)
                    nc.scalar.activation(ret_D, ret_D, ACT.Exp)
                    nc.scalar.activation(ret_xi[:, 0:T], pow_up, ACT.Exp, scale=lg[:, ds(i, 1)])
                    nc.scalar.activation(ret_xi[:, T:], pow_dn, ACT.Exp, scale=lg[:, ds(i + RET_H, 1)])\
                        .then_inc(s["tables"], 1)
                if p == 4:
                    sc.wait_ge(s["state"], i + 1)
                    copy(ret_S, bank(6)).then_inc(s["state_sb"], 1)
                if p == 11:
                    sc.wait_ge(s["o"], i + 1)
                    nc.scalar.activation(ret_sq, bank(5), ACT.Square).then_inc(s["sq"], 1)
                if p == 13:
                    sc.wait_ge(s["mean"], i + 1)
                    nc.scalar.activation(ret_r, ret_r, ACT.Sqrt).then_inc(s["root"], 1)

            def four(p, i):
                s = S["four"]
                if p == 2:
                    sc.wait_ge(s["y"], i + 1)
                    full(sc, "four", i, 1)
                    copy(four_u, bank(A)).then_inc(s_free, 1)
                    full(sc, "four", i, 2)
                    copy(four_g, bank(B)).then_inc(s_free, 1)
                    nc.scalar.drain()
                    nc.scalar.activation(four_g, four_g, ACT.Silu).then_inc(s["gate"], 1)
                if p == 4:
                    sc.wait_ge(s["cols"], i + 1)
                    copy(four_c, PS[:, 4:6, :]).then_inc(s["cols_sb"], 1)
                if p == 6:
                    sc.wait_ge(s["rows"], i + 1)
                    copy(four_f, halves(bank(6))).then_inc(s["rows_sb"], 1)

            def conv(p, i):
                s = S["conv"]
                if p == 2:
                    sc.wait_ge(s["y"], i + 1)
                    full(sc, "conv", i, 1)
                    copy(conv_b, bank(A)).then_inc(s_free, 1)
                    full(sc, "conv", i, 2)
                    copy(conv_x, bank(B)).then_inc(s_free, 1)
                    full(sc, "conv", i, 3)
                    copy(conv_c, bank(C)).then_inc(s_free, 1)
                    full(sc, "conv", i, 4)
                    nc.scalar.activation(conv_g, bank(3), ACT.Silu).then_inc(s_free, 1)

            def gate_rows_copy(n):
                sc.wait_ge(s_gb, n)
                copy(view(gate_rows, 4, 512), PS[:, 4:8, :]).then_inc(s_gr, 1)

            def none(p, i):
                pass

            for t in range(TT):
                sc.dma_start(x[:, t, :], d["x"][0, t * P:(t + 1) * P, :]).then_inc(s_x[t], 16)

            def parameters():
                sc.wait_ge(s_misc, 16 * N_MISC)
                sc.wait_ge(s_pc, 1)
                nc.scalar.activation(silu_c[:, 0, :], pc[:, 1, C_X[1]:C_X[1] + KT], ACT.Silu)
                nc.scalar.activation(silu_c[:, 1, :], pc[:, 2, C_CTX[1]:C_CTX[1] + KT], ACT.Silu)
                nc.scalar.activation(lru_c[:, 1, :], pc[:, 0, LAM[1]:LAM[1] + 8], ACT.Abs)
                nc.scalar.drain()
                nc.scalar.activation(lru_c[:, 1, :], lru_c[:, 1, :], ACT.Exp, scale=-1.0)
                nc.scalar.activation(lg[:, :], lg[:, :], ACT.Exp)
                nc.scalar.activation(nlam[:, :], nlam[:, :], ACT.Exp).then_inc(s_pe_, 1)

            def norm_steps(first, *args):
                k, dst, bias = args
                return {2: [*first, lambda: norm_hi(k, dst, range(4), bias)],
                        **{p: [lambda p=p: norm_hi(k, dst, (p + 1,), bias)] for p in (3, 4, 5, 6)}}

            def after_out(k, sums, bias=None):
                return norm_steps([sums, lambda: norm_root(k)], k, act, bias)

            def shift(cols, first):
                return lambda f: cols[:, first + f:first + f + 1]

            def context_root():
                norm_sums(3, ctx_sb, lambda t: sc.wait_ge(s_ctx, 16) if t == 0 else None)
                norm_root(3)

            def second_block():
                sums1()
                norm_root(2)
                norm_sums(4, x, lambda t: sc.wait_ge(s_fin, t + 1))
                norm_hi(3, act2, range(4))
                norm_root(4)
                norm_hi(3, act2, range(4, 8))

            def decay_to_end():
                sc.wait_ge(s_dec, 1)
                nc.scalar.activation(state_w[:, :, :], state_w[:, :, :], ACT.Exp).then_inc(s_stw, 1)

            def step(post, n, i):
                return lambda: post(n, i)

            def mixes(stage, *groups):
                return [lambda q=q: mix(stage, q) for q in groups]

            def projections_through(stage):
                return lambda: sc.wait_ge(s_used, pieces_before(stage, 0))

            def y_ready(stage):
                return lambda: sc.wait_ge(S[stage]["y"], COUNT[stage] + 1)

            norm_sums(0, x, lambda t: sc.wait_ge(s_x[t], 16))
            norm_root(0)
            parameters()
            stage_loop(sc, "lru", split("lru"), lru, placed({
                **norm_steps([], 0, act, None)}))
            if wanted("kv"):
                split("kv")(0, lambda p: lru(p, COUNT["lru"] - 1))
                stage_loop(sc, "swa", split("swa"), swa, kv)
            if wanted("out0"):
                n = COUNT["swa"] - 1
                post0, sums0 = out_sums("out0")
                stage_loop(sc, "out0", split("out0"), post0, placed({
                    2: [step(swa, 2, n), projections_through("out0"), *mixes("out0", 0, 1, 2), step(swa, 4, n)],
                    5: [step(swa, 6, n)],
                    6: [y_ready("swa"), *mixes("out0", 3)]}))
            if wanted("cq"):
                split("cq")(0, placed(after_out(1, sums0)))
                with sc.Fori(1, 2) as i:
                    split("cq")(i, lambda p: cq(p, i - 1))
                split("cq")(2, lambda p: cq(p, 1))
            if wanted("diff"):
                stage_loop(sc, "diff", split("diff"), diff, cq_end)
                stage_loop(sc, "mla", split("mla"), mla, squeezed(diff, COUNT["diff"] - 1))
            if wanted("out1"):
                n = COUNT["mla"] - 1
                post1, sums1 = out_sums("out1")
                stage_loop(sc, "out1", split("out1"), post1, placed({
                    2: [step(mla, 2, n), projections_through("out1"), *mixes("out1", 0, 1, 2), step(mla, 4, n)],
                    5: [step(mla, 6, n)],
                    6: [y_ready("mla"), *mixes("out1", 3)]}))
            if wanted("ret"):
                stage_loop(sc, "ret", split("ret"), ret, placed({
                    **norm_steps([second_block], 4, act, shift(ada_x, 0)), 0: [context_root], 10: [decay_to_end], 14: [lambda: sc.wait_ge(s_stw, 2)]}))
            if wanted("four"):
                def four_and_mix(p, i):
                    four(p, i)
                    if p == 5:
                        mix_pair(i)
                stage_loop(sc, "four", split("four"), four_and_mix, squeezed(ret, COUNT["ret"] - 1))
            if wanted("out2"):
                n = COUNT["four"] - 1
                post2, sums2 = out_sums("out2")
                stage_loop(sc, "out2", split("out2"), post2, placed({
                    1: [lambda: mix_pair(KT // 2 - 1), step(four, 2, n)],
                    3: [step(four, 4, n), projections_through("out2"), *mixes("out2", 8, 9)],
                    4: mixes("out2", 10),
                    5: [step(four, 6, n)],
                    7: [y_ready("four"), *mixes("out2", 11)],
                    12: [lambda: gate_rows_copy(1)]}))
            if wanted("conv"):
                def conv_and_mix(p, i):
                    conv(p, i)
                    if p == 8:
                        mix_pair(i - 8)
                split("conv")(0, placed(after_out(5, sums2, shift(ada_x, 48))))
                with sc.Fori(1, 9) as i:
                    split("conv")(i, lambda p: conv(p, i - 1))
                with sc.Fori(9, COUNT["conv"]) as i:
                    split("conv")(i, lambda p: conv_and_mix(p, i - 1))
            if wanted("out3"):
                n = COUNT["conv"] - 1
                post3, sums3 = out_sums("out3")
                stage_loop(sc, "out3", split("out3"), post3, placed({
                    1: [lambda: mix_pair(KT // 2 - 1)],
                    2: [step(conv, 2, n), projections_through("out3"), *mixes("out3", 8, 9)],
                    4: mixes("out3", 10),
                    7: [y_ready("conv"), *mixes("out3", 11)],
                    12: [lambda: gate_rows_copy(2)]}))
                sums3()
                norm_root(6)
                sc.wait_ge(s_inv, 1)
                for h in range(2):
                    half = slice(h * D // 2, (h + 1) * D // 2)
                    copy(x[:, 0, half], gained[:, 0, half], scale=stat[:, 3, 0:1]).then_inc(s_first, 1)

        @block.vector
        def _(ve):
            drain = nc.vector.drain
            tt = nc.vector.tensor_tensor
            stt = nc.vector.scalar_tensor_tensor
            ts = nc.vector.tensor_scalar

            def ada_column(slab, sums):
                stage, group = slab
                n = ADA_COLS[stage] // P
                first = n * (ADA_FIRST[stage] + group) + (48 if stage == "ret" else 0)
                ve.wait_ge(s_aps, ADA0[stage] + group + 1)
                r = tt(ada_x[:, ds(first, n)], sums[:, 0:n], pcol(ADA_B, first, n), ALU.add)
                if ada_context(stage):
                    r = tt(ada_c[:, ds(first, n)], sums[:, 3:3 + n], pcol(ADA_B, first, n), ALU.add)
                r.then_inc(s_acol, 1)

            def ada_piece(stage, group, q):
                ring, total = ada_buffers(stage)
                n = ADA_COLS[stage]
                ve.wait_ge(s_aw[q % ADA_RING], 16 * ((ADA0[stage] + group) * 2 + q // ADA_RING + 1))
                for t in range(2):
                    kt = 2 * q + t
                    w = ring[:, q % ADA_RING, t * n:(t + 1) * n]
                    for c, acc in ((1, acc_c), (0, total)) if ada_context(stage) else ((0, total),):
                        cond, sums = silu_c[:, c, kt:kt + 1], acc[:, t % acc.shape[1], :]
                        if kt < acc.shape[1]:
                            last = ts(sums, w, cond, None, ALU.mult)
                        else:
                            last = stt(sums, w, cond, sums, ALU.mult, ALU.add)
                    if t == 0 and acc.shape[1] == 1:
                        drain()
                last.then_inc(s_au, 1)
                drain()

            def split(stage):
                def run(i, hook):
                    for p in range(PIECES[stage]):
                        g = pieces_before(stage, i) + p
                        n = cols(stage, i, p)
                        ve.wait_ge(s_hi, g + 1)
                        tt(w_lo[:, p % RING, 0:n], w_raw[:, p % RING, 0:n], w_hi[:, p % RING, 0:n].bitcast(F32),
                           ALU.subtract).then_inc(s_lo, 1)
                        slab = ada_slab(stage, i, p) if p % 8 == ADA_COL else None
                        if slab and stage == "mla":
                            ada_column(slab, ada_cols(stage, p // 8))
                        hook(p)
                        if slab and stage != "mla":
                            ada_column(slab, ada_cols(stage, p // 8))
                        for q in ada_steps(stage, i, p):
                            ada_piece(stage, i * (PIECES[stage] // 8) + p // 8, q)
                return run

            def root(k):
                ve.wait_ge(s_n["sum"], SUMS[k] + 1)
                if k in (1, 2, 5, 6):
                    nc.vector.tensor_reduce(stat[:, 0, :], parts[:, :, :], AX, ALU.add)
                    drain()
                ts(stat[:, 1, :], stat[:, 0, :], 1.0 / D, EPS, ALU.mult, ALU.add).then_inc(s_n["mean"], 1)
                ve.wait_ge(s_n["root"], SUMS[k] + 1)
                nc.vector.reciprocal(stat[:, 3, :], stat[:, 2, :])
                drain()
                tt(stat[:, 2, :], stat[:, 3, :], stat[:, 3, :], ALU.mult)
                drain()
                tt(stat[:, 2, :], stat[:, 2, :], stat[:, 1, :], ALU.mult)
                drain()
                ts(stat[:, 2, :], stat[:, 2, :], -0.5, 1.5, ALU.mult, ALU.add)
                drain()
                tt(stat[:, 3, :], stat[:, 3, :], stat[:, 2, :], ALU.mult)
                drain()

            def diagonals(k):
                diag = norm_scratch(k)[1]
                for t in range(TT):
                    last = ts(diag[:, t, :], ident[:, :], stat[:, 3, t:t + 1], None, ALU.mult)
                last.then_inc(s_n["diag"], 1)

            def tiles(k, gain, bias, order):
                buffers, _, roots = norm_scratch(k)
                for n in order:
                    tmp = buffers[:, n % buffers.shape[1], :]
                    ve.wait_ge(s_n["psum"], NORM_BANKS[k] + (7 if n < 7 else 8))
                    for h in range(2):
                        f, dst, src = 2 * n + h, tmp[:, h * T:(h + 1) * T], PS[:, n, h * T:(h + 1) * T]
                        if k == 3:
                            last = ts(dst, src, gain(f), bias(f), ALU.mult, ALU.add)
                        else:
                            last = stt(dst, src, gain(f), roots, ALU.mult, ALU.mult)
                    last.then_inc(s_n["tile"], 1)

            def lows(k, bias, dst, order):
                buffers = norm_scratch(k)[0]
                for n in order:
                    tmp = buffers[:, n % buffers.shape[1], :]
                    ve.wait_ge(s_n["hi"], NORM_BANKS[k] + n + 1)
                    hi = dst[:, 2 * n:2 * n + 2, 0:T].bitcast(F32)
                    if bias is None:
                        last = tt(dst[:, 2 * n:2 * n + 2, T:2 * T], halves(tmp), hi, ALU.subtract)
                    else:
                        for h in range(2):
                            last = stt(dst[:, 2 * n + h, T:2 * T], tmp[:, h * T:(h + 1) * T], bias(2 * n + h),
                                       hi[:, h, :], ALU.add, ALU.subtract)
                    last.then_inc(s_n["lo"], 1)

            def broadcast_roots(k):
                ve.wait_ge(s_n["rows"], ROWS[k] + 1)
                nc.vector.tensor_copy(norm_scratch(k)[2], PS[:, 7, 0:T]).then_inc(s_n["rows_sb"], 1)
                drain()

            def normed(k, gain, bias, dst, order):
                for n in order:
                    tiles(k, gain, bias, [n])
                    if n > order[0]:
                        lows(k, bias, dst, [n - 1])
                drain()
                lows(k, bias, dst, [order[-1]])

            def norm(k, gain, bias, dst, order):
                root(k)
                diagonals(k)
                broadcast_roots(k)
                normed(k, gain, bias, dst, order)

            def norm_steps(first, *args):
                return {2: [first], 3: [lambda: normed(*args, (4,))], 4: [lambda: normed(*args, (5,))],
                        5: [lambda: normed(*args, (6,))], 6: [lambda: normed(*args, (7,)), drain]}

            def scaled():
                root(2)
                ve.wait_ge(s_gain, 16)
                for t in range(TT):
                    stt(x[:, t, :], x[:, t, :], stat[:, 3, t:t + 1], gain_bc, ALU.mult, ALU.mult)\
                        .then_inc(s_fin, 1)

            def mix(stage, q):
                kt, n = GROUPS[stage][q]
                dst, at = mix_dst(stage, kt)
                ve.wait_ge(s_yh, MIX0[stage] + q + 1)
                tt(dst[:, at:at + n, T:2 * T], yt[:, kt:kt + n, :], dst[:, at:at + n, 0:T].bitcast(F32),
                   ALU.subtract).then_inc(s_yl, 1)

            def mix_pair(stage, i):
                ve.wait_ge(s_yh, MIX0[stage] + i + 1)
                tt(act2[:, ds(2 * i, 2), T:2 * T], yt[:, ds(2 * i, 2), :], act2[:, ds(2 * i, 2), 0:T].bitcast(F32),
                   ALU.subtract).then_inc(s_yl, 1)

            def lru(p, i):
                s = S["lru"]
                if p == 2:
                    ve.wait_ge(s_free, bank_count("lru", i, 1))
                    xc = halves(lru_xc)
                    for b in range(2):
                        ts(xc[:, b, :], lru_x[:, b, 3:259], pcol(CONV_W, 24 + 2 * i + b),
                           pcol(CONV_B, 2 * i + b), ALU.mult, ALU.add)
                    for tap in range(3):
                        drain()
                        for b in range(2):
                            last = stt(xc[:, b, :], lru_x[:, b, tap:tap + T], pcol(CONV_W, 8 * tap + 2 * i + b),
                                       xc[:, b, :], ALU.mult, ALU.add)
                    last.then_inc(s["conv"], 1)
                if p == 4:
                    ve.wait_ge(s["gate"], i + 1)
                    tt(lru_g, lru_g, lru_sg, ALU.mult)
                if p == 5:
                    ve.wait_ge(s["tanh"], i + 1)
                    ts(lru_r, lru_gr, -1.0, 1.0, ALU.mult, ALU.add)
                    drain()
                    nc.vector.reciprocal(lru_r, lru_r)
                    drain()
                if p == 7:
                    tt(lru_gi, lru_gi, lru_xc, ALU.mult)
                    ve.wait_ge(s["sig"], i + 1)
                    stt(lru_u, lru_u, 2.0, lru_r, ALU.mult, ALU.mult)
                    stt(lru_gr, lru_gr, 1.0, lru_r, ALU.add, ALU.mult)
                    drain()
                    tt(lru_u, lru_u, lru_gi, ALU.mult)
                    drain()
                    for b in range(2):
                        nc.vector.tensor_tensor_scan(halves(lru_xc)[:, b, :], halves(lru_gr)[:, b, :],
                                                     halves(lru_u)[:, b, :], 0.0, ALU.mult, ALU.add)
                    drain()
                    tt(yt[:, ds(2 * i, 2), :], halves(lru_xc), halves(lru_g), ALU.mult).then_inc(s["y"], 1)

            def kv(p, i=0):
                pass

            def scores_max(s_tile, heads, mask, first_bank, done, sink=None):
                h0, n = heads[0], len(heads)
                v = s_tile.rearrange("p (h c) -> p h c", c=384)[:, h0:h0 + n, :]
                tt(v, PS[:, first_bank + h0:first_bank + h0 + n, 0:384],
                   mask.unsqueeze(1).broadcast_to([P, n, 384]), ALU.add)
                drain()
                both = slice(2 * h0, 2 * (h0 + n))
                mx = soft[:, 0, both].rearrange("p (h b) -> p h b", b=2)
                nc.vector.tensor_reduce(mx[:, :, 0], v[:, :, 0:128], AX, ALU.max)
                nc.vector.tensor_reduce(mx[:, :, 1], v[:, :, 128:384], AX, ALU.max)
                drain()
                if sink is not None:
                    tt(mx, mx, sink, ALU.max)
                    drain()
                    tt(soft[:, 3, both].rearrange("p (h b) -> p h b", b=2), sink, mx, ALU.subtract)
                ts(soft[:, 1, both], soft[:, 0, both], -1.0, None, ALU.mult).then_inc(done, 1)

            def normalise(s_tile, heads, weight=None):
                h0, n = heads[0], len(heads)
                v = s_tile.rearrange("p (h c) -> p h c", c=384)[:, h0:h0 + n, :]
                both = slice(2 * h0, 2 * (h0 + n))
                r = soft[:, 4, both].rearrange("p (h b) -> p h b", b=2)
                nc.vector.reciprocal(soft[:, 4, both], soft[:, 2, both])
                drain()
                if weight is not None:
                    weight(soft[:, 4, both])
                    drain()
                tt(v[:, :, 0:128], v[:, :, 0:128], r[:, :, 0:1].broadcast_to([P, n, 128]), ALU.mult)
                return tt(v[:, :, 128:384], v[:, :, 128:384], r[:, :, 1:2].broadcast_to([P, n, 256]), ALU.mult)

            def swa(p, i):
                s = S["swa"]
                if p == 3:
                    for n in range(2):
                        ve.wait_ge(s["scores"], 2 * i + n + 1)
                        sink = sinks[:, ds(4 * i + 2 * n, 2)].unsqueeze(2).broadcast_to([P, 2, 2])
                        scores_max(swa_s, (2 * n, 2 * n + 1), band, 4, s["max"], sink)
                if p == 4:
                    for n in range(2):
                        ve.wait_ge(s["exp"], 2 * i + n + 1)
                        tt(soft[:, 2, 4 * n:4 * n + 4], soft[:, 2, 4 * n:4 * n + 4], soft[:, 3, 4 * n:4 * n + 4], ALU.add)
                        drain()
                        last = normalise(swa_s, (2 * n, 2 * n + 1))
                    last.then_inc(s["prob"], 1)
                if p == 7:
                    ve.wait_ge(s["o"], i + 1)
                    ve.wait_ge(s["gate"], i + 1)
                    tt(yt[:, ds(2 * i + 8, 2), :], halves(bank(4)), halves(swa_g), ALU.mult).then_inc(s["y"], 1)

            def cq_end(p, i=2):
                s = S["cq"]
                if p == 6:
                    ve.wait_ge(s["sums"], 1)
                    ts(cq_r[:, 0, :], PS[:, 5, 0:T], 1.0 / Q_RANK, EPS, ALU.mult, ALU.add)
                    ts(cq_r[:, 1, :], PS[:, 7, 0:T], 1.0 / KV_RANK, EPS, ALU.mult, ALU.add).then_inc(s["mean"], 1)
                    rot = at_q[0:64, 0:T]
                    tt(rot, PS[0:64, 4, 0:T], sin64, ALU.mult)
                    tt(k_rot[:, :], k_raw[:, :], cos64, ALU.mult)
                    drain()
                    tt(k_rot[:, :], k_rot[:, :], rot, ALU.add)
                if p == 7:
                    ve.wait_ge(s["root"], 1)
                    nc.vector.reciprocal(cq_r, cq_r)
                    drain()
                    for t in range(CQ_T + CKV_T):
                        gain = pcol(G_Q, t) if t < CQ_T else pcol(G_KV, t - CQ_T)
                        last = stt(zc[:, t, :], zc[:, t, :], gain, cq_r[:, 0 if t < CQ_T else 1, :],
                                   ALU.mult, ALU.mult)
                    last.then_inc(s["gained"], 1)
                if p == 9:
                    ve.wait_ge(s["hi"], 1)
                    tt(cn[:, :, T:2 * T], zc, cn[:, :, 0:T].bitcast(F32), ALU.subtract).then_inc(s["lo"], 1)

            def diff(p, i):
                s = S["diff"]
                if p == 6:
                    ve.wait_ge(s["scores"], i + 1)
                    scores_max(dif_s, range(4), causal, 4, s["max"])
                if p == 8:
                    ve.wait_ge(s["exp"], i + 1)

                    def second(r):
                        r = r.rearrange("p (h c b) -> p h c b", h=2, c=2)[:, :, 1, :]
                        ts(r, r, nlam[:, 0:1], None, ALU.mult)
                    normalise(dif_s, range(4), second)
                    drain()
                    v = dif_s.rearrange("p (h c n) -> p h c n", h=2, c=2)
                    tt(v[:, :, 0, :], v[:, :, 0, :], v[:, :, 1, :], ALU.add).then_inc(s["prob"], 1)
                if p == 14:
                    ve.wait_ge(s["sum"], i + 1)
                    ts(dif_r, bank(5), 1.0 / 128, EPS, ALU.mult, ALU.add).then_inc(s["mean"], 1)
                if p == 15:
                    ve.wait_ge(s["root"], i + 1)
                    nc.vector.reciprocal(dif_r, dif_r)
                    drain()
                    stt(dif_o, dif_o, sub_g[:, :], dif_r, ALU.mult, ALU.mult)
                    drain()
                    ve.wait_ge(s["gate"], i + 1)
                    tt(yt[:, ds(2 * i + 8, 2), :], halves(dif_o), halves(at_g), ALU.mult).then_inc(s["y"], 1)

            def mla(p, i):
                s = S["mla"]
                if p == 3:
                    ve.wait_ge(s["rot"], i + 1)
                    v0, v1 = halves(mla_qr0), halves(mla_qr)
                    tt(v1, halves(PS[0:64, 5, :]), sin64.unsqueeze(1).broadcast_to([64, 2, T]), ALU.mult)
                    tt(v0, v0, cos64.unsqueeze(1).broadcast_to([64, 2, T]), ALU.mult)
                    drain()
                    tt(v1, v1, v0, ALU.add).then_inc(s["rope"], 1)
                    ve.wait_ge(s["scores"], i + 1)
                    scores_max(mla_s, range(2), causal, 5, s["max"])
                if p == 4:
                    ve.wait_ge(s["exp"], i + 1)
                    normalise(mla_s, range(2)).then_inc(s["prob"], 1)
                if p == 7:
                    ve.wait_ge(s["o"], i + 1)
                    ve.wait_ge(s["gate"], i + 1)
                    tt(yt[:, ds(2 * i, 2), :], halves(bank(5)), halves(at_g), ALU.mult).then_inc(s["y"], 1)

            def ret(p, i):
                s = S["ret"]
                if p == 0:
                    ts(ret_D, rel_up, lg[:, ds(i, 1)], None, ALU.mult)
                    drain()
                    stt(ret_D, rel_dn, lg[:, ds(i + RET_H, 1)], ret_D, ALU.mult, ALU.add).then_inc(s["arg"], 1)
                if p == 4:
                    ve.wait_ge(s["rot"], i + 1)
                    tt(halves(ret_tmp), halves(bank(5)), sin128.unsqueeze(1).broadcast_to([P, 2, T]), ALU.mult)
                    tt(halves(ret_qk), halves(ret_qk), cos128.unsqueeze(1).broadcast_to([P, 2, T]), ALU.mult)
                    drain()
                    tt(ret_qk, ret_qk, ret_tmp, ALU.add).then_inc(s["rope"], 1)
                if p == 5:
                    drain()
                    ve.wait_ge(s["tables"], i + 1)
                    q2 = ret_qk[:, 0:T].unsqueeze(1).broadcast_to([P, 2, T])
                    tt(halves(ret_xi), halves(ret_xi), q2, ALU.mult).then_inc(s["scaled"], 1)
                if p == 8:
                    ve.wait_ge(s["scores"], i + 1)
                    stt(ret_tmp, bank(7), K_SCALE, ret_D, ALU.mult, ALU.mult).then_inc(s["decayed"], 1)
                if p == 13:
                    ve.wait_ge(s["sum"], i + 1)
                    ts(ret_r, PS[:, 6, 0:T], 1.0 / T, EPS, ALU.mult, ALU.add).then_inc(s["mean"], 1)
                if p == 14:
                    ve.wait_ge(s["root"], i + 1)
                    nc.vector.reciprocal(ret_r, ret_r)
                    drain()
                    r2 = ret_r.unsqueeze(1).broadcast_to([P, 2, T])
                    tt(halves(ret_v), halves(bank(5)), r2, ALU.mult)
                    drain()
                    ve.wait_ge(s["gate"], i + 1)
                    tt(yt[:, ds(2 * i, 2), :], halves(ret_v), halves(ret_g), ALU.mult).then_inc(s["y"], 1)

            def four(p, i):
                s = S["four"]
                if p == 7:
                    ve.wait_ge(s["o"], i + 1)
                    ve.wait_ge(s["gate"], i + 1)
                    tt(yt[:, ds(2 * i + 16, 2), :], halves(bank(7)), halves(four_g), ALU.mult).then_inc(s["y"], 1)

            def conv(p, i):
                s = S["conv"]
                if p == 3:
                    ve.wait_ge(s_free, all_left("conv", i))
                    rows = "p (b r n) -> p b r n"
                    z, v = conv_z, conv_y.rearrange(rows, b=2, r=4)
                    tt(z[:, :, :, 1:65], conv_c.rearrange(rows, b=2, r=4), conv_x.rearrange(rows, b=2, r=4),
                       ALU.mult)
                    drain()
                    for tap in (1, 0, 2):
                        for b in range(2):
                            w = pcol(CONV3_W, 32 * tap + 2 * i + b)
                            zs = z[:, b, :, tap:tap + 64]
                            if tap == 1:
                                ts(v[:, b, :, :], zs, w, None, ALU.mult)
                            else:
                                stt(v[:, b, :, :], zs, w, v[:, b, :, :], ALU.mult, ALU.add)
                        drain()
                    tt(conv_y, conv_y, conv_b, ALU.mult)
                    drain()
                    tt(yt[:, ds(2 * i, 2), :], halves(conv_y), halves(conv_g), ALU.mult).then_inc(s["y"], 1)

            def out_of(stage):
                def add(p, i):
                    if p != 2:
                        return
                    if stage in ("out0", "out1"):
                        for t in range(TT):
                            full(ve, stage, i, t + 1)
                            xs = x[:, t, ds(out_cols(i), 512)]
                            tt(xs, xs, bank(A + t), ALU.add).then_inc(s_free, 1)
                        return
                    ve.wait_ge(s_gr, 1 if stage == "out2" else 2)
                    for t in range(TT):
                        full(ve, stage, i, t + 1)
                        tt(out_t[:, t, :], bank(A + t), gate_rows[:, ds(out_cols(i), 512)], ALU.mult)\
                            .then_inc(s_free, 1)
                    drain()
                    xs = x[:, :, ds(out_cols(i), 512)]
                    tt(xs, xs, out_t, ALU.add).then_inc(s_added, 1)
                    if stage == "out3":
                        drain()
                        ve.wait_ge(s_gain, 32)
                        tt(gained[:, :, ds(out_cols(i), 512)], xs,
                           gain_bc[:, ds(out_cols(i), 512)].unsqueeze(1).broadcast_to([P, TT, 512]), ALU.mult)
                return add

            def gate_diags(n, first):
                for q in range(16):
                    ts(gate_diag[:, q, :], ident[:, :], ada_x[:, first + q:first + q + 1], None, ALU.mult)\
                        .then_inc(s_gd, 1)

            def mod_gain(k, norm_col, scale):
                stt(modc[:, k, :], scale, 1.0, norm_col, ALU.add, ALU.mult)
                drain()

            for stage in ("lru", "swa", "diff", "ret", "four", "conv"):
                ve.sem_inc(S[stage]["y"], 1)
            ve.wait_ge(s_pps, 1)
            nc.vector.tensor_copy(pc[:, :, :], PS[:, 7, 0:3 * P].rearrange("p (t n) -> p t n", t=3))

            def none(p, i):
                pass

            def step(post, n, i):
                return lambda: post(n, i)

            def mixes(stage, *groups):
                return [lambda q=q: mix(stage, q) for q in groups]

            def lambda_sums():
                ve.wait_ge(s_misc, 16 * N_MISC)
                for n in range(2):
                    prod = lam_rows[:, 2 * n, :]
                    tt(prod, prod, lam_rows[:, 2 * n + 1, :], ALU.mult)
                drain()
                for n in range(2):
                    nc.vector.tensor_reduce(nlam[:, n:n + 1], lam_rows[:, 2 * n, :], AX, ALU.add)
                drain()
                ts(sub_g[:, :], pcol(G_SUB, 0), 1.0 - LAMBDA_INIT, None, ALU.mult).then_inc(s_pc, 1)

            def parameters():
                ve.wait_ge(s_pe_, 1)
                ts(lg[:, :], lg[:, :], -1.0, None, ALU.mult)
                tt(nlam[:, 0:1], nlam[:, 1:2], nlam[:, 0:1], ALU.subtract)
                e, z, z2, acc = (lru_c[:, k, :] for k in (1, 2, 3, 0))
                ts(z, e, 2.0, None, ALU.add)
                drain()
                ts(nlam[:, 0:1], nlam[:, 0:1], -LAMBDA_INIT, None, ALU.add)
                nc.vector.reciprocal(z, z)
                drain()
                tt(z, z, e, ALU.mult)
                drain()
                tt(z2, z, z, ALU.mult)
                drain()
                ts(acc, z2, 1.0 / 17, None, ALU.mult)
                for k in range(15, 1, -2):
                    drain()
                    stt(acc, acc, 1.0 / k, z2, ALU.add, ALU.mult)
                drain()
                stt(acc, acc, 1.0, z, ALU.add, ALU.mult)
                ts(e, pc[:, 0, LAM[1]:LAM[1] + 8], -1.0, 0.0, ALU.mult, ALU.max)
                drain()
                ts(acc, acc, 2.0, None, ALU.mult)
                drain()
                tt(acc, acc, e, ALU.add)
                drain()
                ts(acc, acc, -4.0, None, ALU.mult).then_inc(s_pc, 1)

            def clear_history():
                nc.vector.memset(lru_x, 0.0)
                drain()

            norm0 = (0, lambda f: pcol(G_L0, f), None, act)

            norm1 = (1, lambda f: pcol(G_L1, f), None, act)
            norm4 = (4, lambda f: modc[:, 1, f:f + 1], lambda f: ada_x[:, f:f + 1], act)
            norm5 = (5, lambda f: modc[:, 2, f:f + 1], lambda f: ada_x[:, 48 + f:49 + f], act)

            def second_norm():
                add0(2, COUNT["out0"] - 1)
                drain()
                norm(*norm1, range(4))

            def context_root():
                root(3)
                diagonals(3)

            def second_block():
                add1(2, COUNT["out1"] - 1)
                drain()
                ada_column(("out1", COUNT["out1"] - 1), ada_cols("out1", 0))
                drain()
                mod_gain(0, pc[:, 0, G_MOD[1]:G_MOD[1] + KT], ada_c[:, KT:2 * KT])
                mod_gain(1, pc[:, 0, G_MOD[1]:G_MOD[1] + KT], ada_x[:, KT:2 * KT])
                gain, bias = lambda f: modc[:, 0, f:f + 1], lambda f: ada_c[:, f:f + 1]
                scaled()
                tiles(3, gain, bias, range(8))
                root(4)
                diagonals(4)
                lows(3, None, act2, range(4))
                broadcast_roots(4)
                normed(*norm4, (0, 1))
                lows(3, None, act2, range(4, 8))
                normed(*norm4, (2, 3))

            def decay_exponents():
                ve.wait_ge(s_cb, 16)
                for n in range(2):
                    tt(state_w[:, :, 2 * n:2 * n + 2],
                       lg[:, RET_H * n:RET_H * (n + 1)].unsqueeze(2).broadcast_to([P, RET_H, 2]),
                       pow_left[:, 2 * n:2 * n + 2].unsqueeze(1).broadcast_to([P, RET_H, 2]), ALU.mult)
                drain().then_inc(s_dec, 1)

            def decay_weights():
                ve.wait_ge(s_stw, 1)
                ts(state_w[:, :, :], state_w[:, :, :], K_SCALE, None, ALU.mult).then_inc(s_stw, 1)

            def last_block():
                add2(2, COUNT["out2"] - 1)
                drain()
                mod_gain(2, pc[:, 0, G_MOD[1] + KT:G_MOD[1] + 2 * KT], ada_x[:, 64:80])
                norm(*norm5, range(4))

            def clear_borders():
                nc.vector.memset(conv_z, 0.0)
                drain()

            root(0)
            diagonals(0)
            broadcast_roots(0)
            lambda_sums()
            parameters()
            steps = norm_steps(lambda: normed(*norm0, range(4)), *norm0)
            stage_loop(ve, "lru", split("lru"), lru, placed({
                **steps, 6: [*steps[6], clear_history]}))
            if wanted("kv"):
                split("kv")(0, lambda p: lru(p, COUNT["lru"] - 1))
                stage_loop(ve, "swa", split("swa"), swa, kv)
            if wanted("out0"):
                n = COUNT["swa"] - 1
                add0 = out_of("out0")
                stage_loop(ve, "out0", split("out0"), add0, placed({
                    2: [*mixes("out0", 0), step(swa, 3, n), *mixes("out0", 1, 2), step(swa, 4, n)],
                    6: [step(swa, 7, n), *mixes("out0", 3)]}))
            if wanted("cq"):
                split("cq")(0, placed(norm_steps(second_norm, *norm1)))
                with ve.Fori(1, 2) as i:
                    split("cq")(i, nothing)
                split("cq")(2, nothing)
            if wanted("diff"):
                stage_loop(ve, "diff", split("diff"), diff, cq_end)

                def diff_end(p):
                    squeezed(diff, COUNT["diff"] - 1)(p)
                    if p == PIECES["mla"] - 1:
                        drain().then_inc(S["mla"]["y"], 1)
                stage_loop(ve, "mla", split("mla"), mla, diff_end)
            if wanted("out1"):
                n = COUNT["mla"] - 1
                add1 = out_of("out1")
                stage_loop(ve, "out1", split("out1"), add1, placed({
                    2: [step(mla, 3, n), *mixes("out1", 0, 1, 2), step(mla, 4, n)],
                    6: [step(mla, 7, n), *mixes("out1", 3)]}))
            if wanted("ret"):
                stage_loop(ve, "ret", split("ret"), ret, placed({
                    **norm_steps(second_block, *norm4), 0: [context_root], 8: [decay_exponents], 12: [decay_weights]}))
            if wanted("four"):
                def four_and_mix(p, i):
                    four(p, i)
                    if p == 5:
                        mix_pair("out2", i)
                stage_loop(ve, "four", split("four"), four_and_mix, squeezed(ret, COUNT["ret"] - 1))
            if wanted("out2"):
                add2 = out_of("out2")
                stage_loop(ve, "out2", split("out2"), add2, placed({
                    1: [lambda: mix_pair("out2", KT // 2 - 1)],
                    3: mixes("out2", 8, 9),
                    4: mixes("out2", 10),
                    7: [step(four, 7, COUNT["four"] - 1), *mixes("out2", 11)],
                    9: [lambda: gate_diags(1, 32)]}))
            if wanted("conv"):
                def conv_and_mix(p, i):
                    conv(p, i)
                    if p == 8:
                        mix_pair("out3", i - 8)
                split("conv")(0, placed({**norm_steps(last_block, *norm5), 8: [clear_borders]}))
                with ve.Fori(1, 9) as i:
                    split("conv")(i, lambda p: conv(p, i - 1))
                with ve.Fori(9, COUNT["conv"]) as i:
                    split("conv")(i, lambda p: conv_and_mix(p, i - 1))
            if wanted("out3"):
                add3 = out_of("out3")
                stage_loop(ve, "out3", split("out3"), add3, placed({
                    1: [lambda: mix_pair("out3", KT // 2 - 1)],
                    2: [step(conv, 3, COUNT["conv"] - 1), *mixes("out3", 8, 9)],
                    4: mixes("out3", 10),
                    7: mixes("out3", 11),
                    9: [lambda: gate_diags(2, 80)]}))
                add3(2, COUNT["out3"] - 1)
                root(6)
                drain().then_inc(s_inv, 1)
                for h in range(2):
                    half = slice(h * D // 2, (h + 1) * D // 2)
                    ts(x[:, 1, half], gained[:, 1, half], stat[:, 3, 1:2], None, ALU.mult).then_inc(s_second, 1)

        @block.tensor
        def _(te):
            mm = nc.tensor.matmul

            def features(out, slot, c, a, kt, start, stop, m=P):
                hi, lo = w_hi[:, slot, c:c + m], w_lo[:, slot, c:c + m]
                mm(out, hi, a[:, kt, 0:T], start=start, stop=False, skip_group_check=True)
                mm(out, hi, a[:, kt, T:2 * T], start=False, stop=False, skip_group_check=True)
                return mm(out, lo, a[:, kt, 0:T], start=False, stop=stop, skip_group_check=True)

            def tokens(out, slot, c, n, a, kt, t, start, stop):
                hi, lo = w_hi[:, slot, c:c + n], w_lo[:, slot, c:c + n]
                ah, al = a[:, kt, t * P:(t + 1) * P], a[:, kt, T + t * P:T + (t + 1) * P]
                mm(out, ah, hi, start=start, stop=False, skip_group_check=True)
                mm(out, ah, lo, start=False, stop=False, skip_group_check=True)
                return mm(out, al, hi, start=False, stop=stop, skip_group_check=True)

            def enter(stage, i, n):
                v = bank_count(stage, i - 1, n) if not isinstance(i, int) or i > 0 else BANK0[stage]
                if not isinstance(v, int) or v > 0:
                    te.wait_ge(s_free, v)
                if isinstance(i, int) and i == 0 and stage in NORM_OF:
                    te.wait_ge(s_n["tile"], NORM_BANKS[NORM_OF[stage]] + BANKS[stage][n - 1] + 1)

            def half(b, n):
                return PS[:, b, n * T:(n + 1) * T]

            def project(stage, i, p):
                slot = p % RING
                first, last = p == 0, p == PIECES[stage] - 1

                def filled(r):
                    return r.then_inc(s_full, 1)

                if stage in ("lru", "swa", "cq", "four"):
                    partial = stage == "cq" and isinstance(i, int) and i == 2
                    n = 320 if partial else 512
                    for q in range(4 if not partial else 3):
                        m = 64 if n - q * P < P else P
                        if first and q % 2 == 0:
                            enter(stage, i, 1 + q // 2)
                        out = PS[0:m, A + q // 2, (q % 2) * T:(q % 2 + 1) * T]
                        for t in range(2):
                            r = features(out, slot, t * n + q * P, act, 2 * p + t,
                                         first and t == 0 and q % 2 == 0, last and t == 1, m)
                        if last and q == 1:
                            filled(r)
                    return r
                if stage == "kv":
                    if first:
                        enter(stage, i, 2)
                    for t in range(2):
                        st, sp_ = first and t == 0, last and t == 1
                        for q in range(2):
                            r = features(half(A, q), slot, t * 384 + q * P, act, 2 * p + t, st and q == 0, sp_)
                        if sp_:
                            filled(r)
                        for k in range(TT):
                            r = tokens(PS[:, B, k * P:(k + 1) * P], slot, t * 384 + 256, P, act, 2 * p + t, k,
                                       st and k == 0, sp_)
                    return r
                if stage in GROUPS:
                    for k in range(TT):
                        if first:
                            enter(stage, i, 1 + k)
                        for t in range(2):
                            a, kt = mix_dst(stage, 2 * out_pair(stage, p) + t)
                            r = tokens(bank(A + k), slot, t * 512, 512, a, kt, k, first and t == 0, last and t == 1)
                        if last and k < TT - 1:
                            filled(r)
                    return r
                if stage == "diff":
                    for b, c in ((A, 0), (B, 256), (C, 768)):
                        if first:
                            enter(stage, i, 1 + b)
                        for q in range(2):
                            r = features(half(b, q), slot, c + q * P, act, p, first and q == 0, last)
                        if last:
                            filled(r)
                    if first:
                        enter(stage, i, 4)
                    for k in range(TT):
                        r = tokens(half(3, k), slot, 512, 256, act, p, k, first and k == 0, last)
                    return r
                if stage == "mla":
                    if p < 4:
                        if first:
                            enter(stage, i, 1)
                        for t in range(4):
                            for q in range(2):
                                r = features(half(C, q), slot, t * 256 + q * P, act, 4 * p + t,
                                             first and t == 0 and q == 0, p == 3 and t == 3)
                        return r
                    if p < 6:
                        h = p - 4
                        if h == 0:
                            enter(stage, i, 5)
                        for t in range(CKV_T):
                            st, sp_ = t == 0, t == CKV_T - 1
                            r = features(half(B, h), slot, t * 256, cn, CQ_T + t, st and h == 0, sp_)
                            for k in range(TT):
                                r = tokens(PS[:, 3, k * T + h * P:k * T + (h + 1) * P], slot, t * 256 + P, P, cn,
                                           CQ_T + t, k, st and h == 0 and k == 0, sp_)
                        return r
                    h = p - 6
                    for t in range(CQ_T):
                        st, sp_ = t == 0, t == CQ_T - 1
                        r = features(half(A, h), slot, t * 192, cn, t, st and h == 0, sp_)
                        r = features(PS[0:64, 4, h * T:(h + 1) * T], slot, t * 192 + P, cn, t, st and h == 0, sp_, 64)
                    return r
                if stage == "ret":
                    def two(b, c, n):
                        if first:
                            enter(stage, i, n)
                        for q in range(2):
                            r = features(half(b, q), slot, c + q * P, act, p, first and q == 0, last)
                        return r
                    r = two(A, 0, 1)
                    if last:
                        filled(r)
                    if first:
                        enter(stage, i, 2)
                    for k in range(TT):
                        r = tokens(half(C, k), slot, 256, 256, act, p, k, first and k == 0, last)
                    if last:
                        filled(r)
                    for k in range(TT):
                        if first:
                            enter(stage, i, 3 + k)
                        r = tokens(PS[:, 3 + k, 0:384], slot, 128, 384, act2, p, k, first, last)
                        if last:
                            filled(r)
                    return two(B, 512, 5)
                for b in range(4):
                    if first:
                        enter(stage, i, 1 + b)
                    for q in range(2):
                        r = features(half(b, q), slot, 256 * b + q * P, act, p, first and q == 0, last)
                    if last and b < 3:
                        filled(r)
                return r

            def ada_sums(slab, sums):
                stage, group = slab
                total = ada_buffers(stage)[1]
                te.wait_ge(s_au, 8 * (ADA0[stage] + group + 1))
                for b in range(ADA_COLS[stage] // P):
                    for c, acc in enumerate((total, acc_c) if ada_context(stage) else (total,)):
                        n = acc.shape[1]
                        for t in range(n):
                            last = mm(sums[:, 3 * c + b:3 * c + b + 1], acc[:, t, b * P:(b + 1) * P], ones[:, 0:1],
                                      start=t == 0, stop=t == n - 1, skip_group_check=True)
                last.then_inc(s_aps, 1)

            def run(stage):
                def unit(i, hook):
                    for p in range(PIECES[stage]):
                        if isinstance(i, int) and i == 0:
                            inputs_ready(stage, p)
                        slab = ada_slab(stage, i, p) if p % 8 == 0 else None
                        if slab:
                            ada_sums(slab, ada_cols(stage, p // 8))
                        te.wait_ge(s_lo, pieces_before(stage, i) + p + 1)
                        project(stage, i, p).then_inc(s_used, 1)
                        hook(p)
                return unit

            def norm(k, src, first, others):
                diag = norm_scratch(k)[1]

                def pair(b):
                    if k == 4:
                        te.wait_ge(s_n["tile"], NORM_BANKS[3] + b + 1)
                    for f in (2 * b, 2 * b + 1):
                        for t in range(TT):
                            c = (f % 2) * T + t * P
                            dst, tokens = PS[:, b, c:c + P], src[:, t, f * P:(f + 1) * P]
                            if k == 3:
                                r = mm(dst, tokens, diag[:, t, :], start=True, stop=True, skip_group_check=True)
                            else:
                                r = nc.tensor.transpose(dst, tokens, ident[:, :])
                    r.then_inc(s_n["psum"], 1)

                first()
                if k == 3:
                    te.wait_ge(s_n["diag"], DIAGS[k] + 1)
                for b in range(2, 7):
                    pair(b)
                others()
                for b in range(2):
                    pair(b)
                if k != 3:
                    te.wait_ge(s_n["diag"], DIAGS[k] + 1)
                    if k == 4:
                        te.wait_ge(s_n["tile"], NORM_BANKS[3] + 8)
                    for t in range(TT):
                        r = mm(PS[:, 7, t * P:(t + 1) * P], ones[:, :], diag[:, t, :], start=True, stop=True,
                               skip_group_check=True)
                    r.then_inc(s_n["rows"], 1)
                    te.wait_ge(s_n["rows_sb"], ROWS[k] + 1)
                pair(7)

            def inputs_ready(stage, p):
                if stage in GROUPS:
                    tiles = [2 * out_pair(stage, p), 2 * out_pair(stage, p) + 1]
                    for q, (kt, n) in enumerate(GROUPS[stage]):
                        if tiles[0] == kt:
                            te.wait_ge(s_yl, MIX0[stage] + q + 1)
                if stage not in NORM_OF:
                    return
                k = NORM_OF[stage]
                if p == 0 and stage == "cq":
                    te.wait_ge(s_n["tile"], NORM_BANKS[k] + 3)
                if PIECES[stage] == 8 or p % 2 == 0:
                    te.wait_ge(s_n["lo"], NORM_BANKS[k] + (p if PIECES[stage] == 8 else p // 2) + 1)

            def lru(p, i):
                s = S["lru"]
                if p == 2:
                    te.wait_ge(s["conv"], i + 1)
                    te.wait_ge(s_gw, 32 * i + 32)
                    te.wait_ge(s["y"], i + 1)
                    for b in range(2):
                        for w in range(2):
                            r = mm(half(4 + w, b), gate_w[:, b, w, :], halves(lru_xc)[:, b, :], start=True, stop=True,
                                   skip_group_check=True)
                    r.then_inc(s["gates"], 1)

            def kv(p, i=0):
                pass

            def sets_scores(pairs, first_bank):
                for n, terms in enumerate(pairs):
                    for lo, hi, q0, keys in ((0, 128, 0, P), (128, 384, P, T)):
                        for m, (q, k) in enumerate(terms):
                            r = mm(PS[:, first_bank + n, lo:hi], q[:, q0:q0 + P], k[:, 0:keys], start=m == 0,
                                   stop=m == len(terms) - 1, skip_group_check=True)
                return r

            def transposes(tiles, first_bank):
                for n, tile in enumerate(tiles):
                    for b in range(3):
                        r = nc.tensor.transpose(PS[:, first_bank + n, b * P:(b + 1) * P], tile[:, b * P:(b + 1) * P],
                                                ident[:, :])
                return r

            def values(out, v, pT):
                mm(out[:, 0:P], v(0), pT[:, 0:P], start=True, stop=True, skip_group_check=True)
                mm(out[:, P:T], v(0), pT[:, P:2 * P], start=True, stop=False, skip_group_check=True)
                return mm(out[:, P:T], v(1), pT[:, 2 * P:3 * P], start=False, stop=True, skip_group_check=True)

            def swa(p, i):
                s = S["swa"]
                if p == 0:
                    te.wait_ge(s_free, bank_count("swa", i, 1))
                    te.wait_ge(s["y"], i + 1)
                    q = halves(swa_q)
                    pairs = [[(q[64 * (h % 2):64 * (h % 2) + 64, h // 2, :], swa_k[64 * (h % 2):64 * (h % 2) + 64, :])]
                             for h in range(4)]
                    for n in range(2):
                        sets_scores(pairs[2 * n:2 * n + 2], 4 + 2 * n).then_inc(s["scores"], 1)
                if p == 4:
                    te.wait_ge(s["prob"], i + 1)
                    v = view(swa_s, 4, 384)
                    transposes([v[:, h, :] for h in range(4)], 4).then_inc(s["probT"], 1)
                if p == 6:
                    te.wait_ge(s["probT_sb"], i + 1)
                    v = view(swa_t, 4, 384)
                    for h in range(4):
                        r = values(PS[64 * (h % 2):64 * (h % 2) + 64, 4, (h // 2) * T:(h // 2 + 1) * T],
                                   lambda t: swa_v[:, t, :], v[:, h, :])
                    r.then_inc(s["o"], 1)

            def cq_end(p, i=2):
                s = S["cq"]
                if p == 1:
                    te.wait_ge(s["squares"], 1)
                    mm(half(4, 0), rot64, k_raw[:, :], start=True, stop=True, skip_group_check=True)
                    for t in range(CQ_T + CKV_T):
                        q = t < CQ_T
                        r = mm(PS[:, 5 if q else 7, 0:T], ones[:, :], cq_sq[:, t, :], start=t in (0, CQ_T),
                               stop=t in (CQ_T - 1, CQ_T + CKV_T - 1), skip_group_check=True)
                    r.then_inc(s["sums"], 1)
                if p == 7:
                    te.wait_ge(s["gained"], 1)

            def diff(p, i):
                s = S["diff"]
                q, k = halves(at_q), halves(at_k)
                if p == 1:
                    te.wait_ge(s_free, all_left("diff", i))
                    te.wait_ge(s["y"], i + 1)
                    te.wait_ge(s_acol, ADA0["diff"] + 2 * i + 2)
                    pairs = [[(q[64 * c:64 * c + 64, h, :], k[64 * c:64 * c + 64, h, :])]
                             for h in range(2) for c in range(2)]
                    sets_scores(pairs, 4).then_inc(s["scores"], 1)
                if p == 7:
                    te.wait_ge(s["prob"], i + 1)
                    v = dif_s.rearrange("p (h c n) -> p h c n", h=2, c=2)
                    transposes([v[:, h, 0, :] for h in range(2)], 4).then_inc(s["probT"], 1)
                if p == 9:
                    te.wait_ge(s["probT_sb"], i + 1)
                    v, t2 = halves(at_v), view(dif_t, 2, 384)
                    for h in range(2):
                        r = values(half(6, h), lambda t: v[:, t, h * P:(h + 1) * P], t2[:, h, :])
                    r.then_inc(s["o"], 1)
                if p == 11:
                    te.wait_ge(s["sq"], i + 1)
                    mm(bank(5), ones[:, :], dif_sq, start=True, stop=True, skip_group_check=True)\
                        .then_inc(s["sum"], 1)

            def mla(p, i):
                s = S["mla"]
                q, k, qr = halves(at_q), halves(at_k), halves(mla_qr)
                if p == 0:
                    te.wait_ge(s_free, bank_count("mla", i, 2))
                    te.wait_ge(s["y"], i + 1)
                    mm(bank(5), rot64, mla_qr0, start=True, stop=True, skip_group_check=True)\
                        .then_inc(s["rot"], 1)
                if p == 1:
                    te.wait_ge(s_free, bank_count("mla", i, 4))
                    te.wait_ge(s["rope"], i + 1)
                    pairs = [[(q[:, h, :], k[:, h, :]), (qr[:, h, :], k_rot[:, :])] for h in range(2)]
                    sets_scores(pairs, 5).then_inc(s["scores"], 1)
                if p == 4:
                    te.wait_ge(s["prob"], i + 1)
                    v = view(mla_s, 2, 384)
                    transposes([v[:, h, :] for h in range(2)], 5).then_inc(s["probT"], 1)
                if p == 6:
                    te.wait_ge(s["probT_sb"], i + 1)
                    v, t2 = halves(at_v), view(mla_t, 2, 384)
                    for h in range(2):
                        r = values(half(5, h), lambda t: v[:, t, h * P:(h + 1) * P], t2[:, h, :])
                    r.then_inc(s["o"], 1)

            def ret(p, i):
                s = S["ret"]
                if p == 1:
                    te.wait_ge(s_free, all_left("ret", i))
                    te.wait_ge(s["y"], i + 1)
                    mm(bank(5), rot128, ret_qk, start=True, stop=True, skip_group_check=True).then_inc(s["rot"], 1)
                    kc, vc = view(ret_kc, 4, P), halves(ret_vc)
                    for n in range(2):
                        for t in range(TT):
                            r = mm(half(6, n), kc[:, 2 * n + t, :], vc[:, t, :], start=t == 0, stop=t == TT - 1,
                                   skip_group_check=True)
                    r.then_inc(s["state"], 1)
                if p == 5:
                    te.wait_ge(s["rope"], i + 1)
                    te.wait_ge(s_acol, ADA0["ret"] + 2 * i + 2)
                    for j in range(TT):
                        r = mm(half(7, j), ret_qk[:, T + j * P:T + (j + 1) * P], ret_qk[:, 0:T], start=True, stop=True,
                               skip_group_check=True)
                    r.then_inc(s["scores"], 1)
                if p == 7:
                    te.wait_ge(s["decayed"], i + 1)
                    te.wait_ge(s["scaled"], i + 1)
                    te.wait_ge(s["state_sb"], i + 1)
                    v, sd, xi = halves(ret_v), halves(ret_tmp), halves(ret_xi)
                    for e in range(2):
                        terms = [(v[:, j, e * P:(e + 1) * P], sd[:, j, :]) for j in range(TT)]
                        terms += [(ret_S[:, n * T + e * P:n * T + (e + 1) * P], xi[:, n, :]) for n in range(2)]
                        for m, (a, b) in enumerate(terms):
                            r = mm(half(5, e), a, b, start=m == 0, stop=m == 3, skip_group_check=True)
                    r.then_inc(s["o"], 1)
                if p == 10:
                    te.wait_ge(s["sq"], i + 1)
                    for e in range(2):
                        r = mm(PS[:, 6, 0:T], ones[:, :], halves(ret_sq)[:, e, :], start=e == 0, stop=e == 1,
                               skip_group_check=True)
                    r.then_inc(s["sum"], 1)

            def four(p, i):
                s = S["four"]
                if p == 1:
                    te.wait_ge(s_free, all_left("four", i))
                    te.wait_ge(s["y"], i + 1)
                    u = halves(four_u)
                    for t in range(TT):
                        for c in range(2):
                            r = mm(bank(4 + t), u[:, c, t * P:(t + 1) * P], dft[:, c, :], start=c == 0, stop=c == 1,
                                   skip_group_check=True)
                    r.then_inc(s["cols"], 1)
                if p == 3:
                    te.wait_ge(s["cols_sb"], i + 1)
                    for e in range(2):
                        for t in range(TT):
                            mm(half(6, e), four_c[:, t, e * P:(e + 1) * P], dft[:, t, 0:T], start=t == 0, stop=False,
                               skip_group_check=True)
                            r = mm(half(6, e), four_c[:, t, T + e * P:T + (e + 1) * P], dft_ns[:, t, :], start=False,
                                   stop=t == 1, skip_group_check=True)
                    r.then_inc(s["rows"], 1)
                if p == 5:
                    te.wait_ge(s["rows_sb"], i + 1)
                    te.wait_ge(s_fno, 16 * i + 16)
                    for e in range(2):
                        for c in range(2):
                            r = mm(half(7, e), fno[:, c, e * P:(e + 1) * P], four_f[:, c, :], start=c == 0,
                                   stop=c == 1, skip_group_check=True)
                    r.then_inc(s["o"], 1)

            def gates_rows(n):
                for q in range(16):
                    te.wait_ge(s_gd, 16 * (n - 1) + q + 1)
                    r = mm(PS[:, 4 + q // 4, (q % 4) * P:(q % 4 + 1) * P], ones[:, :],
                           gate_diag[:, q, :], start=True, stop=True, skip_group_check=True)
                r.then_inc(s_gb, 1)

            def none(p, i):
                pass

            te.wait_ge(s_set, 1)
            te.wait_ge(s_par, 16 * N_PARAM)
            for t in range(3):
                r = nc.tensor.transpose(PS[:, 7, t * P:(t + 1) * P], prow[:, t, :], ident[:, :])
            r.then_inc(s_pps, 1)
            def step(post, n, i):
                return lambda: post(n, i)

            norm(0, x, lambda: [te.wait_ge(s_x[t], 16) for t in range(TT)], lambda: None)
            stage_loop(te, "lru", run("lru"), lru, nothing)
            if wanted("kv"):
                run("kv")(0, lambda p: lru(p, COUNT["lru"] - 1))
                stage_loop(te, "swa", run("swa"), swa, kv)
            if wanted("out0"):
                n = COUNT["swa"] - 1
                swa(0, n)
                stage_loop(te, "out0", run("out0"), none, placed({2: [step(swa, 4, n)], 4: [step(swa, 6, n)]}))
            if wanted("cq"):
                def first_columns():
                    te.wait_ge(s_free, all_left("out0", 2))
                    te.wait_ge(s_acol, ADA0["cq"] - 1)
                norm(1, x, first_columns, lambda: te.wait_ge(s_free, BANK0["cq"]))
                run("cq")(0, nothing)
                with te.Fori(1, 2) as i:
                    run("cq")(i, nothing)
                run("cq")(2, nothing)
            if wanted("diff"):
                stage_loop(te, "diff", run("diff"), diff, cq_end)
                stage_loop(te, "mla", run("mla"), mla, squeezed(diff, COUNT["diff"] - 1))
            if wanted("out1"):
                n = COUNT["mla"] - 1
                mla(0, n)
                mla(1, n)
                stage_loop(te, "out1", run("out1"), none, placed({2: [step(mla, 4, n)], 4: [step(mla, 6, n)]}))
                ada_sums(("out1", COUNT["out1"] - 1), ada_cols("out1", 0))
            if wanted("ret"):
                def context():
                    te.wait_ge(s_ctx, 16)
                    te.wait_ge(s_acol, ADA0["ret"])

                def tokens_scaled():
                    te.wait_ge(s_fin, TT)
                norm(3, ctx_sb, context, lambda: te.wait_ge(s_free, BANK0["ret"]))
                norm(4, x, tokens_scaled, lambda: None)
                stage_loop(te, "ret", run("ret"), ret, placed({15: [lambda: te.wait_ge(s_cb, 16)]}))
            if wanted("four"):
                stage_loop(te, "four", run("four"), four, squeezed(ret, COUNT["ret"] - 1))
            if wanted("out2"):
                n = COUNT["four"] - 1
                stage_loop(te, "out2", run("out2"), none, placed({
                    1: [step(four, 1, n)], 3: [step(four, 3, n)], 5: [step(four, 5, n)],
                    11: [lambda: gates_rows(1)]}))
            if wanted("conv"):
                def first_columns():
                    te.wait_ge(s_added, COUNT["out2"] - 1)
                    te.wait_ge(s_gr, 1)
                norm(5, x, first_columns, lambda: te.wait_ge(s_added, COUNT["out2"]))
                stage_loop(te, "conv", run("conv"), none, nothing)
            if wanted("out3"):
                stage_loop(te, "out3", run("out3"), none, placed({11: [lambda: gates_rows(2)]}))


_INS = ["x", "norm_gains", "final_norm_gain", "l0_w_in", "l0_conv_w", "l0_conv_b", "l0_gate_x_w", "l0_gate_x_b",
        "l0_gate_a_w", "l0_gate_a_b", "l0_lru_lambda", "l0_sinks", "l0_w_out", "l1_w_in", "l1_q_norm", "l1_w_uq",
        "l1_kv_norm", "l1_w_ukv", "l1_lambda_q1", "l1_lambda_k1", "l1_lambda_q2", "l1_lambda_k2", "l1_subln",
        "l1_w_out", "c_2", "ctx_2", "c_ctx_2", "ada_w_2", "ada_b_2", "norm_w_2", "ev_w_in_2", "ret_decay_logit_2",
        "fno_w_2", "ev_w_out_2", "od_w_in_2", "conv_w_2", "od_w_out_2", "final_norm_w_2"]


def kernel(**inputs):
    import concourse.bacc as bacc
    from concourse.bass_utils import run_bass_kernel_spmd

    nc = bacc.Bacc("TRN2", target_bir_lowering=False, num_devices=1)
    arrays = {name: np.ascontiguousarray(inputs[name]) for name in _INS}
    arrays["const_a"], arrays["const_b"] = constants()
    drams = {name: nc.dram_tensor(f"in_{name}", a.shape, mybir.dt.from_np(a.dtype), kind="ExternalInput").ap()
             for name, a in arrays.items()}
    out = nc.dram_tensor("out_0", (1, T, D), F32, kind="ExternalOutput").ap()
    build(nc, drams, out)
    r = run_bass_kernel_spmd(nc, [{f"in_{name}": a for name, a in arrays.items()}], core_ids=[0])
    return r.results[0]["out_0"]
```
